# Optimizing a Trainium2 kernel written in Bass

```python
import math
import jax, jax.numpy as jnp
from jax import lax
import numpy as np

D_MODEL = 1024
BATCH = 1
SEQ = 512
DEPTH = 1

MEM_LEN = 256
HEAD_DIM = 64
A_HEADS = 8
A_KV_HEADS = 2
A_HALF_WIN = 128
B_HEADS = 8
B_BRANCHES = ((128, 1), (512, 4), (2048, 16))
MIX_WIDTH = (A_HEADS + B_HEADS) * HEAD_DIM
IN_SIZES = (A_HEADS * HEAD_DIM, A_KV_HEADS * HEAD_DIM, A_KV_HEADS * HEAD_DIM,
            B_HEADS * HEAD_DIM, B_HEADS * HEAD_DIM, B_HEADS * HEAD_DIM)
N_BUCKETS = 32
MAX_DISTANCE = 1024
X_HEADS = 4
X_HEAD_DIM = D_MODEL // X_HEADS
N_GROUPS = 4
EXPERTS_PER_GROUP = 8
TOP_K = 2
D_EXPERT = 512
ALPHA = (2.0 * DEPTH) ** 0.25
BETA = (8.0 * DEPTH) ** -0.25
LN_EPS = 1e-5
NEG = -1e30

kernel_name = "hybrid_dilated_window_moe_encoder"

def layer_norm(x, g, b):
    xf = x.astype(jnp.float32)
    mu = jnp.mean(xf, -1, keepdims=True)
    var = jnp.mean(jnp.square(xf - mu), -1, keepdims=True)
    return ((xf - mu) * lax.rsqrt(var + LN_EPS) * g.astype(jnp.float32) + b.astype(jnp.float32)).astype(x.dtype)

def rms_norm(x, g):
    xf = x.astype(jnp.float32)
    return (xf * lax.rsqrt(jnp.mean(jnp.square(xf), -1, keepdims=True) + LN_EPS) * g.astype(jnp.float32)).astype(x.dtype)

def t5_bucket(rel):
    nb = N_BUCKETS // 2
    max_exact = nb // 2
    ret = (rel > 0).astype(np.int32) * nb
    n = np.abs(rel)
    n_safe = np.maximum(n, 1).astype(np.float64)
    large = max_exact + (np.log(n_safe / max_exact) / np.log(MAX_DISTANCE / max_exact)
                         * (nb - max_exact)).astype(np.int32)
    large = np.minimum(large, nb - 1)
    return (ret + np.where(n < max_exact, n, large)).astype(np.int32)

def banded_attention(q, k, v, half, dil, rel_bias, sink=None):
    B, S, H, Dh = q.shape
    Hk = k.shape[2]
    G = H // Hk
    n = S // dil
    nb = -(-n // half)
    n_pad = nb * half

    def to_sub(t):
        h = t.shape[2]
        t = t.reshape(B, n, dil, h, Dh).transpose(0, 2, 1, 3, 4)
        return t.reshape(B * dil, n, h, Dh)

    qs, ks, vs = to_sub(q), to_sub(k), to_sub(v)
    qs = jnp.pad(qs, ((0, 0), (0, n_pad - n), (0, 0), (0, 0)))
    kpad = ((0, 0), (half, n_pad - n + half), (0, 0), (0, 0))
    ks = jnp.pad(ks, kpad)
    vs = jnp.pad(vs, kpad)
    qb = qs.reshape(B * dil, nb, half, Hk, G, Dh)
    kb = ks.reshape(B * dil, nb + 2, half, Hk, Dh)
    vb = vs.reshape(B * dil, nb + 2, half, Hk, Dh)
    kw = jnp.concatenate([kb[:, :-2], kb[:, 1:-1], kb[:, 2:]], axis=2)
    vw = jnp.concatenate([vb[:, :-2], vb[:, 1:-1], vb[:, 2:]], axis=2)

    scores = jnp.einsum('bnqhgd,bnchd->bnhgqc', qb, kw,
                        preferred_element_type=jnp.float32) * (Dh ** -0.5)
    rel_sub = np.arange(3 * half)[None, :] - half - np.arange(half)[:, None]
    band = np.abs(rel_sub) <= half
    key_pos = np.arange(nb)[:, None] * half - half + np.arange(3 * half)[None, :]
    key_ok = (key_pos >= 0) & (key_pos < n)
    mask = band[None] & key_ok[:, None, :]
    bias = rel_bias[t5_bucket(dil * rel_sub)].astype(jnp.float32)
    bias = bias.reshape(half, 3 * half, Hk, G).transpose(2, 3, 0, 1)
    logits = jnp.where(mask[None, :, None, None], scores + bias[None, None], NEG)
    if sink is not None:
        sink_col = jnp.broadcast_to(sink.astype(jnp.float32).reshape(1, 1, Hk, G, 1, 1),
                                    logits.shape[:-1] + (1,))
        lse = jax.nn.logsumexp(jnp.concatenate([logits, sink_col], -1), axis=-1)
    else:
        lse = jax.nn.logsumexp(logits, axis=-1)
    p = jnp.exp(logits - lse[..., None])
    o = jnp.einsum('bnhgqc,bnchd->bnqhgd', p.astype(v.dtype), vw)
    o = o.reshape(B * dil, n_pad, H, Dh)[:, :n].reshape(B, dil, n, H, Dh)
    o = o.transpose(0, 2, 1, 3, 4).reshape(B, S, H, Dh)
    lse = lse.transpose(0, 1, 4, 2, 3).reshape(B * dil, n_pad, H)[:, :n]
    lse = lse.reshape(B, dil, n, H).transpose(0, 2, 1, 3).reshape(B, S, H)
    return o, lse

def hybrid_mixer(h, w_in, rel_bias, sink_a, norm_a_g, norm_b_g, w_out):
    B, S, _ = h.shape
    proj = h @ w_in
    splits = [int(s) for s in np.cumsum(IN_SIZES)[:-1]]
    qa, ka, va, qb, kb, vb = jnp.split(proj, splits, axis=-1)
    qa = qa.reshape(B, S, A_HEADS, HEAD_DIM)
    ka = ka.reshape(B, S, A_KV_HEADS, HEAD_DIM)
    va = va.reshape(B, S, A_KV_HEADS, HEAD_DIM)
    qb = qb.reshape(B, S, B_HEADS, HEAD_DIM)
    kb = kb.reshape(B, S, B_HEADS, HEAD_DIM)
    vb = vb.reshape(B, S, B_HEADS, HEAD_DIM)
    oa, _ = banded_attention(qa, ka, va, A_HALF_WIN, 1, rel_bias[:, :A_HEADS], sink_a)
    outs, lses = [], []
    for win, dil in B_BRANCHES:
        o, l = banded_attention(qb, kb, vb, (win // 2) // dil, dil, rel_bias[:, A_HEADS:])
        outs.append(o)
        lses.append(l)
    wts = jax.nn.softmax(jnp.stack(lses), axis=0)
    ob = jnp.sum(wts[..., None] * jnp.stack(outs).astype(jnp.float32), axis=0).astype(h.dtype)
    ya = rms_norm(oa.reshape(B, S, A_HEADS * HEAD_DIM), norm_a_g)
    yb = rms_norm(ob.reshape(B, S, B_HEADS * HEAD_DIM), norm_b_g)
    return jnp.concatenate([ya, yb], axis=-1) @ w_out

def memory_cross_attention(h, mem, wq, wkv, wo):
    B, S, _ = h.shape
    M = mem.shape[1]
    q = (h @ wq).reshape(B, S, X_HEADS, X_HEAD_DIM)
    k, v = jnp.split(mem @ wkv, 2, axis=-1)
    k = k.reshape(B, M, X_HEADS, X_HEAD_DIM)
    v = v.reshape(B, M, X_HEADS, X_HEAD_DIM)
    s = jnp.einsum('bshd,bmhd->bhsm', q, k, preferred_element_type=jnp.float32) * (X_HEAD_DIM ** -0.5)
    p = jax.nn.softmax(s, axis=-1)
    o = jnp.einsum('bhsm,bmhd->bshd', p.astype(v.dtype), v).reshape(B, S, D_MODEL)
    return o @ wo

def hierarchical_moe(h, w_group, b_group, w_router, b_router, w_gate, w_up, w_down):
    B, S, D = h.shape
    xt = h.reshape(B * S, D)
    T = xt.shape[0]
    g_logits = (xt @ w_group).astype(jnp.float32) + b_group.astype(jnp.float32)
    g_prob = jax.nn.softmax(g_logits, axis=-1)
    _, g_idx = lax.top_k(g_logits, 1)
    g_p = jnp.take_along_axis(g_prob, g_idx, axis=-1)
    e_logits = ((xt @ w_router).astype(jnp.float32) + b_router.astype(jnp.float32))
    e_logits = e_logits.reshape(T, N_GROUPS, EXPERTS_PER_GROUP)
    e_sel = jnp.take_along_axis(e_logits, g_idx[:, :, None], axis=1)[:, 0]
    top_v, top_i = lax.top_k(e_sel, TOP_K)
    top_w = jax.nn.softmax(top_v, axis=-1)
    e_gate = jnp.sum(jax.nn.one_hot(top_i, EXPERTS_PER_GROUP, dtype=jnp.float32) * top_w[..., None], axis=1)
    gate = jax.nn.one_hot(g_idx[:, 0], N_GROUPS, dtype=jnp.float32)[:, :, None] * (g_p[:, :, None] * e_gate[:, None, :])
    y = jnp.zeros((T, D), jnp.float32)
    for g in range(N_GROUPS):
        for e in range(EXPERTS_PER_GROUP):
            hid = jax.nn.silu(xt @ w_gate[g, e]) * (xt @ w_up[g, e])
            y = y + ((gate[:, g, e:e + 1].astype(hid.dtype) * hid) @ w_down[g, e]).astype(jnp.float32)
    return y.astype(h.dtype).reshape(B, S, D)

def setup_inputs(seed: int = 0) -> dict:
    key = jax.random.key(seed)
    ks = jax.random.split(key, 32)
    f32 = jnp.float32
    L, D = DEPTH, D_MODEL
    nrm = lambda k, shape, scale: jax.random.normal(k, shape, f32) * scale
    gain = lambda k, shape: 1.0 + 0.02 * jax.random.normal(k, shape, f32)
    col_scale = np.concatenate([np.full(s, BETA if i in (2, 5) else 1.0, np.float32)
                                for i, s in enumerate(IN_SIZES)])
    xkv_scale = np.concatenate([np.ones(D, np.float32), np.full(D, BETA, np.float32)])
    return {
        "x": jax.random.normal(ks[0], (BATCH, SEQ, D), f32),
        "mem": jax.random.normal(ks[1], (BATCH, MEM_LEN, D), f32),
        "ln_in_g": gain(ks[2], (D,)),
        "ln_in_b": nrm(ks[3], (D,), 0.02),
        "w_in": nrm(ks[4], (L, D, sum(IN_SIZES)), D ** -0.5) * jnp.asarray(col_scale),
        "rel_bias": nrm(ks[5], (N_BUCKETS, A_HEADS + B_HEADS), 0.5),
        "sink_a": nrm(ks[6], (L, A_HEADS), 0.5),
        "norm_a_g": gain(ks[7], (L, A_HEADS * HEAD_DIM)),
        "norm_b_g": gain(ks[8], (L, B_HEADS * HEAD_DIM)),
        "w_out": nrm(ks[9], (L, MIX_WIDTH, D), MIX_WIDTH ** -0.5 * BETA),
        "ln1_g": gain(ks[10], (L, D)),
        "ln1_b": nrm(ks[11], (L, D), 0.02),
        "xq": nrm(ks[12], (L, D, D), D ** -0.5),
        "xkv": nrm(ks[13], (L, D, 2 * D), D ** -0.5) * jnp.asarray(xkv_scale),
        "xo": nrm(ks[14], (L, D, D), D ** -0.5 * BETA),
        "ln2_g": gain(ks[15], (L, D)),
        "ln2_b": nrm(ks[16], (L, D), 0.02),
        "w_group": nrm(ks[17], (L, D, N_GROUPS), D ** -0.5),
        "b_group": nrm(ks[18], (L, N_GROUPS), 0.01),
        "w_router": nrm(ks[19], (L, D, N_GROUPS * EXPERTS_PER_GROUP), D ** -0.5),
        "b_router": nrm(ks[20], (L, N_GROUPS * EXPERTS_PER_GROUP), 0.01),
        "w_gate": nrm(ks[21], (L, N_GROUPS, EXPERTS_PER_GROUP, D, D_EXPERT), D ** -0.5 * BETA),
        "w_up": nrm(ks[22], (L, N_GROUPS, EXPERTS_PER_GROUP, D, D_EXPERT), D ** -0.5 * BETA),
        "w_down": nrm(ks[23], (L, N_GROUPS, EXPERTS_PER_GROUP, D_EXPERT, D), D_EXPERT ** -0.5 * BETA),
        "ln3_g": gain(ks[24], (L, D)),
        "ln3_b": nrm(ks[25], (L, D), 0.02),
    }

def reference(x, mem, ln_in_g, ln_in_b, w_in, rel_bias, sink_a, norm_a_g, norm_b_g, w_out,
              ln1_g, ln1_b, xq, xkv, xo, ln2_g, ln2_b, w_group, b_group, w_router, b_router,
              w_gate, w_up, w_down, ln3_g, ln3_b):
    h = layer_norm(x, ln_in_g, ln_in_b)
    for l in range(DEPTH):
        mix = hybrid_mixer(h, w_in[l], rel_bias, sink_a[l], norm_a_g[l], norm_b_g[l], w_out[l])
        h = layer_norm(ALPHA * h + mix, ln1_g[l], ln1_b[l])
        xa = memory_cross_attention(h, mem, xq[l], xkv[l], xo[l])
        h = layer_norm(ALPHA * h + xa, ln2_g[l], ln2_b[l])
        ff = hierarchical_moe(h, w_group[l], b_group[l], w_router[l], b_router[l],
                              w_gate[l], w_up[l], w_down[l])
        h = layer_norm(ALPHA * h + ff, ln3_g[l], ln3_b[l])
    return h


_drawn_inputs = setup_inputs


def setup_inputs(seed=0):
    import zlib

    import numpy as np

    out = dict(_drawn_inputs(seed))
    spreads = {}
    factors = {'sink_a': 8.0,
     'norm_a_g': 8.0,
     'norm_b_g': 21.417,
     'ln1_g': 2.797,
     'ln1_b': 2.748,
     'ln2_g': 2.786,
     'ln2_b': 2.78,
     'b_group': 8.0,
     'b_router': 25.195,
     'ln3_g': 8.239,
     'ln3_b': 8.016}
    for name, (base, spread) in spreads.items():
        noise = np.random.default_rng([zlib.crc32(name.encode()), seed]).standard_normal(out[name].shape)
        drawn = base * np.exp(spread * noise) if base else spread * noise
        out[name] = __import__('jax').numpy.asarray(drawn.astype(out[name].dtype))
    for name, factor in factors.items():
        out[name] = (out[name] * factor).astype(out[name].dtype)
    return out
```

```python
from contextlib import ExitStack

import concourse.bass as bass
from concourse import mybir

F32 = mybir.dt.float32
BF16 = mybir.dt.bfloat16
I32 = mybir.dt.int32
U32 = mybir.dt.uint32
ALU = mybir.AluOpType
ACT = mybir.ActivationFunctionType
AX = mybir.AxisListType.X

P = 128
D = 1024
KC = D // P
SEQ = 512
NT = SEQ // P
MEM = 256
MT = MEM // P
HD = 64
XH, XD = 4, 256
NG, EG = 4, 8
NE = NG * EG
FE = 512
FC = FE // P
NR = NG + NE
ALPHA = 2.0 ** 0.25
EPS = 1e-5
BIG = 1e30
HALF = 64
UNIT = 4096
LEVELS = SEQ // P
COLS = (LEVELS + 1) * NE
OOB = 4096
TZW = 896
TZ0 = 384

PLAN = [("memT", 4, "AD"), ("bias", 2, "DD"), ("xk", 8, "AD"), ("xv", 4, "AD"), ("hT", 8, "AD"),
        ("qa", 4, "AD"), ("ka", 1, "A"), ("va", 1, "D"), ("qb", 4, "AD"), ("kb", 4, "AD"), ("vb", 4, "AD"),
        ("yT", 8, "DD"), ("mix", 8, "DD"), ("h1T", 8, "AD"), ("xq", 8, "AD"), ("xo", 8, "DD"), ("h2T", 8, "AD")]
JOB, EVAC = {}, ""
for _name, _n, _engines in PLAN:
    JOB[_name] = len(EVAC)
    EVAC += (_engines * _n)[:_n]


def evacs(engine, job):
    return EVAC[:job + 1].count(engine)


SLABS = ["xk0", "xk1", "xv0", "xv1", "qa", "kava", "qb", "kb", "vb", "wo0", "wo1", "xq0", "xq1", "xo0", "xo1"]
LAST = dict(xk0=JOB["xk"] + 3, xk1=JOB["xk"] + 7, xv0=JOB["xv"] + 1, xv1=JOB["xv"] + 3, qa=JOB["qa"] + 3,
            kava=JOB["va"], qb=JOB["qb"] + 3, kb=JOB["kb"] + 3, vb=JOB["vb"] + 3, wo0=JOB["mix"] + 3,
            wo1=JOB["mix"] + 7, xq0=JOB["xq"] + 3, xq1=JOB["xq"] + 7, xo0=JOB["xo"] + 3, xo1=JOB["xo"] + 7)
LOADS = {"qa": 2 * KC}

PAIRS = [("A", j) for j in range(4)] + [("B", j) for j in range(4)]


def head_of(pair, hb):
    group, j = PAIRS[pair]
    return j + 4 * hb if group == "A" else 8 + 2 * j + hb


def keys_of(pair, tile):
    if PAIRS[pair][0] == "B":
        return list(range(NT))
    return [k for k in (tile - 1, tile, tile + 1) if 0 <= k < NT]


def build(nc, x, mem, ln_in_g, ln_in_b, w_in, rel_bias, sink_a, norm_a_g, norm_b_g, w_out, ln1_g, ln1_b,
          xq, xkv, xo, ln2_g, ln2_b, w_group, b_group, w_router, b_router, w_gate, w_up, w_down,
          ln3_g, ln3_b, bucket_onehot, band_mask, out):
    h2_dram = nc.dram_tensor("h2_dram", (SEQ, D), F32, kind="Internal").ap()
    y_dram = nc.dram_tensor("y_dram", (2 * SEQ, D), F32, kind="Internal").ap()
    bias_dram = nc.dram_tensor("bias_dram", (16, 1024), F32, kind="Internal").ap()

    wk = lambda w, a, b: w[0, :, a:b].rearrange("(k p) n -> p k n", p=P)
    slab_src = {"xk0": wk(xkv, 0, 512), "xk1": wk(xkv, 512, 1024), "xv0": wk(xkv, 1024, 1536),
                "xv1": wk(xkv, 1536, 2048), "qa": wk(w_in, 0, 512), "kava": wk(w_in, 512, 768),
                "qb": wk(w_in, 768, 1280), "kb": wk(w_in, 1280, 1792), "vb": wk(w_in, 1792, 2304),
                "wo0": wk(w_out, 0, 512), "wo1": wk(w_out, 512, 1024), "xq0": wk(xq, 0, 512),
                "xq1": wk(xq, 512, 1024), "xo0": wk(xo, 0, 512), "xo1": wk(xo, 512, 1024)}
    gate_src = w_gate.rearrange("a g e (k p) n -> (a g e) p k n", p=P)
    up_src = w_up.rearrange("a g e (k p) n -> (a g e) p k n", p=P)
    down_src = w_down.rearrange("a g e (k p) n -> (a g e) p k n", p=P)

    with ExitStack() as ctx:
        def sb(name, shape, dt=F32):
            return ctx.enter_context(nc.sbuf_tensor(name, shape, dt))

        def sem(name):
            return ctx.enter_context(nc.semaphore(name))

        PS = ctx.enter_context(nc.psum_tensor("PS", [P, 8, 512], F32))

        units = sb("units", [P, 6 * UNIT])
        unit = lambda u: units[:, u * UNIT:(u + 1) * UNIT]
        slab = lambda s: unit(SLABS.index(s) % 4).rearrange("p (k n) -> p k n", k=KC)
        scratch = units[:, 4 * UNIT:6 * UNIT]
        toep = lambda s: scratch[:, s * TZW:(s + 1) * TZW]
        prob = lambda s: scratch[:, 4 * TZW + 512 * s:4 * TZW + 512 * (s + 1)]
        probT = lambda s: scratch[:, 4 * TZW + 2048 + 512 * s:4 * TZW + 2048 + 512 * (s + 1)]
        onehot = scratch[0:32, 4 * TZW:4 * TZW + 1024]
        maskrow = scratch[0:16, 4 * TZW + 1024:4 * TZW + 2048]
        biasrow = scratch[0:16, 4 * TZW + 2048:4 * TZW + 3072]

        H = sb("H", [P, NT, D])
        R2 = sb("R2", [P, 4096])
        hT = R2[:, :].rearrange("p (k s) -> p k s", k=KC)
        Y = R2[:, :].rearrange("p (t f) -> p t f", t=NT)
        comb = R2[:, :].rearrange("p (b r f) -> p b r f", b=2, r=2)

        Q = sb("Q", [P, 9216])
        memR = Q[:, 0:2048].rearrange("p (t f) -> p t f", t=MT)
        memT = Q[:, 2048:4096].rearrange("p (k s) -> p k s", k=KC)
        qaT = Q[:, 0:2048].rearrange("p (j s) -> p j s", j=4)
        kaT = Q[:, 2048:2560]
        va = Q[:, 2560:3072].rearrange("p (t f) -> p t f", t=NT)
        qbT = Q[:, 3072:5120].rearrange("p (j s) -> p j s", j=4)
        kbT = Q[:, 5120:7168].rearrange("p (j s) -> p j s", j=4)
        vb = Q[:, 7168:9216].rearrange("p (t f) -> p t f", t=NT)
        yT = Q[:, 0:4096].rearrange("p (k s) -> p k s", k=KC)
        xqT = Q[:, 4096:8192].rearrange("p (k s) -> p k s", k=KC)

        XKV = sb("XKV", [P, 4096])
        xkT = XKV[:, 0:2048].rearrange("p (k s) -> p k s", k=KC)
        xv = XKV[:, 2048:4096].rearrange("p (t f) -> p t f", t=MT)
        lnG = sb("lnG", [P, D])
        lnB = sb("lnB", [P, D])
        XW = sb("XW", [P, 3072])
        xprob = XW[:, 0:1024].rearrange("p (b i m) -> p b i m", b=2, i=2)
        xprobT = XW[:, 1024:3072].rearrange("p (b m s) -> p b m s", b=2, m=MT)

        ident = sb("ident", [P, P])
        relb = sb("relb", [32, 16])
        nsink = sb("nsink", [P, 8])
        gains = sb("gains", [P, KC])
        stats = sb("stats", [P, NT, 2, 6])
        meanvar = sb("meanvar", [P, NT, 2])
        rstd = sb("rstd", [P, NT])
        half_neg = sb("half_neg", [P, 8])
        nmax = sb("nmax", [P, 64])
        rsum = sb("rsum", [P, 64])
        rinv = sb("rinv", [P, 64])
        sinkx = sb("sinkx", [P, 8])
        ssq = sb("ssq", [P, 8])
        rms = sb("rms", [P, 8])
        xnmax = sb("xnmax", [P, 16])
        xrsum = sb("xrsum", [P, 16])
        xrinv = sb("xrinv", [P, 16])

        xg = lambda u: Q[:, 1024 * u:1024 * u + 1024]
        xgT = lambda u: Q[:, 2048 + 1024 * u:3072 + 1024 * u].rearrange("p (k s) -> p k s", k=KC)
        hid = Q[:, 4096:4608]
        silu = Q[:, 4608:5632].rearrange("p (b f) -> p b f", b=2)
        hidT = lambda u: Q[:, 5632 + 512 * u:6144 + 512 * u].rearrange("p (k s) -> p k s", k=FC)
        yrow = lambda u: Q[:, 6656 + 1024 * u:7680 + 1024 * u]
        pick = lambda u: Q[:, 8704 + 256 * u:8960 + 256 * u].bitcast(BF16).rearrange("p (t s) -> p t s", t=NT)
        gate_w = lambda u: unit(3 * u).rearrange("p (k n) -> p k n", k=KC)
        up_w = lambda u: unit(3 * u + 1).rearrange("p (k n) -> p k n", k=KC)
        down_w = lambda u: unit(3 * u + 2).rearrange("p (k n) -> p k n", k=FC)
        posJ = XW[:, 0:NT * COLS].rearrange("p (t c) -> p t c", t=NT)
        rankJ = XW[:, 640:640 + NT * COLS].rearrange("p (t c) -> p t c", t=NT)
        lg = XW[:, 1280:1424].rearrange("p (t c) -> p t c", t=NT)
        gsel = XW[:, 1424:1440].rearrange("p (t c) -> p t c", t=NT)
        gexp = XW[:, 1440:1456].rearrange("p (t c) -> p t c", t=NT)
        es = XW[:, 1456:1584].rearrange("p (t c) -> p t c", t=NT)
        tmp = XW[:, 1584:1712].rearrange("p (t c) -> p t c", t=NT)
        first = XW[:, 1712:1840].rearrange("p (t c) -> p t c", t=NT)
        second = XW[:, 1840:1968].rearrange("p (t c) -> p t c", t=NT)
        small = XW[:, 1968:2016].rearrange("p (n t) -> p n t", t=NT)
        countJ = XW[0:1, 2048:2048 + COLS].bitcast(I32)
        n_pairs = XW[0:1, 2210:2211].bitcast(I32)
        lev = XW[0:1, 2212:2216]
        chosen = XW[:, 2240:2304].bitcast(BF16).rearrange("p (t c) -> p t c", t=NT)
        gatew = sb("gatew", [P, NT, 2])
        router_w = sb("router_w", [P, KC, NR])
        router_b = sb("router_b", [P, NR])
        iota_e = sb("iota_e", [P, NE])
        iota_s = sb("iota_s", [P, P], BF16)
        before = sb("before", [P, P], BF16)
        ones = sb("ones", [P, P], BF16)
        numbers = sb("numbers", [P, NT, 3], BF16)
        idxf = sb("idxf", [P, 5])
        gidx = sb("gidx", [P, 2], U32)
        sidx = sb("sidx", [P, 2], U32)
        sidx_next = sb("sidx_next", [P, 2])

        mem_in, x_in, small_in, gain_in, table_in = map(sem, ["mem_in", "x_in", "small_in", "gain_in", "table_in"])
        lng_in = [sem(f"lng_in{i}") for i in range(4)]
        slab_in = [sem(f"slab_in{i}") for i in range(4)]
        ident_ok = sem("ident_ok")
        consts_ok = sem("consts_ok")
        job_done = sem("job_done")
        evac_act = sem("evac_act")
        evac_dve = sem("evac_dve")
        bias_out = sem("bias_out")
        toep_in = [sem(f"toep_in{i}") for i in range(4)]
        var_ok, rstd_ok, h_ok = map(sem, ["var_ok", "rstd_ok", "h_ok"])
        s_done, l_done, e_done, t_done, pv_done = map(sem, ["s_done", "l_done", "e_done", "t_done", "pv_done"])
        pt_act, pt_dve = map(sem, ["pt_act", "pt_dve"])
        sinkd_ok, sinke_ok, y_ok = map(sem, ["sinkd_ok", "sinke_ok", "y_ok"])
        ssq_ok, rms_ok, yn_ok = map(sem, ["ssq_ok", "rms_ok", "yn_ok"])
        xs_done, xm_done, xe_done, xp_done, xt_done = map(sem, ["xs_done", "xm_done", "xe_done", "xp_done", "xt_done"])
        xpt_act, xpt_dve, xpv_done, xo_act, xo_dve = map(sem, ["xpt_act", "xpt_dve", "xpv_done", "xo_act", "xo_dve"])
        dve_chain, pool_chain, act_chain = map(sem, ["dve_chain", "pool_chain", "act_chain"])
        out_done = sem("out_done")
        router_in = sem("router_in")
        gate_in = [sem(f"gate_in{u}") for u in range(2)]
        up_in = [sem(f"up_in{u}") for u in range(2)]
        down_in = [sem(f"down_in{u}") for u in range(2)]
        h2_out = sem("h2_out")
        logits_done, gexp_in, gexp_ok, chosen_ok, pos_done, table_ok = map(
            sem, ["logits_done", "gexp_in", "gexp_ok", "chosen_ok", "pos_done", "table_ok"])
        pick_ok, idxmm_done, idx_ok, sidx_ok = map(sem, ["pick_ok", "idxmm_done", "idx_ok", "sidx_ok"])
        row_in = [sem(f"row_in{u}") for u in range(2)]
        row_out = [sem(f"row_out{u}") for u in range(2)]
        xt2_done, xgt_act, xgt_dve, ht_done, hidt_ok = map(sem, ["xt2_done", "xgt_act", "xgt_dve", "ht_done", "hidt_ok"])
        gu_done, silu_ok, hid_ok, down_done, ya_ok, yd_ok = (
            [sem(f"{name}{s}") for s in range(2)]
            for name in ("gu_done", "silu_ok", "hid_ok", "down_done", "ya_ok", "yd_ok"))
        dve_loop, alpha_ok, comb_used, pool_turn = map(sem, ["dve_loop", "alpha_ok", "comb_used", "pool_turn"])
        comb_in = [sem(f"comb_in{u}") for u in range(2)]

        block = ctx.enter_context(nc.Block())

        def waits_evac(eng, job):
            eng.wait_ge(evac_act, evacs("A", job))
            eng.wait_ge(evac_dve, evacs("D", job))

        def first_pair(p):
            return isinstance(p, int) and p == 0

        def col_of(p, u):
            return slice(2 * p + u, 2 * p + u + 1) if isinstance(p, int) else bass.ds(p * 2 + u, 1)

        def flipped(ap):
            return ap.rearrange("p (t s) -> p t s", s=P)[:, :, ::-1]

        def tiles(ap):
            return ap.rearrange("p (t s) -> p t s", s=P)

        @block.sync
        def _(sp):
            sp.dma_start(memR, mem[0].rearrange("(t p) f -> p t f", p=P)).then_inc(mem_in, 16)

            def load_slab(s):
                i = SLABS.index(s)
                if i >= 4:
                    sp.wait_ge(job_done, LAST[SLABS[i - 4]] + 1)
                dst = slab(s)
                if s == "kava":
                    dst = dst[:, :, 0:256]
                if s == "qa":
                    dst = dst.rearrange("p k (j b d) -> p k b j d", b=2, d=HD)
                    src = slab_src[s].rearrange("p k (b j d) -> p k b j d", b=2, d=HD)
                    for k in range(KC):
                        for b in range(2):
                            sp.dma_start(dst[:, k, b], src[:, k, b]).then_inc(slab_in[i % 4], 16)
                    return
                sp.dma_start(dst, slab_src[s]).then_inc(slab_in[i % 4], 16)

            for s in SLABS[0:2]:
                load_slab(s)
            sp.dma_start(H[:, :, :], x[0].rearrange("(t p) f -> p t f", p=P)).then_inc(x_in, 16)
            for s in SLABS[2:6]:
                load_slab(s)
            sp.wait_ge(evac_dve, evacs("D", JOB["bias"] + 1))
            sp.dma_start(bias_dram, biasrow).then_inc(bias_out, 16)

            def load_toeplitz(q):
                head = head_of(q // 2, q % 2)
                lo, hi = (TZ0 - P, TZ0 + 2 * P) if head < 8 else (0, TZW)
                src = bass.AP(bias_dram.tensor, head * 1024 + 1 + lo, [[1, P], [1, hi - lo]])
                if q >= 4:
                    sp.wait_ge(l_done, 8 * (q // 2 - 1))
                sp.dma_start(toep(q % 4)[:, lo:hi], src).then_inc(toep_in[q % 4], 16)

            sp.wait_ge(bias_out, 16)
            for q in range(4):
                load_toeplitz(q)
            for s in SLABS[6:13]:
                load_slab(s)
            for q in range(4, 16):
                load_toeplitz(q)
            load_slab("xo0")
            load_slab("xo1")
            sp.wait_ge(pv_done, 64)
            sp.dma_start(up_w(1), up_src[1]).then_inc(up_in[1], 16)
            sp.dma_start(down_w(1), down_src[1]).then_inc(down_in[1], 16)
            sp.wait_ge(job_done, LAST["xq0"] + 1)
            sp.dma_start(gate_w(1), gate_src[1]).then_inc(gate_in[1], 16)
            sp.wait_ge(job_done, LAST["xq1"] + 1)
            sp.dma_start(gate_w(0), gate_src[0]).then_inc(gate_in[0], 16)
            sp.wait_ge(job_done, LAST["xo0"] + 1)
            sp.dma_start(up_w(0), up_src[0]).then_inc(up_in[0], 16)
            sp.wait_ge(job_done, LAST["xo1"] + 1)
            sp.dma_start(down_w(0), down_src[0]).then_inc(down_in[0], 16)

            def load_pair(pair, expert):
                for u in range(2):
                    for s in range(2):
                        sp.wait_ge(gu_done[s], pair * 2 + (u - 1))
                    sp.dma_start(gate_w(u), gate_src[bass.ds(expert + u, 1)].rearrange("a p k n -> p (a k) n")).then_inc(gate_in[u], 16)
                    sp.dma_start(up_w(u), up_src[bass.ds(expert + u, 1)].rearrange("a p k n -> p (a k) n")).then_inc(up_in[u], 16)
                    for s in range(2):
                        sp.wait_ge(down_done[s], pair * 2 + (u - 1))
                    sp.dma_start(down_w(u), down_src[bass.ds(expert + u, 1)].rearrange("a p k n -> p (a k) n")).then_inc(down_in[u], 16)

            with sp.Fori(1, NE // 2) as p:
                load_pair(p, p * 2)
            sp.wait_ge(table_ok, 1)
            pairs = sp.value_load(n_pairs, min_val=NE // 2, max_val=NE // 2 * LEVELS)
            with sp.If(pairs > NE // 2):
                with sp.Fori(NE // 2, pairs, NE // 2) as base:
                    with sp.Fori(0, NE // 2) as p:
                        load_pair(base + p, p * 2)
            for u in range(2):
                sp.wait_ge(row_out[u], pairs * 16)
            y_src = y_dram.rearrange("(r t p) f -> t p r f", r=2, p=P)
            for t in range(NT):
                if t >= 2:
                    sp.wait_ge(comb_used, t - 1)
                sp.dma_start(comb[:, t % 2], y_src[t]).then_inc(comb_in[t % 2], 16)
            for t in range(NT):
                sp.wait_ge(h_ok, 3 * NT + t + 1)
                sp.dma_start(out[0, P * t:P * t + P, :], H[:, t, :]).then_inc(out_done, 16)
            sp.wait_ge(out_done, 16 * NT)

        @block.gpsimd
        def _(pool):
            chain = [0]

            def link(ins):
                chain[0] += 1
                ins.then_inc(pool_chain, 1)
                pool.wait_ge(pool_chain, chain[0])

            link(nc.gpsimd.memset(ident[:, :], 0.0))
            nc.gpsimd.affine_select(out=ident[:, :], in_=ident[:, :], compare_op=ALU.not_equal, fill=1.0, base=0,
                                    pattern=[[-1, P]], channel_multiplier=1).then_inc(ident_ok, 1)
            nc.gpsimd.memset(half_neg[:, :], -0.5)
            nc.gpsimd.iota(iota_e[:, :], [[1, NE]], base=0, channel_multiplier=0, allow_small_or_imprecise_dtypes=True)
            nc.gpsimd.iota(iota_s[:, :], [[1, P]], base=0, channel_multiplier=0, allow_small_or_imprecise_dtypes=True)
            nc.gpsimd.memset(numbers[:, :, 0:1], 1.0)
            nc.gpsimd.iota(numbers[:, :, 1:2], [[0, NT]], base=0, channel_multiplier=1, allow_small_or_imprecise_dtypes=True)
            nc.gpsimd.iota(numbers[:, :, 2:3], [[1, NT]], base=0, channel_multiplier=0, allow_small_or_imprecise_dtypes=True)
            link(nc.gpsimd.memset(ones[:, :], 1.0))
            nc.gpsimd.affine_select(out=before[:, :], in_=ones[:, :], compare_op=ALU.is_gt, fill=0.0, base=0,
                                    pattern=[[1, P]], channel_multiplier=-1).then_inc(consts_ok, 1)
            pool.wait_ge(consts_ok, 1)

            def layer_rstd(n):
                t = n % NT
                pool.wait_ge(var_ok, n + 1)
                link(nc.gpsimd.tensor_scalar(rstd[:, t:t + 1], meanvar[:, t, 1:2], EPS, None, ALU.add))
                nc.gpsimd.tensor_tensor(rstd[:, t:t + 1], rstd[:, t:t + 1], half_neg[:, 0:1], ALU.pow).then_inc(rstd_ok, 1)

            for n in range(NT):
                layer_rstd(n)
            for g in range(2):
                pool.wait_ge(ssq_ok, NT * (g + 1))
                part = slice(NT * g, NT * g + NT)
                link(nc.gpsimd.tensor_scalar(rms[:, part], ssq[:, part], 1.0 / 512, EPS, ALU.mult, ALU.add))
                nc.gpsimd.tensor_tensor(rms[:, part], rms[:, part], half_neg[:, part], ALU.pow).then_inc(rms_ok, 1)
            for n in range(NT, 3 * NT):
                layer_rstd(n)

            def gather(u, rows):
                pool.indirect_dma_start(xg(u)[0:rows], None, h2_dram, bass.IndirectOffsetOnAxis(gidx[0:rows, u:u + 1], 0),
                                        bounds_check=SEQ - 1, oob_is_err=False).then_inc(row_in[u], 16)

            def scatter(u, rows):
                pool.indirect_dma_start(y_dram, bass.IndirectOffsetOnAxis(sidx[0:rows, u:u + 1], 0), yrow(u)[0:rows], None,
                                        bounds_check=2 * SEQ - 1, oob_is_err=False).then_inc(row_out[u], 16)

            pool.wait_ge(table_ok, 1)
            pairs = pool.value_load(n_pairs, min_val=NE // 2, max_val=NE // 2 * LEVELS)
            pool.wait_ge(h2_out, 16 * NT)
            for w in range(2):
                pool.wait_ge(idx_ok, w + 1)
                gather(w, P)
            nc.gpsimd.tensor_scalar(H[:, :, :].rearrange("p t f -> p (t f)"), H[:, :, :].rearrange("p t f -> p (t f)"),
                                    ALPHA, None, ALU.mult).then_inc(alpha_ok, 1)
            def visits(p):
                for u in range(2):
                    now = pool.value_load(countJ[:, col_of(p, u)], min_val=0, max_val=SEQ)
                    then = pool.value_load(countJ[:, col_of(p, u + 2)], min_val=0, max_val=SEQ)
                    pool.wait_ge(idx_ok, p * 2 + (u + 3))
                    pool.wait_ge(xt2_done, p * 2 + (u + 1))
                    pool.sem_inc(pool_turn, 1)
                    with pool.If(then > HALF):
                        gather(u, P)
                    with pool.Else():
                        gather(u, HALF)
                    pool.wait_ge(sidx_ok, p * 2 + (u + 1))
                    for s in range(2):
                        pool.wait_ge(ya_ok[s], p * 2 + (u + 1))
                        pool.wait_ge(yd_ok[s], p * 2 + (u + 1))
                    pool.sem_inc(pool_turn, 1)
                    with pool.If(now > HALF):
                        scatter(u, P)
                    with pool.Else():
                        scatter(u, HALF)

            visits(0)
            with pool.Fori(1, pairs) as p:
                visits(p)
            for u in range(2):
                pool.wait_ge(row_in[u], pairs * 16 + 16)
            pool.sem_inc(pool_turn, 1)
            for n in range(3 * NT, 4 * NT):
                layer_rstd(n)

        @block.scalar
        def _(act):
            act.dma_start(relb[:, :], rel_bias).then_inc(table_in, 16)
            act.dma_start(onehot, bucket_onehot).then_inc(table_in, 16)
            act.dma_start(maskrow, band_mask).then_inc(table_in, 16)
            act.dma_start(lnG[:, :], ln_in_g.rearrange("(a f) -> a f", a=1).partition_broadcast(P)).then_inc(lng_in[0], 16)
            act.dma_start(lnB[:, :], ln_in_b.rearrange("(a f) -> a f", a=1).partition_broadcast(P)).then_inc(lng_in[0], 16)
            act.dma_start(nsink[:, :], sink_a.partition_broadcast(P)).then_inc(small_in, 16)
            act.dma_start(gains[:, 0:4], norm_a_g[0].rearrange("(k p) -> p k", p=P),
                          allow_slow_non_contiguous=True).then_inc(gain_in, 16)
            act.dma_start(gains[:, 4:8], norm_b_g[0].rearrange("(k p) -> p k", p=P),
                          allow_slow_non_contiguous=True).then_inc(gain_in, 16)

            def load_norm(i, g, b):
                act.wait_ge(h_ok, NT * i)
                act.dma_start(lnG[:, :], g.partition_broadcast(P)).then_inc(lng_in[i], 16)
                act.dma_start(lnB[:, :], b.partition_broadcast(P)).then_inc(lng_in[i], 16)

            def job_copy(job, dst, src, scale=1.0):
                act.wait_ge(job_done, job + 1)
                nc.scalar.activation(dst, src, ACT.Copy, scale=scale).then_inc(evac_act, 1)

            def my_jobs(name):
                base = JOB[name]
                n = dict((a, b) for a, b, _ in PLAN)[name]
                return [i for i in range(n) if EVAC[base + i] == "A"]

            for i in my_jobs("memT"):
                job_copy(JOB["memT"] + i, memT[:, 4 * (i % 2):4 * (i % 2) + 4, P * (i // 2):P * (i // 2) + P],
                         PS[:, (JOB["memT"] + i) % 4, :].rearrange("p (c s) -> p c s", c=4))
            for i in my_jobs("xk"):
                job_copy(JOB["xk"] + i, xkT[:, i, :], PS[:, (JOB["xk"] + i) % 4, 0:MEM])
            for i in my_jobs("xv"):
                job_copy(JOB["xv"] + i, xv[:, i % 2, 512 * (i // 2):512 * (i // 2) + 512], PS[:, (JOB["xv"] + i) % 4, :])
            for i in my_jobs("hT"):
                job_copy(JOB["hT"] + i, hT[:, 4 * (i % 2):4 * (i % 2) + 4, P * (i // 2):P * (i // 2) + P],
                         PS[:, (JOB["hT"] + i) % 4, :].rearrange("p (c s) -> p c s", c=4))
            for i in my_jobs("qa"):
                job_copy(JOB["qa"] + i, flipped(qaT[:, i, :]), tiles(PS[:, (JOB["qa"] + i) % 4, :]), -HD ** -0.5)
            job_copy(JOB["ka"], kaT, PS[:, JOB["ka"] % 4, :])
            for i in my_jobs("qb"):
                job_copy(JOB["qb"] + i, flipped(qbT[:, i, :]), tiles(PS[:, (JOB["qb"] + i) % 4, :]), -HD ** -0.5)
            for i in my_jobs("kb"):
                job_copy(JOB["kb"] + i, kbT[:, i, :], PS[:, (JOB["kb"] + i) % 4, :])
            for i in my_jobs("vb"):
                job_copy(JOB["vb"] + i, vb[:, i, :], PS[:, (JOB["vb"] + i) % 4, :])
            load_norm(1, ln1_g, ln1_b)

            def sum_squares(g, t):
                nc.scalar.activation(XW[:, 0:512], Y[:, t, 512 * g:512 * g + 512], ACT.Square,
                                     accum_out=ssq[:, NT * g + t:NT * g + t + 1]).then_inc(ssq_ok, 1)
                act.wait_ge(ssq_ok, NT * g + t + 1)

            for m in range(34):
                if m < 32:
                    for n in (2 * m, 2 * m + 1):
                        w = P * len(keys_of(n // 8, (n // 2) % 4))
                        act.wait_ge(l_done, n + 1)
                        nc.scalar.activation(prob(n % 4)[:, 0:w], prob(n % 4)[:, 0:w], ACT.Exp, bias=nmax[:, n:n + 1],
                                             scale=-1.0, accum_out=rsum[:, n:n + 1]).then_inc(e_done, 1)
                if 1 <= m <= 32:
                    n = 2 * (m - 1)
                    w = P * len(keys_of(n // 8, (n // 2) % 4))
                    act.wait_ge(t_done, n + 1)
                    if n >= 4:
                        act.wait_ge(pv_done, n - 3)
                    nc.scalar.activation(probT(n % 4)[:, 0:w], PS[:, 4 + n % 2, 0:w], ACT.Copy).then_inc(pt_act, 1)
                if m >= 5 and (m - 2) % 4 == 3 and PAIRS[(m - 2) // 4][0] == "A":
                    act.wait_ge(sinkd_ok, (m - 2) // 4 + 1)
                    nc.scalar.activation(sinkx[:, :], sinkx[:, :], ACT.Exp).then_inc(sinke_ok, 1)
                if m == 18:
                    act.wait_ge(y_ok, 4)
                    for t in range(NT):
                        sum_squares(0, t)
            act.wait_ge(y_ok, 8)
            for t in range(NT):
                sum_squares(1, t)
            for i in my_jobs("h1T"):
                job_copy(JOB["h1T"] + i, hT[:, 4 * (i % 2):4 * (i % 2) + 4, P * (i // 2):P * (i // 2) + P],
                         PS[:, (JOB["h1T"] + i) % 4, :].rearrange("p (c s) -> p c s", c=4))
            for i in my_jobs("xq"):
                job_copy(JOB["xq"] + i, xqT[:, i, :], PS[:, (JOB["xq"] + i) % 4, :], -XD ** -0.5)
            load_norm(2, ln2_g, ln2_b)

            def o_copy(h):
                act.wait_ge(xpv_done, 2 * h + 1)
                nc.scalar.activation(yT[:, 2 * h, :], PS[:, 6, :], ACT.Copy).then_inc(xo_act, 1)

            for h in range(XH):
                for u in (2 * h, 2 * h + 1):
                    act.wait_ge(xm_done, u + 1)
                    if h >= 1:
                        act.wait_ge(xt_done, h)
                    for i in range(2):
                        nc.scalar.activation(xprob[:, u % 2, i, :], PS[:, u % 4, 256 * i:256 * i + 256], ACT.Exp,
                                             bias=xnmax[:, 2 * u + i:2 * u + i + 1], scale=-1.0,
                                             accum_out=xrsum[:, 2 * u + i:2 * u + i + 1]).then_inc(xe_done, 1)
                act.wait_ge(xt_done, h + 1)
                if h >= 2:
                    act.wait_ge(xpv_done, 2 * (h - 1))
                nc.scalar.activation(xprobT[:, h % 2, 0, :], PS[:, 4, :], ACT.Copy).then_inc(xpt_act, 1)
                if h >= 1:
                    o_copy(h - 1)
            o_copy(XH - 1)
            act.dma_start(router_w[:, :, 0:NG], w_group[0].rearrange("(k p) n -> p k n", p=P)).then_inc(router_in, 16)
            act.dma_start(router_w[:, :, NG:NR], w_router[0].rearrange("(k p) n -> p k n", p=P)).then_inc(router_in, 16)
            act.dma_start(router_b[:, 0:NG], b_group.partition_broadcast(P)).then_inc(router_in, 16)
            act.dma_start(router_b[:, NG:NR], b_router.partition_broadcast(P)).then_inc(router_in, 16)
            for i in my_jobs("h2T"):
                job_copy(JOB["h2T"] + i, hT[:, 4 * (i % 2):4 * (i % 2) + 4, P * (i // 2):P * (i // 2) + P],
                         PS[:, (JOB["h2T"] + i) % 4, :].rearrange("p (c s) -> p c s", c=4))
                act.dma_start(h2_dram[P * (i // 2):P * (i // 2) + P, :], H[:, i // 2, :]).then_inc(h2_out, 16)
            load_norm(3, ln3_g, ln3_b)
            act.wait_ge(gexp_in, 1)
            nc.scalar.activation(gexp, gexp, ACT.Exp).then_inc(gexp_ok, 1)
            act.wait_ge(gexp_in, 2)
            nc.scalar.activation(small[:, 4, :], small[:, 4, :], ACT.Exp).then_inc(gexp_ok, 1)

            act.wait_ge(table_ok, 1)
            pairs = act.value_load(n_pairs, min_val=NE // 2, max_val=NE // 2 * LEVELS)
            act.wait_ge(xt2_done, 1)
            nc.scalar.activation(xgT(0)[:, 0:4, :], PS[:, 2, :].rearrange("p (c s) -> p c s", c=4), ACT.Copy).then_inc(xgt_act, 1)
            def visits(p):
                for u in range(2):
                    n = act.value_load(countJ[:, col_of(p, u)], min_val=0, max_val=SEQ)

                    def silu_of(s):
                        act.wait_ge(gu_done[s], p * 2 + (u + 1))
                        nc.scalar.activation(silu[HALF:P, s, :], PS[0:HALF, s, :], ACT.Silu).then_inc(silu_ok[s], 1)

                    def y_left(s):
                        act.wait_ge(down_done[s], p * 2 + (u + 1))
                        nc.scalar.activation(yrow(u)[HALF * s:HALF * s + HALF, 0:512], PS[0:HALF, 5 + s, :],
                                             ACT.Copy).then_inc(ya_ok[s], 1)

                    silu_of(0)
                    with act.If(n > HALF):
                        silu_of(1)
                    with act.Else():
                        act.sem_inc(silu_ok[1], 1)
                    act.wait_ge(xt2_done, p * 2 + (u + 2))
                    nc.scalar.activation(xgT(1 - u)[:, 0:4, :], PS[:, 2, :].rearrange("p (c s) -> p c s", c=4),
                                         ACT.Copy).then_inc(xgt_act, 1)
                    if not first_pair(p):
                        act.wait_ge(row_out[u], p * 16)
                    y_left(0)
                    with act.If(n > HALF):
                        y_left(1)
                    with act.Else():
                        act.sem_inc(ya_ok[1], 1)

            visits(0)
            with act.Fori(1, pairs) as p:
                visits(p)

        @block.vector
        def _(dve):
            chain = [0]

            def link(ins):
                chain[0] += 1
                ins.then_inc(dve_chain, 1)
                dve.wait_ge(dve_chain, chain[0])

            def my_jobs(name):
                base = JOB[name]
                n = dict((a, b) for a, b, _ in PLAN)[name]
                return [i for i in range(n) if EVAC[base + i] == "D"]

            def job_copy(job, dst, src, scale=1.0):
                dve.wait_ge(job_done, job + 1)
                if scale == 1.0:
                    nc.vector.tensor_copy(dst, src).then_inc(evac_dve, 1)
                else:
                    nc.vector.tensor_scalar(dst, src, scale, None, ALU.mult).then_inc(evac_dve, 1)

            def norm_stats(n):
                t = n % NT
                for c in range(2):
                    last = nc.vector.bn_stats(stats[:, t, c, :], H[:, t, 512 * c:512 * c + 512])
                link(last)
                nc.vector.bn_aggr(meanvar[:, t, :], stats[:, t, :, :].rearrange("p c s -> p (c s)")).then_inc(var_ok, 1)

            def norm_apply(n):
                t = n % NT
                dve.wait_ge(var_ok, n + 1)
                dve.wait_ge(rstd_ok, n + 1)
                link(nc.vector.tensor_scalar(H[:, t, :], H[:, t, :], meanvar[:, t, 0:1], rstd[:, t:t + 1],
                                             ALU.subtract, ALU.mult))
                dve.wait_ge(lng_in[n // NT], 32)
                link(nc.vector.tensor_tensor(H[:, t, :], H[:, t, :], lnG[:, :], ALU.mult))
                nc.vector.tensor_tensor(H[:, t, :], H[:, t, :], lnB[:, :], ALU.add).then_inc(h_ok, 1)

            for i in my_jobs("memT"):
                job_copy(JOB["memT"] + i, memT[:, 4 * (i % 2):4 * (i % 2) + 4, P * (i // 2):P * (i // 2) + P],
                         PS[:, (JOB["memT"] + i) % 4, :].rearrange("p (c s) -> p c s", c=4))
            dve.wait_ge(table_in, 48)
            for i in range(2):
                job = JOB["bias"] + i
                dve.wait_ge(job_done, job + 1)
                nc.vector.scalar_tensor_tensor(biasrow[:, 512 * i:512 * i + 512], PS[0:16, job % 4, :], -1.0,
                                               maskrow[:, 512 * i:512 * i + 512], ALU.mult, ALU.add).then_inc(evac_dve, 1)
            dve.wait_ge(small_in, 16)
            link(nc.vector.tensor_scalar(nsink[:, :], nsink[:, :], -1.0, None, ALU.mult))
            for i in my_jobs("xk")[:1]:
                job_copy(JOB["xk"] + i, xkT[:, i, :], PS[:, (JOB["xk"] + i) % 4, 0:MEM])
            dve.wait_ge(x_in, 16)
            todo = [i for i in my_jobs("xk")[1:]] + [8 + i for i in my_jobs("xv")]

            def xkv_copy(i):
                if i < 8:
                    job_copy(JOB["xk"] + i, xkT[:, i, :], PS[:, (JOB["xk"] + i) % 4, 0:MEM])
                else:
                    j = i - 8
                    job_copy(JOB["xv"] + j, xv[:, j % 2, 512 * (j // 2):512 * (j // 2) + 512], PS[:, (JOB["xv"] + j) % 4, :])

            for t in range(NT):
                norm_stats(t)
                if t < len(todo):
                    xkv_copy(todo[t])
                norm_apply(t)
            for i in todo[NT:]:
                xkv_copy(i)
            for i in my_jobs("hT"):
                job_copy(JOB["hT"] + i, hT[:, 4 * (i % 2):4 * (i % 2) + 4, P * (i // 2):P * (i // 2) + P],
                         PS[:, (JOB["hT"] + i) % 4, :].rearrange("p (c s) -> p c s", c=4))
            for i in my_jobs("qa"):
                job_copy(JOB["qa"] + i, flipped(qaT[:, i, :]), tiles(PS[:, (JOB["qa"] + i) % 4, :]), -HD ** -0.5)
            job_copy(JOB["va"], va.rearrange("p t f -> p (t f)"), PS[:, JOB["va"] % 4, :])
            for i in my_jobs("qb"):
                job_copy(JOB["qb"] + i, flipped(qbT[:, i, :]), tiles(PS[:, (JOB["qb"] + i) % 4, :]), -HD ** -0.5)
            for i in my_jobs("kb"):
                job_copy(JOB["kb"] + i, kbT[:, i, :], PS[:, (JOB["kb"] + i) % 4, :])
            for i in my_jobs("vb"):
                job_copy(JOB["vb"] + i, vb[:, i, :], PS[:, (JOB["vb"] + i) % 4, :])

            for m in range(34):
                if m < 32:
                    for n in (2 * m, 2 * m + 1):
                        pair, tile, hb = n // 8, (n // 2) % 4, n % 2
                        keys = keys_of(pair, tile)
                        w = P * len(keys)
                        x0 = TZ0 + P * (keys[0] - tile)
                        q = 2 * pair + hb
                        head = head_of(pair, hb)
                        dve.wait_ge(toep_in[q % 4], 16 * (q // 4 + 1))
                        dve.wait_ge(s_done, n + 1)
                        if n >= 4:
                            dve.wait_ge(t_done, n - 3)
                        nc.vector.tensor_tensor_reduce(
                            out=prob(n % 4)[:, 0:w], in0=PS[:, n % 4, 0:w], in1=toep(q % 4)[:, x0:x0 + w], scale=1.0,
                            scalar=nsink[:, head:head + 1] if head < 8 else 3e38, op0=ALU.add, op1=ALU.min,
                            accum_out=nmax[:, n:n + 1]).then_inc(l_done, 1)
                if 1 <= m <= 32:
                    n = 2 * (m - 1) + 1
                    w = P * len(keys_of(n // 8, (n // 2) % 4))
                    dve.wait_ge(t_done, n + 1)
                    if n >= 4:
                        dve.wait_ge(pv_done, n - 3)
                    nc.vector.tensor_copy(probT(n % 4)[:, 0:w], PS[:, 4 + n % 2, 0:w]).then_inc(pt_dve, 1)
                if m >= 5 and (m - 2) % 4 == 3:
                    pair = (m - 2) // 4
                    group, j = PAIRS[pair]
                    part = slice(8 * pair, 8 * pair + 8)
                    dve.wait_ge(e_done, 8 * pair + 8)
                    if group == "A":
                        sk = nsink[:, :].rearrange("p (b j) -> p b j", b=2)[:, :, j].unsqueeze(1).to_broadcast([P, NT, 2])
                        if pair:
                            dve.wait_ge(sinke_ok, pair)
                        nc.vector.tensor_tensor(sinkx[:, :].rearrange("p (i b) -> p i b", b=2),
                                                nmax[:, part].rearrange("p (i b) -> p i b", b=2), sk,
                                                ALU.subtract).then_inc(sinkd_ok, 1)
                        dve.wait_ge(sinke_ok, pair + 1)
                        link(nc.vector.tensor_tensor(rsum[:, part], rsum[:, part], sinkx[:, :], ALU.add))
                        dst = Y[:, :, 0:512].rearrange("p t (b j d) -> p t b j d", b=2, d=HD)[:, :, :, j, :]
                    else:
                        dst = Y[:, :, 512:1024].rearrange("p t (j b d) -> p t j b d", b=2, d=HD)[:, :, j, :, :]
                    link(nc.vector.reciprocal(rinv[:, part], rsum[:, part]))
                    dve.wait_ge(pv_done, 8 * pair + 8)
                    inv = rinv[:, part].rearrange("p (i b) -> p i b", b=2).unsqueeze(3).to_broadcast([P, NT, 2, HD])
                    nc.vector.tensor_tensor(dst, PS[:, 6 + pair % 2, :].rearrange("p (i b d) -> p i b d", b=2, d=HD),
                                            inv, ALU.mult).then_inc(y_ok, 1)
                if m == 22:
                    dve.wait_ge(rms_ok, 1)
                    for t in range(NT):
                        nc.vector.tensor_scalar(Y[:, t, 0:512], Y[:, t, 0:512], rms[:, t:t + 1], None,
                                                ALU.mult).then_inc(yn_ok, 1)
            dve.wait_ge(rms_ok, 2)
            for t in range(NT):
                nc.vector.tensor_scalar(Y[:, t, 512:1024], Y[:, t, 512:1024], rms[:, NT + t:NT + t + 1], None,
                                        ALU.mult).then_inc(yn_ok, 1)
            dve.wait_ge(gain_in, 32)
            for i in range(8):
                job, g, t = JOB["yT"] + i, i // 4, i % 4
                dve.wait_ge(job_done, job + 1)
                gain = gains[:, 4 * g:4 * g + 4].unsqueeze(2).to_broadcast([P, 4, P])
                nc.vector.tensor_tensor(yT[:, 4 * g:4 * g + 4, P * t:P * t + P][:, :, ::-1],
                                        PS[:, job % 4, :].rearrange("p (c s) -> p c s", c=4), gain,
                                        ALU.mult).then_inc(evac_dve, 1)

            def residual(name, norm):
                for i in range(8):
                    job, hf, t = JOB[name] + i, i // 4, i % 4
                    cols = slice(512 * hf, 512 * hf + 512)
                    dve.wait_ge(job_done, job + 1)
                    nc.vector.scalar_tensor_tensor(H[:, t, cols], H[:, t, cols], ALPHA, PS[:, job % 4, :], ALU.mult,
                                                   ALU.add).then_inc(evac_dve, 1)
                    if hf:
                        dve.wait_ge(evac_dve, evacs("D", job))
                        norm_stats(NT * norm + t)
                        norm_apply(NT * norm + t)

            residual("mix", 1)
            for i in my_jobs("h1T"):
                job_copy(JOB["h1T"] + i, hT[:, 4 * (i % 2):4 * (i % 2) + 4, P * (i // 2):P * (i // 2) + P],
                         PS[:, (JOB["h1T"] + i) % 4, :].rearrange("p (c s) -> p c s", c=4))
            for i in my_jobs("xq"):
                job_copy(JOB["xq"] + i, xqT[:, i, :], PS[:, (JOB["xq"] + i) % 4, :], -XD ** -0.5)

            def o_copy(h):
                dve.wait_ge(xpv_done, 2 * h + 2)
                nc.vector.tensor_copy(yT[:, 2 * h + 1, :], PS[:, 7, :]).then_inc(xo_dve, 1)

            for h in range(XH):
                for u in (2 * h, 2 * h + 1):
                    dve.wait_ge(xs_done, u + 1)
                    nc.vector.tensor_reduce(xnmax[:, 2 * u:2 * u + 2], PS[:, u % 4, :].rearrange("p (i m) -> p i m", i=2),
                                            AX, ALU.min).then_inc(xm_done, 1)
                for u in (2 * h, 2 * h + 1):
                    dve.wait_ge(xe_done, 2 * u + 2)
                    link(nc.vector.reciprocal(xrinv[:, 2 * u:2 * u + 2], xrsum[:, 2 * u:2 * u + 2]))
                    for i in range(2):
                        nc.vector.tensor_scalar(xprob[:, u % 2, i, :], xprob[:, u % 2, i, :],
                                                xrinv[:, 2 * u + i:2 * u + i + 1], None, ALU.mult).then_inc(xp_done, 1)
                dve.wait_ge(xt_done, h + 1)
                if h >= 2:
                    dve.wait_ge(xpv_done, 2 * (h - 1))
                nc.vector.tensor_copy(xprobT[:, h % 2, 1, :], PS[:, 5, :]).then_inc(xpt_dve, 1)
                if h >= 1:
                    o_copy(h - 1)
            o_copy(XH - 1)
            residual("xo", 2)
            for i in my_jobs("h2T"):
                job_copy(JOB["h2T"] + i, hT[:, 4 * (i % 2):4 * (i % 2) + 4, P * (i // 2):P * (i // 2) + P],
                         PS[:, (JOB["h2T"] + i) % 4, :].rearrange("p (c s) -> p c s", c=4))

            over = lambda ap, n: ap.unsqueeze(2).to_broadcast([P, NT, n])
            tt, ts, stt = nc.vector.tensor_tensor, nc.vector.tensor_scalar, nc.vector.scalar_tensor_tensor
            reduce = nc.vector.tensor_reduce
            dve.wait_ge(router_in, 64)
            dve.wait_ge(logits_done, NT)
            link(tt(lg, PS[:, 4, 0:NT * NR].rearrange("p (t c) -> p t c", t=NT),
                    router_b[:, :].unsqueeze(1).to_broadcast([P, NT, NR]), ALU.add))
            gl, el = lg[:, :, 0:NG], lg[:, :, NG:NR]

            def first_of(dst, values, n, top, at):
                link(reduce(top, values, AX, ALU.max))
                link(tt(dst, values, over(top, n), ALU.is_equal))
                link(stt(dst, dst, -100.0, iota_e[:, 0:n].unsqueeze(1).to_broadcast([P, NT, n]), ALU.mult, ALU.add))
                link(reduce(at, dst, AX, ALU.min))
                link(tt(dst, dst, over(at, n), ALU.is_equal))

            first_of(gsel, gl, NG, small[:, 0, :], small[:, 1, :])
            tt(gexp, gl, over(small[:, 0, :], NG), ALU.subtract).then_inc(gexp_in, 1)
            link(ts(tmp[:, :, 0:NG], gsel, -1.0, BIG, ALU.add, ALU.mult))
            group = lambda ap: ap.unsqueeze(3).to_broadcast([P, NT, NG, EG])
            by_group = lambda ap: ap.rearrange("p t (g e) -> p t g e", g=NG)
            link(tt(by_group(es), by_group(el), group(gsel), ALU.mult))
            link(tt(by_group(es), by_group(es), group(tmp[:, :, 0:NG]), ALU.add))
            first_of(first, es, NE, small[:, 2, :], small[:, 1, :])
            link(stt(es, first, -3 * BIG, es, ALU.mult, ALU.add))
            first_of(second, es, NE, small[:, 3, :], small[:, 1, :])
            link(tt(chosen, first, second, ALU.add))
            nc.vector.engine_nop().then_inc(chosen_ok, 1)
            tt(small[:, 4, :], small[:, 3, :], small[:, 2, :], ALU.subtract).then_inc(gexp_in, 1)
            link(stt(tmp, second, 2.0, first, ALU.mult, ALU.add))
            link(nc.vector.tensor_copy(rankJ.rearrange("p t (l e) -> p t l e", e=NE),
                                       tmp.unsqueeze(2).to_broadcast([P, NT, LEVELS + 1, NE])))
            dve.wait_ge(pos_done, 1)
            link(stt(tmp, PS[:, 5, 0:P].rearrange("p (t c) -> p t c", t=NT), 1.0, chosen, ALU.add, ALU.mult))
            for level in range(LEVELS + 1):
                last = ts(posJ[:, :, NE * level:NE * level + NE], tmp, -1.0 - P * level, None, ALU.add)
            link(last)

            def pick_rows(u, col):
                for t in range(NT):
                    last = ts(pick(u)[:, t, :], iota_s[:, :], posJ[:, t, col], rankJ[:, t, col], ALU.is_equal, ALU.mult)
                last.then_inc(pick_ok, 1)

            pick_rows(0, slice(0, 1))
            pick_rows(1, slice(1, 2))
            counts = PS[0:1, 5, P:P + NE]
            for level in range(LEVELS + 1):
                ts(countJ[:, NE * level:NE * level + NE], counts, -1.0 * P * level, 0.0, ALU.add, ALU.max)
            link(reduce(lev[:, 0:1], counts, AX, ALU.max))
            link(ts(lev[:, 1:2], lev[:, 0:1], 1.0 * P, 1.0, ALU.is_gt, ALU.add))
            for level in range(2, LEVELS):
                link(stt(lev[:, 1:2], lev[:, 0:1], 1.0 * P * level, lev[:, 1:2], ALU.is_gt, ALU.add))
            ts(n_pairs, lev[:, 1:2], NE / 2, None, ALU.mult).then_inc(table_ok, 1)

            def tokens_of_slots(u, wait_for):
                idx = PS[:, 7, 0:3]
                ts(idxf[:, 0:1], idx[:, 0:1], -0.5, 1.5, ALU.mult, ALU.add)
                ts(idxf[:, 2:3], idx[:, 0:1], 0.0, 1.0 * OOB, ALU.is_equal, ALU.mult)
                ts(idxf[:, 3:4], idx[:, 0:1], 1.0 * SEQ, -1.0 * SEQ, ALU.mult, ALU.add)
                wait_for(ts(idxf[:, 1:2], idx[:, 2:3], 1.0 * P, None, ALU.mult))
                wait_for(tt(idxf[:, 1:2], idxf[:, 1:2], idx[:, 1:2], ALU.add))
                wait_for(stt(idxf[:, 4:5], idxf[:, 1:2], idxf[:, 0:1], idxf[:, 2:3], ALU.mult, ALU.add))
                wait_for(tt(sidx_next[:, u:u + 1], idxf[:, 4:5], idxf[:, 3:4], ALU.add))
                nc.vector.tensor_copy(gidx[:, u:u + 1], idxf[:, 4:5]).then_inc(idx_ok, 1)

            for w in range(2):
                dve.wait_ge(idxmm_done, w + 1)
                tokens_of_slots(w, link)
            dve.wait_ge(gexp_ok, 2)
            link(reduce(small[:, 5, :], gexp, AX, ALU.add))
            link(nc.vector.reciprocal(small[:, 6, :], small[:, 5, :]))
            link(ts(small[:, 7, :], small[:, 4, :], 1.0, None, ALU.add))
            link(nc.vector.reciprocal(small[:, 8, :], small[:, 7, :]))
            link(tt(gatew[:, :, 0], small[:, 8, :], small[:, 6, :], ALU.mult))
            link(tt(gatew[:, :, 1], gatew[:, :, 0], small[:, 4, :], ALU.mult))

            dve.wait_ge(table_ok, 1)
            pairs = dve.value_load(n_pairs, min_val=NE // 2, max_val=NE // 2 * LEVELS)
            dve.wait_ge(xt2_done, 1)
            nc.vector.tensor_copy(xgT(0)[:, 4:8, :], PS[:, 3, :].rearrange("p (c s) -> p c s", c=4)).then_inc(xgt_dve, 1)

            per_visit = 4
            def visits(p):
                for u in range(2):
                    seen = [0]

                    def loop_link(ins):
                        seen[0] += 1
                        ins.then_inc(dve_loop, 1)
                        dve.wait_ge(dve_loop, p * (2 * per_visit) + (per_visit * u + seen[0]))

                    n = dve.value_load(countJ[:, col_of(p, u)], min_val=0, max_val=SEQ)
                    if not first_pair(p):
                        dve.wait_ge(row_out[u], p * 16)
                    nc.vector.tensor_copy(sidx[:, u:u + 1], sidx_next[:, u:u + 1]).then_inc(sidx_ok, 1)
                    dve.wait_ge(idxmm_done, p * 2 + (u + 1))
                    pick_rows(u, col_of(p, u + 2))

                    def gated(s):
                        dve.wait_ge(silu_ok[s], p * 2 + (u + 1))
                        tt(hid[HALF * s:HALF * s + HALF, :], silu[HALF:P, s, :], PS[HALF:P, s, :],
                           ALU.mult).then_inc(hid_ok[s], 1)

                    def y_right(s):
                        dve.wait_ge(down_done[s], p * 2 + (u + 1))
                        nc.vector.tensor_copy(yrow(u)[HALF * s:HALF * s + HALF, 512:1024],
                                              PS[HALF:P, 5 + s, :]).then_inc(yd_ok[s], 1)

                    gated(0)
                    with dve.If(n > HALF):
                        gated(1)
                    with dve.Else():
                        dve.sem_inc(hid_ok[1], 1)
                    dve.wait_ge(xt2_done, p * 2 + (u + 2))
                    nc.vector.tensor_copy(xgT(1 - u)[:, 4:8, :],
                                          PS[:, 3, :].rearrange("p (c s) -> p c s", c=4)).then_inc(xgt_dve, 1)
                    dve.wait_ge(ht_done, p * 2 + (u + 1))
                    nc.vector.tensor_copy(hidT(u), PS[:, 4, :].rearrange("p (c s) -> p c s", c=FC)).then_inc(hidt_ok, 1)
                    dve.wait_ge(idxmm_done, p * 2 + (u + 3))
                    dve.wait_ge(row_in[u], p * 16 + 16)
                    tokens_of_slots(u, loop_link)
                    assert seen[0] == per_visit
                    y_right(0)
                    with dve.If(n > HALF):
                        y_right(1)
                    with dve.Else():
                        dve.sem_inc(yd_ok[1], 1)

            visits(0)
            with dve.Fori(1, pairs) as p:
                visits(p)

            dve.wait_ge(alpha_ok, 1)
            for t in range(NT):
                dve.wait_ge(comb_in[t % 2], 16 * (t // 2 + 1))
                link(stt(H[:, t, :], comb[:, t % 2, 0, :], gatew[:, t, 0:1], H[:, t, :], ALU.mult, ALU.add))
                stt(H[:, t, :], comb[:, t % 2, 1, :], gatew[:, t, 1:2], H[:, t, :], ALU.mult, ALU.add).then_inc(comb_used, 1)
                dve.wait_ge(comb_used, t + 1)
                norm_stats(3 * NT + t)
                norm_apply(3 * NT + t)

        @block.tensor
        def _(pe):
            def free(job):
                if job >= 4:
                    letter = EVAC[job - 4]
                    pe.wait_ge(evac_act if letter == "A" else evac_dve, evacs(letter, job - 4))

            def transposes(job, src, width=4):
                for c in range(width):
                    last = nc.tensor.transpose(PS[:, job % 4, P * c:P * c + P], src[:, P * c:P * c + P], ident[:, :])
                last.then_inc(job_done, 1)

            def landed(s):
                i = SLABS.index(s)
                pe.wait_ge(slab_in[i % 4], 16 * sum(LOADS.get(x, 1) for x in SLABS[i % 4:i + 1:4]))

            def product(job, lhs, rhs, width=512, chunks=KC):
                for k in range(chunks):
                    last = nc.tensor.matmul(PS[:, job % 4, 0:width], lhs(k), rhs(k), start=(k == 0), stop=(k == chunks - 1))
                last.then_inc(job_done, 1)

            pe.wait_ge(ident_ok, 1)
            pe.wait_ge(mem_in, 16)
            for i in range(4):
                transposes(JOB["memT"] + i, memR[:, i // 2, 512 * (i % 2):512 * (i % 2) + 512])
            pe.wait_ge(table_in, 48)
            for i in range(2):
                job = JOB["bias"] + i
                free(job)
                nc.tensor.matmul(PS[0:16, job % 4, :], relb[:, :], onehot[:, 512 * i:512 * i + 512], start=True,
                                 stop=True).then_inc(job_done, 1)
            waits_evac(pe, JOB["memT"] + 3)
            for i in range(8):
                if i % 4 == 0:
                    landed(f"xk{i // 4}")
                w = slab(f"xk{i // 4}")
                free(JOB["xk"] + i)
                product(JOB["xk"] + i, lambda k: w[:, k, P * (i % 4):P * (i % 4) + P], lambda k: memT[:, k, :], MEM)
            for i in range(4):
                if i % 2 == 0:
                    landed(f"xv{i // 2}")
                w = slab(f"xv{i // 2}")
                free(JOB["xv"] + i)
                product(JOB["xv"] + i, lambda k: memT[:, k, P * (i % 2):P * (i % 2) + P], lambda k: w[:, k, :])
            for i in range(8):
                pe.wait_ge(h_ok, i // 2 + 1)
                free(JOB["hT"] + i)
                transposes(JOB["hT"] + i, H[:, i // 2, 512 * (i % 2):512 * (i % 2) + 512])
            waits_evac(pe, JOB["hT"] + 7)
            landed("qa")
            w = slab("qa")
            for i in range(4):
                free(JOB["qa"] + i)
                product(JOB["qa"] + i, lambda k: w[:, k, P * i:P * i + P], lambda k: hT[:, k, :])
            landed("kava")
            w = slab("kava")
            free(JOB["ka"])
            product(JOB["ka"], lambda k: w[:, k, 0:P], lambda k: hT[:, k, :])
            job = JOB["va"]
            free(job)
            for t in range(NT):
                for k in range(KC):
                    last = nc.tensor.matmul(PS[:, job % 4, P * t:P * t + P], hT[:, k, P * t:P * t + P], w[:, k, P:2 * P],
                                            start=(k == 0), stop=(k == KC - 1))
            last.then_inc(job_done, 1)
            for name in ("qb", "kb"):
                landed(name)
                w = slab(name)
                for i in range(4):
                    free(JOB[name] + i)
                    product(JOB[name] + i, lambda k: w[:, k, P * i:P * i + P], lambda k: hT[:, k, :])
            landed("vb")
            w = slab("vb")
            for i in range(4):
                free(JOB["vb"] + i)
                product(JOB["vb"] + i, lambda k: hT[:, k, P * i:P * i + P], lambda k: w[:, k, :])
            waits_evac(pe, JOB["vb"] + 3)

            def scores(n):
                pair, tile, hb = n // 8, (n // 2) % 4, n % 2
                group, j = PAIRS[pair]
                qT, kT = (qaT[:, j, :], kaT) if group == "A" else (qbT[:, j, :], kbT[:, j, :])
                keys = keys_of(pair, tile)
                rows = slice(HD * hb, HD * hb + HD)
                if n >= 4:
                    pe.wait_ge(l_done, n - 3)
                nc.tensor.matmul(PS[:, n % 4, 0:P * len(keys)], qT[rows, P * tile:P * tile + P],
                                 kT[rows, P * keys[0]:P * (keys[-1] + 1)], start=True, stop=True).then_inc(s_done, 1)

            def turn(n):
                keys = keys_of(n // 8, (n // 2) % 4)
                pe.wait_ge(e_done, n + 1)
                if n >= 2:
                    pe.wait_ge(pt_act if n % 2 == 0 else pt_dve, n // 2)
                for c in range(len(keys)):
                    last = nc.tensor.transpose(PS[:, 4 + n % 2, P * c:P * c + P], prob(n % 4)[:, P * c:P * c + P], ident[:, :])
                last.then_inc(t_done, 1)

            def values(n):
                pair, tile, hb = n // 8, (n // 2) % 4, n % 2
                group, j = PAIRS[pair]
                keys = keys_of(pair, tile)
                pe.wait_ge(pt_act if n % 2 == 0 else pt_dve, n // 2 + 1)
                if n % 8 == 0 and pair >= 2:
                    pe.wait_ge(y_ok, pair - 1)
                col = 2 * tile + hb
                for c, key in enumerate(keys):
                    v = va[:, key, HD * hb:HD * hb + HD] if group == "A" else vb[:, key, P * j + HD * hb:P * j + HD * hb + HD]
                    last = nc.tensor.matmul(PS[:, 6 + pair % 2, HD * col:HD * col + HD], probT(n % 4)[:, P * c:P * c + P], v,
                                            start=(c == 0), stop=(c == len(keys) - 1))
                last.then_inc(pv_done, 1)

            for m in range(34):
                if m < 32:
                    scores(2 * m)
                    scores(2 * m + 1)
                if 1 <= m <= 32:
                    turn(2 * m - 2)
                    turn(2 * m - 1)
                if m >= 2:
                    values(2 * m - 4)
                    values(2 * m - 3)

            for i in range(8):
                pe.wait_ge(yn_ok, i + 1)
                free(JOB["yT"] + i)
                transposes(JOB["yT"] + i, Y[:, i % 4, 512 * (i // 4):512 * (i // 4) + 512])

            def dense_out(name, slabs, src):
                for i in range(8):
                    if i % 4 == 0:
                        landed(slabs[i // 4])
                    w = slab(slabs[i // 4])
                    free(JOB[name] + i)
                    product(JOB[name] + i, lambda k: src[:, k, P * (i % 4):P * (i % 4) + P], lambda k: w[:, k, :])

            waits_evac(pe, JOB["yT"] + 7)
            dense_out("mix", ("wo0", "wo1"), yT)
            for i in range(8):
                pe.wait_ge(h_ok, NT + i // 2 + 1)
                free(JOB["h1T"] + i)
                transposes(JOB["h1T"] + i, H[:, i // 2, 512 * (i % 2):512 * (i % 2) + 512])
            waits_evac(pe, JOB["h1T"] + 7)
            for i in range(8):
                if i % 4 == 0:
                    landed(f"xq{i // 4}")
                w = slab(f"xq{i // 4}")
                free(JOB["xq"] + i)
                product(JOB["xq"] + i, lambda k: w[:, k, P * (i % 4):P * (i % 4) + P], lambda k: hT[:, k, :])
            waits_evac(pe, JOB["xq"] + 7)

            def xscores(h):
                for u in (2 * h, 2 * h + 1):
                    if h >= 2:
                        pe.wait_ge(xe_done, 2 * (u - 4) + 2)
                    for i in range(2):
                        tile = 2 * (u % 2) + i
                        for c in range(2):
                            last = nc.tensor.matmul(PS[:, u % 4, 256 * i:256 * i + 256],
                                                    xqT[:, 2 * h + c, P * tile:P * tile + P], xkT[:, 2 * h + c, :],
                                                    start=(c == 0), stop=(c == 1))
                    last.then_inc(xs_done, 1)

            def xvalues(h):
                pe.wait_ge(xpt_act, h + 1)
                pe.wait_ge(xpt_dve, h + 1)
                for c in range(2):
                    if h:
                        pe.wait_ge(xo_act if c == 0 else xo_dve, h)
                    for mt in range(MT):
                        last = nc.tensor.matmul(PS[:, 6 + c, :], xv[:, mt, XD * h + P * c:XD * h + P * c + P],
                                                xprobT[:, h % 2, mt, :], start=(mt == 0), stop=(mt == MT - 1))
                    last.then_inc(xpv_done, 1)

            xscores(0)
            for h in range(XH):
                if h + 1 < XH:
                    xscores(h + 1)
                pe.wait_ge(xp_done, 4 * h + 4)
                if h:
                    pe.wait_ge(xpt_act, h)
                    pe.wait_ge(xpt_dve, h)
                for mt in range(MT):
                    for i in range(NT):
                        u = 2 * h + i // 2
                        last = nc.tensor.transpose(PS[:, 4 + mt, P * i:P * i + P],
                                                   xprob[:, u % 2, i % 2, P * mt:P * mt + P], ident[:, :])
                last.then_inc(xt_done, 1)
                if h:
                    xvalues(h - 1)
            xvalues(XH - 1)
            pe.wait_ge(xo_act, XH)
            pe.wait_ge(xo_dve, XH)
            dense_out("xo", ("xo0", "xo1"), yT)

            def router(t):
                waits_evac(pe, JOB["h2T"] + 2 * t + 1)
                for k in range(KC):
                    last = nc.tensor.matmul(PS[:, 4, NR * t:NR * t + NR], hT[:, k, P * t:P * t + P], router_w[:, k, :],
                                            start=(k == 0), stop=(k == KC - 1))
                last.then_inc(logits_done, 1)

            pe.wait_ge(router_in, 64)
            for i in range(8):
                pe.wait_ge(h_ok, 2 * NT + i // 2 + 1)
                free(JOB["h2T"] + i)
                transposes(JOB["h2T"] + i, H[:, i // 2, 512 * (i % 2):512 * (i % 2) + 512])
                if i % 2 and i > 1:
                    router(i // 2 - 1)
            router(NT - 1)
            pe.wait_ge(consts_ok, 1)
            pe.wait_ge(chosen_ok, 1)
            for t in range(NT):
                for s in range(t + 1):
                    nc.tensor.matmul(PS[:, 5, NE * t:NE * t + NE], before[:, :] if s == t else ones[:, :], chosen[:, s, :],
                                     start=(s == 0), stop=(s == t))
            for t in range(NT):
                last = nc.tensor.matmul(PS[:, 5, P:P + NE], ones[:, :], chosen[:, t, :], start=(t == 0), stop=(t == NT - 1))
            last.then_inc(pos_done, 1)

            def slot_tokens(u):
                for t in range(NT):
                    last = nc.tensor.matmul(PS[:, 7, 0:3], pick(u)[:, t, :], numbers[:, t, :], start=(t == 0), stop=(t == NT - 1))
                last.then_inc(idxmm_done, 1)

            def turn_rows(u):
                for c in range(KC):
                    last = nc.tensor.transpose(PS[:, 2 + c // 4, P * (c % 4):P * (c % 4) + P], xg(u)[:, P * c:P * c + P], ident[:, :])
                last.then_inc(xt2_done, 1)

            pe.wait_ge(pick_ok, 1)
            slot_tokens(0)
            pe.wait_ge(pick_ok, 2)
            pe.wait_ge(idx_ok, 1)
            slot_tokens(1)
            pe.wait_ge(row_in[0], 16)
            turn_rows(0)
            pe.wait_ge(table_ok, 1)
            pairs = pe.value_load(n_pairs, min_val=NE // 2, max_val=NE // 2 * LEVELS)
            def visits(p):
                for u in range(2):
                    n = pe.value_load(countJ[:, col_of(p, u)], min_val=0, max_val=SEQ)

                    def gate_up(s):
                        slots = slice(HALF * s, HALF * s + HALF)
                        for k in range(KC):
                            nc.tensor.matmul(PS[0:HALF, s, :], xgT(u)[:, k, slots], gate_w(u)[:, k, :],
                                             start=(k == 0), stop=(k == KC - 1))
                            last = nc.tensor.matmul(PS[HALF:P, s, :], xgT(u)[:, k, slots], up_w(u)[:, k, :],
                                                    start=(k == 0), stop=(k == KC - 1))
                        last.then_inc(gu_done[s], 1)

                    def down(s):
                        slots = slice(HALF * s, HALF * s + HALF)
                        for k in range(FC):
                            nc.tensor.matmul(PS[0:HALF, 5 + s, :], hidT(u)[:, k, slots], down_w(u)[:, k, 0:512],
                                             start=(k == 0), stop=(k == FC - 1))
                            last = nc.tensor.matmul(PS[HALF:P, 5 + s, :], hidT(u)[:, k, slots], down_w(u)[:, k, 512:1024],
                                                    start=(k == 0), stop=(k == FC - 1))
                        last.then_inc(down_done[s], 1)

                    pe.wait_ge(gate_in[u], p * 16 + 16)
                    pe.wait_ge(up_in[u], p * 16 + 16)
                    pe.wait_ge(xgt_act, p * 2 + (u + 1))
                    pe.wait_ge(xgt_dve, p * 2 + (u + 1))
                    gate_up(0)
                    with pe.If(n > HALF):
                        gate_up(1)
                    with pe.Else():
                        pe.sem_inc(gu_done[1], 1)
                    pe.wait_ge(row_in[1 - u], p * 16 + (16 if u == 0 else 32))
                    turn_rows(1 - u)
                    pe.wait_ge(pick_ok, p * 2 + (u + 3))
                    pe.wait_ge(idx_ok, p * 2 + (u + 2))
                    slot_tokens(u)
                    pe.wait_ge(hid_ok[0], p * 2 + (u + 1))
                    pe.wait_ge(hid_ok[1], p * 2 + (u + 1))
                    for c in range(FC):
                        last = nc.tensor.transpose(PS[:, 4, P * c:P * c + P], hid[:, P * c:P * c + P], ident[:, :])
                    last.then_inc(ht_done, 1)
                    pe.wait_ge(down_in[u], p * 16 + 16)
                    pe.wait_ge(hidt_ok, p * 2 + (u + 1))
                    for s in range(2):
                        if u or not first_pair(p):
                            pe.wait_ge(ya_ok[s], p * 2 + u)
                            pe.wait_ge(yd_ok[s], p * 2 + u)
                    down(0)
                    with pe.If(n > HALF):
                        down(1)
                    with pe.Else():
                        pe.sem_inc(down_done[1], 1)

            visits(0)
            with pe.Fori(1, pairs) as p:
                visits(p)


def shape_tables():
    import numpy as np

    rel = np.arange(1024) - 512
    n = np.abs(rel)
    large = 8 + (np.log(np.maximum(n, 1) / 8) / np.log(1024 / 8) * 8).astype(np.int32)
    bucket = (rel > 0) * 16 + np.where(n < 8, n, np.minimum(large, 15))
    onehot = (np.arange(32)[:, None] == bucket[None]).astype(np.float32)
    reach_b = (n <= 64) * 1 + ((n <= 256) & (rel % 4 == 0)) + (rel % 16 == 0)
    a = np.where(n <= 128, 0.0, BIG)
    b = np.where(reach_b > 0, -np.log(np.maximum(reach_b, 1)), BIG)
    mask = np.concatenate([np.tile(a, (8, 1)), np.tile(b, (8, 1))]).astype(np.float32)
    return onehot, mask


_INS = ["x", "mem", "ln_in_g", "ln_in_b", "w_in", "rel_bias", "sink_a", "norm_a_g", "norm_b_g", "w_out", "ln1_g",
        "ln1_b", "xq", "xkv", "xo", "ln2_g", "ln2_b", "w_group", "b_group", "w_router", "b_router", "w_gate", "w_up",
        "w_down", "ln3_g", "ln3_b"]


def kernel(**inputs):
    import numpy as np
    import concourse.bacc as bacc
    from concourse.bass_utils import run_bass_kernel_spmd

    nc = bacc.Bacc("TRN2", target_bir_lowering=False, num_devices=1)
    arrays = {f"in_{name}": np.ascontiguousarray(inputs[name]) for name in _INS}
    arrays["in_bucket_onehot"], arrays["in_band_mask"] = shape_tables()
    args = [nc.dram_tensor(n, a.shape, mybir.dt.from_np(a.dtype), kind="ExternalInput").ap() for n, a in arrays.items()]
    out = nc.dram_tensor("out_dram", (1, SEQ, D), F32, kind="ExternalOutput").ap()
    build(nc, *args, out)
    result = run_bass_kernel_spmd(nc, [arrays], core_ids=[0])
    return result.results[0]["out_dram"]
```

```python
from contextlib import ExitStack

import concourse.bass as bass
from concourse import mybir

F32 = mybir.dt.float32
F32R = mybir.dt.float32r
BF16 = mybir.dt.bfloat16
I32 = mybir.dt.int32
U32 = mybir.dt.uint32
ALU = mybir.AluOpType
ACT = mybir.ActivationFunctionType
AX = mybir.AxisListType.X

P = 128
D = 1024
KC = D // P
SEQ = 512
NT = SEQ // P
MEM = 256
MT = MEM // P
HD = 64
XH, XD = 4, 256
NG, EG = 4, 8
NE = NG * EG
FE = 512
FC = FE // P
NR = NG + NE
ALPHA = 2.0 ** 0.25
EPS = 1e-5
BIG = 1e30
HALF = 64
UNIT = 4096
LEVELS = SEQ // P
COLS = (LEVELS + 1) * NE
OOB = 4096
TZW = 896
TZ0 = 384

PLAN = [("memT", 4, "BB", None), ("xk", 8, "AD", None), ("bias", 2, "DD", None), ("xv", 2, "AD", None),
        ("hT", 4, "BB", None), ("xv", 1, "A", None), ("hT", 4, "BB", None), ("xv", 1, "D", None), ("qa", 4, "AD", None), ("ka", 1, "A", None), ("va", 1, "D", None), ("qb", 4, "AD", None),
        ("kb", 4, "AD", None), ("vb", 4, "AD", None), ("yT", 4, "BB", (4, 5, 4, 5)), ("yT", 4, "BB", (6, 7, 4, 5)),
        ("mix", 7, "DD", None), ("h1T", 4, "BB", (4, 5, 6, 7)), ("mix", 1, "DD", None), ("h1T", 4, "BB", (4, 5, 6, 7)),
        ("xq", 4, "AD", None), ("xq", 4, "AD", (4, 5, 6, 7)), ("xo", 7, "DD", None), ("h2T", 4, "AD", (5, 6, 7, 5)),
        ("xo", 1, "DD", None), ("h2T", 4, "AD", None)]
JOBS, EVAC, BANK, _ring = {}, "", [], 0
for _name, _n, _engines, _banks in PLAN:
    for _i in range(_n):
        JOBS.setdefault(_name, []).append(len(EVAC))
        EVAC += _engines[_i % 2]
        BANK.append(_banks[_i] if _banks else _ring % 4)
        _ring += not _banks


def job_of(name, i):
    return JOBS[name][i]


def evacs(engine, job):
    return sum(letter in (engine, "B") for letter in EVAC[:job + 1])


SLABS = ["xk0", "xk1", "xv0", "xv1", "qa", "kava", "qb", "kb", "vb", "wo0", "wo1", "xq0", "xq1", "xo0", "xo1"]
LAST = dict(xk0=job_of("xk", 3), xk1=job_of("xk", 7), xv0=job_of("xv", 1), xv1=job_of("xv", 3), qa=job_of("qa", 3),
            kava=job_of("va", 0), qb=job_of("qb", 3), kb=job_of("kb", 3), vb=job_of("vb", 3), wo0=job_of("mix", 3),
            wo1=job_of("mix", 7), xq0=job_of("xq", 3), xq1=job_of("xq", 7), xo0=job_of("xo", 3), xo1=job_of("xo", 7))
STAGES = 3
PIECES = 4
POOL_SLABS = ["xv1", "xq0", "xo1"]

PAIRS = [("A", j) for j in range(4)] + [("B", j) for j in range(4)]


def head_of(pair, hb):
    group, j = PAIRS[pair]
    return 2 * j + hb + (8 if group == "B" else 0)


def keys_of(pair, tile):
    if PAIRS[pair][0] == "B":
        return list(range(NT))
    return [k for k in (tile - 1, tile, tile + 1) if 0 <= k < NT]


def build(nc, x, mem, ln_in_g, ln_in_b, w_in, rel_bias, sink_a, norm_a_g, norm_b_g, w_out, ln1_g, ln1_b,
          xq, xkv, xo, ln2_g, ln2_b, w_group, b_group, w_router, b_router, w_gate, w_up, w_down,
          ln3_g, ln3_b, bucket_onehot, band_mask, out):
    y_dram = nc.dram_tensor("y_dram", (2 * SEQ, D), F32, kind="Internal").ap()
    bias_dram = nc.dram_tensor("bias_dram", (16, 1024), F32, kind="Internal").ap()

    wk = lambda w, a, b: w[0, :, a:b].rearrange("(k p) n -> p k n", p=P)
    slab_src = {"xk0": wk(xkv, 0, 512), "xk1": wk(xkv, 512, 1024), "xv0": wk(xkv, 1024, 1536),
                "xv1": wk(xkv, 1536, 2048), "qa": wk(w_in, 0, 512), "kava": wk(w_in, 512, 768),
                "qb": wk(w_in, 768, 1280), "kb": wk(w_in, 1280, 1792), "vb": wk(w_in, 1792, 2304),
                "wo0": wk(w_out, 0, 512), "wo1": wk(w_out, 512, 1024), "xq0": wk(xq, 0, 512),
                "xq1": wk(xq, 512, 1024), "xo0": wk(xo, 0, 512), "xo1": wk(xo, 512, 1024)}
    gate_src = w_gate.rearrange("a g e (k p) n -> (a g e) p k n", p=P)
    up_src = w_up.rearrange("a g e (k p) n -> (a g e) p k n", p=P)
    down_src = w_down.rearrange("a g e (k p) n -> (a g e) p k n", p=P)

    with ExitStack() as ctx:
        def sb(name, shape, dt=F32):
            return ctx.enter_context(nc.sbuf_tensor(name, shape, dt))

        def sem(name):
            return ctx.enter_context(nc.semaphore(name))

        PS = ctx.enter_context(nc.psum_tensor("PS", [P, 8, 512], F32))

        arena = -(-nc.sbuf_base // 32) * 32
        units = sb("units", [P, 6 * UNIT])
        R2 = sb("R2", [P, 4096])
        Q = sb("Q", [P, 9216])

        def parts(name, start, floats):
            return nc.alloc_sbuf_tensor_at(name, [P, floats], F32R, offset=arena + 4 * start, align_bytes=32)

        unit = lambda u: units[:, u * UNIT:(u + 1) * UNIT]
        slab = lambda s: unit(SLABS.index(s) % STAGES).rearrange("p (k n) -> p k n", k=KC)
        w_lo = parts("w_lo", 0, STAGES * UNIT)
        w_hi = parts("w_hi", STAGES * UNIT, 2 * UNIT)
        slab_lo = lambda i: w_lo[:, (i % STAGES) * UNIT:(i % STAGES + 1) * UNIT].rearrange("p (k n) -> p k n", k=KC)
        slab_hi = lambda i: w_hi[:, (i % 2) * UNIT:(i % 2 + 1) * UNIT].rearrange("p (k n) -> p k n", k=KC)
        aT_lo = parts("aT_lo", 5 * UNIT, UNIT)[:, :].rearrange("p (k s) -> p k s", k=KC)
        toep_b = lambda s: units[:, 5 * UNIT + s * TZW:5 * UNIT + (s + 1) * TZW]
        prob = lambda s: units[:, 2 * UNIT + 512 * s:2 * UNIT + 512 * (s + 1)]
        probT = lambda s: units[:, 2 * UNIT + 2048 + 512 * s:2 * UNIT + 2048 + 512 * (s + 1)]

        H = sb("H", [P, NT, D])
        aT_hi = parts("aT_hi", 6 * UNIT, 4096)[:, :].rearrange("p (k s) -> p k s", k=KC)
        h2T = R2[:, :].rearrange("p (k s) -> p k s", k=KC)
        Y = R2[:, :].rearrange("p (t f) -> p t f", t=NT)
        comb = R2[:, :].rearrange("p (b r f) -> p b r f", b=2, r=2)

        in_q = lambda name, start, floats: parts(name, 6 * UNIT + 4096 + start, floats)[:, :].rearrange("p (k s) -> p k s", k=KC)
        memR = Q[:, 0:2048].rearrange("p (t f) -> p t f", t=MT)
        memT_hi = in_q("memT_hi", 2048, 2048)
        memT_lo = in_q("memT_lo", 4096, 2048)
        qaT = Q[:, 0:2048].rearrange("p (j s) -> p j s", j=4)
        va = Q[:, 2560:3072].rearrange("p (t f) -> p t f", t=NT)
        qbT = Q[:, 3072:5120].rearrange("p (j s) -> p j s", j=4)
        kbT = Q[:, 5120:7168].rearrange("p (j s) -> p j s", j=4)
        vb = Q[:, 7168:9216].rearrange("p (t f) -> p t f", t=NT)
        yT_hi = in_q("yT_hi", 0, 4096)
        yT_lo = in_q("yT_lo", 4096, 4096)
        xqT = Q[:, 4096:8192].rearrange("p (k s) -> p k s", k=KC)

        XKV = sb("XKV", [P, 4096])
        xkT = XKV[:, 0:2048].rearrange("p (k s) -> p k s", k=KC)
        xv = XKV[:, 2048:4096].rearrange("p (t f) -> p t f", t=MT)
        lnG = sb("lnG", [P, D])
        kaT = lambda g: Q[:, 2048:2560] if g == 0 else lnG[:, 0:512]
        lnB = sb("lnB", [P, D])
        XW = sb("XW", [P, 3072])
        toep_a = lambda s: XW[:, s * 3 * P:(s + 1) * 3 * P]
        onehot = XW[0:32, 0:1024]
        maskrow = XW[0:16, 1024:2048]
        biasrow = XW[0:16, 2048:3072]
        xprob = lambda h: (XW[:, 0:1024] if h % 2 == 0 else lnG[:, :]).rearrange("p (t m) -> p t m", t=NT)
        xprobT = XW[:, 1024:3072].rearrange("p (b m s) -> p b m s", b=2, m=MT)

        ident = sb("ident", [P, P])
        relb = sb("relb", [32, 16])
        nsink = sb("nsink", [P, 8])
        gains = sb("gains", [P, KC])
        stats = sb("stats", [P, NT, 2, 6])
        meanvar = sb("meanvar", [P, NT, 2])
        rstd = sb("rstd", [P, NT])
        half_neg = sb("half_neg", [P, 8])
        nmax = sb("nmax", [P, 64])
        rsum = sb("rsum", [P, 64])
        rinv = sb("rinv", [P, 64])
        sinkx = sb("sinkx", [P, 8])
        ssq = sb("ssq", [P, 8])
        rms = sb("rms", [P, 8])
        xnmax = sb("xnmax", [P, 16])
        xrsum = sb("xrsum", [P, 16])
        xrinv = sb("xrinv", [P, 16])

        h2_part = lambda i: (XKV[:, 2048 * i:2048 * i + 2048] if i < 2 else Q[:, 7168:9216]).bitcast(BF16).rearrange(
            "p (t f) -> p t f", t=NT)
        rest = Q[:, 6144:7168]
        xg = lambda s: R2[:, 2048 + 512 * s:2560 + 512 * s]
        silu = R2[:, 3072:4096].rearrange("p (b f) -> p b f", b=2)
        yrow = lambda u: R2[:, 1024 * u:1024 + 1024 * u]
        xgT = lambda u: Q[:, 1024 * u:1024 + 1024 * u].rearrange("p (k s) -> p k s", k=KC)
        hid = Q[:, 2048:2560]
        hidT = lambda u: Q[:, 2560 + 512 * u:3072 + 512 * u].rearrange("p (k s) -> p k s", k=FC)
        in_bf16 = lambda start: Q[:, start:start + 256].bitcast(BF16).rearrange("p (t s) -> p t s", t=NT)
        pick = lambda u: in_bf16(3584 + 256 * u)
        ranked = lambda u: in_bf16(4096 + 256 * u)
        gate_w = lambda u: unit(3 * u).rearrange("p (k n) -> p k n", k=KC)
        up_w = lambda u: unit(3 * u + 1).rearrange("p (k n) -> p k n", k=KC)
        down_w = lambda u: unit(3 * u + 2).rearrange("p (k n) -> p k n", k=FC)
        posJ = XW[:, 0:NT * COLS].rearrange("p (t c) -> p t c", t=NT)
        rankJ = XW[:, 640:640 + NT * COLS].rearrange("p (t c) -> p t c", t=NT)
        lg = XW[:, 1280:1424].rearrange("p (t c) -> p t c", t=NT)
        gsel = XW[:, 1424:1440].rearrange("p (t c) -> p t c", t=NT)
        gexp = XW[:, 1440:1456].rearrange("p (t c) -> p t c", t=NT)
        es = XW[:, 1456:1584].rearrange("p (t c) -> p t c", t=NT)
        tmp = XW[:, 1584:1712].rearrange("p (t c) -> p t c", t=NT)
        first = XW[:, 1712:1840].rearrange("p (t c) -> p t c", t=NT)
        second = XW[:, 1840:1968].rearrange("p (t c) -> p t c", t=NT)
        small = XW[:, 1968:2016].rearrange("p (n t) -> p n t", t=NT)
        countJ = XW[0:1, 2048:2048 + COLS].bitcast(I32)
        n_pairs = XW[0:1, 2210:2211].bitcast(I32)
        lev = XW[0:1, 2212:2216]
        chosen = XW[:, 2240:2304].bitcast(BF16).rearrange("p (t c) -> p t c", t=NT)
        gatew = sb("gatew", [P, NT, 2])
        router_w = sb("router_w", [P, KC, NR])
        router_b = sb("router_b", [P, NR])
        iota_e = sb("iota_e", [P, NE])
        iota_s = sb("iota_s", [P, P], BF16)
        before = sb("before", [P, P], BF16)
        ones = sb("ones", [P, P], BF16)
        numbers = sb("numbers", [P, NT, 3], BF16)
        idxf = sb("idxf", [P, 5])
        sidx = sb("sidx", [P, 2], U32)
        sidx_next = sb("sidx_next", [P, 2])

        small_in, gain_in, table_in = map(sem, ["small_in", "gain_in", "table_in"])
        mem_in = [sem(f"mem_in{t}") for t in range(MT)]
        x_in = [sem(f"x_in{t}") for t in range(NT)]
        lng_in = [sem(f"lng_in{i}") for i in range(4)]
        slab_in = [sem(f"slab_in{i}") for i in range(STAGES)]
        first_in = [sem(f"first_in{c}") for c in range(PIECES)]
        hi_ok, lo_dve, lo_pool = map(sem, ["hi_ok", "lo_dve", "lo_pool"])
        ident_ok = sem("ident_ok")
        consts_ok = sem("consts_ok")
        job_done = sem("job_done")
        evac_act = sem("evac_act")
        evac_dve = sem("evac_dve")
        bias_out = sem("bias_out")
        toep_a_in = sem("toep_a_in")
        toep_b_in = [sem(f"toep_b_in{i}") for i in range(4)]
        var_ok, rstd_ok, h_ok = map(sem, ["var_ok", "rstd_ok", "h_ok"])
        s_done, l_done, e_done, t_done, pv_done = map(sem, ["s_done", "l_done", "e_done", "t_done", "pv_done"])
        pt_act, pt_dve = map(sem, ["pt_act", "pt_dve"])
        sinkd_ok, sinke_ok, y_ok = map(sem, ["sinkd_ok", "sinke_ok", "y_ok"])
        ssq_ok, rms_ok, yn_ok = map(sem, ["ssq_ok", "rms_ok", "yn_ok"])
        xs_done, xm_done, xe_done, xp_done, xt_done = map(sem, ["xs_done", "xm_done", "xe_done", "xp_done", "xt_done"])
        xpt_act, xpt_dve, xpv_done, xo_act, xo_dve = map(sem, ["xpt_act", "xpt_dve", "xpv_done", "xo_act", "xo_dve"])
        dve_chain, pool_chain, act_chain = map(sem, ["dve_chain", "pool_chain", "act_chain"])
        out_done = sem("out_done")
        router_in = sem("router_in")
        gate_in = [sem(f"gate_in{u}") for u in range(2)]
        up_in = [sem(f"up_in{u}") for u in range(2)]
        down_in = [sem(f"down_in{u}") for u in range(2)]
        part_ok, rest_ok = map(sem, ["part_ok", "rest_ok"])
        parts_act = sem("parts_act")
        logits_done, gexp_in, gexp_ok, chosen_ok, pos_done, table_ok = map(
            sem, ["logits_done", "gexp_in", "gexp_ok", "chosen_ok", "pos_done", "table_ok"])
        pick_ok, idxmm_done, idx_ok, sidx_ok = map(sem, ["pick_ok", "idxmm_done", "idx_ok", "sidx_ok"])
        row_out = [sem(f"row_out{u}") for u in range(2)]
        ht_done, hidt_ok = map(sem, ["ht_done", "hidt_ok"])
        gu_done, silu_ok, hid_ok, down_done, ya_ok, yd_ok, rows_done, rows_ok, xt2_done, xgt_ok = (
            [sem(f"{name}{s}") for s in range(2)]
            for name in ("gu_done", "silu_ok", "hid_ok", "down_done", "ya_ok", "yd_ok", "rows_done", "rows_ok",
                         "xt2_done", "xgt_ok"))
        dve_loop, alpha_ok, comb_used, pool_turn = map(sem, ["dve_loop", "alpha_ok", "comb_used", "pool_turn"])
        comb_in = [sem(f"comb_in{u}") for u in range(2)]

        block = ctx.enter_context(nc.Block())

        def waits_evac(eng, job):
            eng.wait_ge(evac_act, evacs("A", job))
            eng.wait_ge(evac_dve, evacs("D", job))

        def first_pair(p):
            return isinstance(p, int) and p == 0

        def from_halves(s):
            return PS[:, 2 + s, :].rearrange("p (c b s) -> p c b s", c=4, b=2)

        def col_of(p, u):
            return slice(2 * p + u, 2 * p + u + 1) if isinstance(p, int) else bass.ds(p * 2 + u, 1)

        def flipped(ap):
            return ap.rearrange("p (t s) -> p t s", s=P)[:, :, ::-1]

        def tiles(ap):
            return ap.rearrange("p (t s) -> p t s", s=P)

        def piece(ap, s, c):
            n = KC // PIECES
            return ap[:, n * c:n * c + n, 0:256 if s == "kava" else 512]

        def landings(s):
            i = SLABS.index(s)
            return 16 * (i // STAGES + (i % STAGES > 0))

        def lo_written(eng, name, pieces=PIECES):
            mine = [x for x in SLABS if (x in POOL_SLABS) == (name in POOL_SLABS)]
            eng.wait_ge(lo_pool if name in POOL_SLABS else lo_dve, PIECES * mine.index(name) + pieces)

        def half_tile(ap, i, backwards=False):
            t, half = (i % 4, i // 4) if backwards else (i // 2, i % 2)
            ap = ap[:, 4 * half:4 * half + 4, P * t:P * t + P]
            return ap[:, :, ::-1] if backwards else ap

        @block.sync
        def _(sp):
            for t in range(MT):
                sp.dma_start(memR[:, t, :], mem[0, P * t:P * t + P, :]).then_inc(mem_in[t], 16)

            def load_slab(s):
                i = SLABS.index(s)
                if i >= STAGES:
                    sp.wait_ge(job_done, LAST[SLABS[i - STAGES]] + 1)
                if s == "xq0":
                    sp.wait_ge(pv_done, 64)
                if s == "kava":
                    sp.dma_start(slab(s)[:, :, 0:256], slab_src[s]).then_inc(slab_in[i % STAGES], 16)
                elif i == 0:
                    for c in range(PIECES):
                        sp.dma_start(piece(slab(s), s, c), piece(slab_src[s], s, c)).then_inc(first_in[c], 16)
                else:
                    sp.dma_start(slab(s), slab_src[s]).then_inc(slab_in[i % STAGES], 16)

            load_slab("xk0")
            load_slab("xk1")
            for t in range(NT):
                sp.dma_start(H[:, t, :], x[0, P * t:P * t + P, :]).then_inc(x_in[t], 16)
            sp.dma_start(lnG[:, :], ln_in_g.rearrange("(a f) -> a f", a=1).partition_broadcast(P)).then_inc(lng_in[0], 16)
            sp.dma_start(lnB[:, :], ln_in_b.rearrange("(a f) -> a f", a=1).partition_broadcast(P)).then_inc(lng_in[0], 16)
            load_slab("xv0")
            load_slab("xv1")
            load_slab("qa")
            sp.wait_ge(evac_dve, evacs("D", job_of("bias", 1)))
            sp.dma_start(bias_dram, biasrow).then_inc(bias_out, 16)
            sp.wait_ge(bias_out, 16)
            sp.dma_start(XW[:, :].rearrange("p (h w) -> p h w", h=8),
                         bass.AP(bias_dram.tensor, 1 + TZ0 - P, [[1, P], [1024, 8], [1, 3 * P]])).then_inc(toep_a_in, 16)
            sp.dma_start(nsink[:, :], sink_a.partition_broadcast(P)).then_inc(small_in, 16)
            for s in SLABS[5:11]:
                load_slab(s)
                if s == "kava":
                    for g, gain in enumerate((norm_a_g, norm_b_g)):
                        sp.dma_start(gains[:, 4 * g:4 * g + 4], gain[0].rearrange("(k p) -> p k", p=P),
                                     allow_slow_non_contiguous=True).then_inc(gain_in, 16)
            sp.wait_ge(job_done, job_of("vb", 3) + 1)
            for q in range(8):
                if q >= 4:
                    sp.wait_ge(l_done, 8 * (4 + q // 2 - 1))
                src = bass.AP(bias_dram.tensor, (8 + q) * 1024 + 1, [[1, P], [1, TZW]])
                sp.dma_start(toep_b(q % 4), src).then_inc(toep_b_in[q % 4], 16)
            for s in SLABS[11:15]:
                load_slab(s)
            sp.wait_ge(job_done, LAST["xq1"] + 1)
            sp.dma_start(gate_w(0), gate_src[0]).then_inc(gate_in[0], 16)
            sp.wait_ge(job_done, LAST["xo0"] + 1)
            sp.dma_start(up_w(0), up_src[0]).then_inc(up_in[0], 16)
            sp.dma_start(up_w(1), up_src[1]).then_inc(up_in[1], 16)
            sp.wait_ge(job_done, LAST["xo1"] + 1)
            sp.dma_start(down_w(0), down_src[0]).then_inc(down_in[0], 16)
            sp.dma_start(gate_w(1), gate_src[1]).then_inc(gate_in[1], 16)
            sp.dma_start(down_w(1), down_src[1]).then_inc(down_in[1], 16)

            def load_pair(pair, expert):
                for u in range(2):
                    for s in range(2):
                        sp.wait_ge(gu_done[s], pair * 2 + (u - 1))
                    sp.dma_start(gate_w(u), gate_src[bass.ds(expert + u, 1)].rearrange("a p k n -> p (a k) n")).then_inc(gate_in[u], 16)
                    sp.dma_start(up_w(u), up_src[bass.ds(expert + u, 1)].rearrange("a p k n -> p (a k) n")).then_inc(up_in[u], 16)
                    for s in range(2):
                        sp.wait_ge(down_done[s], pair * 2 + (u - 1))
                    sp.dma_start(down_w(u), down_src[bass.ds(expert + u, 1)].rearrange("a p k n -> p (a k) n")).then_inc(down_in[u], 16)

            with sp.Fori(1, NE // 2) as p:
                load_pair(p, p * 2)
            sp.wait_ge(table_ok, 1)
            pairs = sp.value_load(n_pairs, min_val=NE // 2, max_val=NE // 2 * LEVELS)
            with sp.If(pairs > NE // 2):
                with sp.Fori(NE // 2, pairs, NE // 2) as base:
                    with sp.Fori(0, NE // 2) as p:
                        load_pair(base + p, p * 2)
            for u in range(2):
                sp.wait_ge(row_out[u], pairs * 16)
            y_src = y_dram.rearrange("(r t p) f -> t p r f", r=2, p=P)
            for t in range(NT):
                if t >= 2:
                    sp.wait_ge(comb_used, t - 1)
                sp.dma_start(comb[:, t % 2], y_src[t]).then_inc(comb_in[t % 2], 16)
            for t in range(NT):
                sp.wait_ge(h_ok, 3 * NT + t + 1)
                sp.dma_start(out[0, P * t:P * t + P, :], H[:, t, :]).then_inc(out_done, 16)
            sp.wait_ge(out_done, 16 * NT)

        @block.gpsimd
        def _(pool):
            chain = [0]

            def link(ins):
                chain[0] += 1
                ins.then_inc(pool_chain, 1)
                pool.wait_ge(pool_chain, chain[0])

            link(nc.gpsimd.memset(ident[:, :], 0.0))
            nc.gpsimd.affine_select(out=ident[:, :], in_=ident[:, :], compare_op=ALU.not_equal, fill=1.0, base=0,
                                    pattern=[[-1, P]], channel_multiplier=1).then_inc(ident_ok, 1)
            nc.gpsimd.memset(half_neg[:, :], -0.5)
            nc.gpsimd.iota(iota_e[:, :], [[1, NE]], base=0, channel_multiplier=0, allow_small_or_imprecise_dtypes=True)
            nc.gpsimd.iota(iota_s[:, :], [[1, P]], base=0, channel_multiplier=0, allow_small_or_imprecise_dtypes=True)
            nc.gpsimd.memset(numbers[:, :, 0:1], 1.0)
            nc.gpsimd.iota(numbers[:, :, 1:2], [[0, NT]], base=0, channel_multiplier=1, allow_small_or_imprecise_dtypes=True)
            nc.gpsimd.iota(numbers[:, :, 2:3], [[1, NT]], base=0, channel_multiplier=0, allow_small_or_imprecise_dtypes=True)
            link(nc.gpsimd.memset(ones[:, :], 1.0))
            nc.gpsimd.affine_select(out=before[:, :], in_=ones[:, :], compare_op=ALU.is_gt, fill=0.0, base=0,
                                    pattern=[[1, P]], channel_multiplier=-1).then_inc(consts_ok, 1)
            pool.wait_ge(consts_ok, 1)

            def layer_rstd(n):
                t = n % NT
                pool.wait_ge(var_ok, n + 1)
                link(nc.gpsimd.tensor_scalar(rstd[:, t:t + 1], meanvar[:, t, 1:2], EPS, None, ALU.add))
                nc.gpsimd.tensor_tensor(rstd[:, t:t + 1], rstd[:, t:t + 1], half_neg[:, 0:1], ALU.pow).then_inc(rstd_ok, 1)

            def split_lo(name):
                i = SLABS.index(name)
                for c in range(PIECES):
                    pool.wait_ge(hi_ok, PIECES * i + c + 1)
                    nc.gpsimd.tensor_tensor(piece(slab_lo(i), name, c), piece(slab(name), name, c),
                                            piece(slab_hi(i), name, c).bitcast(F32), ALU.subtract).then_inc(lo_pool, 1)

            for n in range(NT):
                layer_rstd(n)
            split_lo("xv1")
            for g in range(2):
                pool.wait_ge(ssq_ok, NT * (g + 1))
                part = slice(NT * g, NT * g + NT)
                link(nc.gpsimd.tensor_scalar(rms[:, part], ssq[:, part], 1.0 / 512, EPS, ALU.mult, ALU.add))
                nc.gpsimd.tensor_tensor(rms[:, part], rms[:, part], half_neg[:, part], ALU.pow).then_inc(rms_ok, 1)
            def h2_parts(t):
                pool.wait_ge(parts_act, 2 * t + 1)
                nc.gpsimd.tensor_tensor(rest, H[:, t, :], h2_part(0)[:, t, :], ALU.subtract).then_inc(rest_ok, 1)
                pool.wait_ge(rest_ok, t + 1)
                pool.wait_ge(parts_act, 2 * t + 2)
                nc.gpsimd.tensor_tensor(h2_part(2)[:, t, :], rest, h2_part(1)[:, t, :], ALU.subtract).then_inc(part_ok, 1)
                pool.wait_ge(part_ok, t + 1)

            split_lo("xq0")
            for n in range(NT, 2 * NT):
                layer_rstd(n)
            split_lo("xo1")
            for n in range(2 * NT, 3 * NT):
                if n == 3 * NT - 1:
                    h2_parts(0)
                layer_rstd(n)
            for t in range(1, NT):
                h2_parts(t)

            def scatter(u, rows):
                pool.indirect_dma_start(y_dram, bass.IndirectOffsetOnAxis(sidx[0:rows, u:u + 1], 0), yrow(u)[0:rows], None,
                                        bounds_check=2 * SEQ - 1, oob_is_err=False).then_inc(row_out[u], 16)

            pool.wait_ge(table_ok, 1)
            pairs = pool.value_load(n_pairs, min_val=NE // 2, max_val=NE // 2 * LEVELS)
            nc.gpsimd.tensor_scalar(H[:, :, :].rearrange("p t f -> p (t f)"), H[:, :, :].rearrange("p t f -> p (t f)"),
                                    ALPHA, None, ALU.mult).then_inc(alpha_ok, 1)
            def visits(p):
                for u in range(2):
                    now = pool.value_load(countJ[:, col_of(p, u)], min_val=0, max_val=SEQ)
                    pool.wait_ge(sidx_ok, p * 2 + (u + 1))
                    for s in range(2):
                        pool.wait_ge(ya_ok[s], p * 2 + (u + 1))
                        pool.wait_ge(yd_ok[s], p * 2 + (u + 1))
                    pool.sem_inc(pool_turn, 1)
                    with pool.If(now > HALF):
                        scatter(u, P)
                    with pool.Else():
                        scatter(u, HALF)

            visits(0)
            with pool.Fori(1, pairs) as p:
                visits(p)
            pool.sem_inc(pool_turn, 1)
            for n in range(3 * NT, 4 * NT):
                layer_rstd(n)

        @block.scalar
        def _(act):
            act.dma_start(relb[:, :], rel_bias).then_inc(table_in, 16)
            act.dma_start(onehot, bucket_onehot).then_inc(table_in, 16)
            act.dma_start(maskrow, band_mask).then_inc(table_in, 16)

            def load_norm(i, g, b):
                act.wait_ge(h_ok, NT * i)
                act.dma_start(lnG[:, :], g.partition_broadcast(P)).then_inc(lng_in[i], 16)
                act.dma_start(lnB[:, :], b.partition_broadcast(P)).then_inc(lng_in[i], 16)

            def job_copy(job, dst, src, scale=1.0):
                act.wait_ge(job_done, job + 1)
                nc.scalar.activation(dst, src, ACT.Copy, scale=scale).then_inc(evac_act, 1)

            def my_jobs(name):
                return [i for i, job in enumerate(JOBS[name]) if EVAC[job] == "A"]

            def split_hi(name):
                i = SLABS.index(name)
                if i:
                    act.wait_ge(slab_in[i % STAGES], landings(name))
                if i >= 2:
                    act.wait_ge(job_done, LAST[SLABS[i - 2]] + 1)
                for c in range(PIECES):
                    if i == 0:
                        act.wait_ge(first_in[c], 16)
                    if name in ("wo0", "wo1"):
                        for k in range(2 * c, 2 * c + 2):
                            last = nc.scalar.activation(slab_hi(i)[:, k, :], slab(name)[:, k, :], ACT.Copy,
                                                        scale=gains[:, k:k + 1])
                    else:
                        last = nc.scalar.activation(piece(slab_hi(i), name, c), piece(slab(name), name, c), ACT.Copy)
                    last.then_inc(hi_ok, 1)

            def tile_hi(name, i, dst, backwards=False):
                job = job_of(name, i)
                act.wait_ge(job_done, job + 1)
                nc.scalar.activation(half_tile(dst, i, backwards), PS[:, BANK[job], :].rearrange("p (c s) -> p c s", c=4),
                                     ACT.Copy).then_inc(evac_act, 1)

            for i in range(4):
                tile_hi("memT", i, memT_hi)
            split_hi("xk0")
            for i in my_jobs("xk"):
                job_copy(job_of("xk", i), xkT[:, i, :], PS[:, BANK[job_of("xk", i)], 0:MEM])
                if i % 4 == 0:
                    split_hi(("xk1", "xv0")[i // 4])
            split_hi("xv1")
            for i in my_jobs("xv"):
                job_copy(job_of("xv", i), xv[:, i % 2, 512 * (i // 2):512 * (i // 2) + 512], PS[:, BANK[job_of("xv", i)], :])
                for j in range(2 * i, 2 * i + 4):
                    tile_hi("hT", j, aT_hi)
                if i == 0:
                    split_hi("qa")
            for i in my_jobs("qa"):
                job_copy(job_of("qa", i), flipped(qaT[:, i, :]), tiles(PS[:, BANK[job_of("qa", i)], :]), -HD ** -0.5)
                if i == 0:
                    split_hi("kava")
            split_hi("qb")
            act.wait_ge(job_done, job_of("ka", 0) + 1)
            for g in range(2):
                for part in range(2):
                    last = nc.scalar.activation(kaT(g)[HD * part:HD * part + HD, :],
                                                PS[HD * g:HD * g + HD, BANK[job_of("ka", 0)], :], ACT.Copy)
            last.then_inc(evac_act, 1)
            for i in my_jobs("qb"):
                job_copy(job_of("qb", i), flipped(qbT[:, i, :]), tiles(PS[:, BANK[job_of("qb", i)], :]), -HD ** -0.5)
                if i == 0:
                    split_hi("kb")
            for i in my_jobs("kb"):
                job_copy(job_of("kb", i), kbT[:, i, :], PS[:, BANK[job_of("kb", i)], :])
                if i == 0:
                    split_hi("vb")
            act.wait_ge(gain_in, 32)
            for i in my_jobs("vb"):
                job_copy(job_of("vb", i), vb[:, i, :], PS[:, BANK[job_of("vb", i)], :])
                if i == 0:
                    split_hi("wo0")

            def sum_squares(g, t):
                nc.scalar.activation(XW[:, 0:512], Y[:, t, 512 * g:512 * g + 512], ACT.Square,
                                     accum_out=ssq[:, NT * g + t:NT * g + t + 1]).then_inc(ssq_ok, 1)
                act.wait_ge(ssq_ok, NT * g + t + 1)

            for m in range(34):
                if m < 32:
                    for n in (2 * m, 2 * m + 1):
                        w = P * len(keys_of(n // 8, (n // 2) % 4))
                        act.wait_ge(l_done, n + 1)
                        nc.scalar.activation(prob(n % 4)[:, 0:w], prob(n % 4)[:, 0:w], ACT.Exp, bias=nmax[:, n:n + 1],
                                             scale=-1.0, accum_out=rsum[:, n:n + 1]).then_inc(e_done, 1)
                if 1 <= m <= 32:
                    n = 2 * (m - 1)
                    w = P * len(keys_of(n // 8, (n // 2) % 4))
                    act.wait_ge(t_done, n + 1)
                    if n >= 4:
                        act.wait_ge(pv_done, n - 3)
                    nc.scalar.activation(probT(n % 4)[:, 0:w], PS[:, 4 + n % 2, 0:w], ACT.Copy).then_inc(pt_act, 1)
                if m >= 5 and (m - 2) % 4 == 3 and PAIRS[(m - 2) // 4][0] == "A":
                    act.wait_ge(sinkd_ok, (m - 2) // 4 + 1)
                    nc.scalar.activation(sinkx[:, :], sinkx[:, :], ACT.Exp).then_inc(sinke_ok, 1)
                if m == 18:
                    act.wait_ge(y_ok, 4)
                    load_norm(1, ln1_g, ln1_b)
                    for t in range(NT):
                        sum_squares(0, t)
            for i in range(4):
                tile_hi("yT", i, yT_hi, backwards=True)
            act.wait_ge(y_ok, 8)
            for t in range(NT):
                sum_squares(1, t)
            for i in range(4, 8):
                tile_hi("yT", i, yT_hi, backwards=True)
            split_hi("wo1")
            split_hi("xq0")
            for i in range(8):
                tile_hi("h1T", i, aT_hi)

            def q_copy(i):
                job_copy(job_of("xq", i), xqT[:, i, :], PS[:, BANK[job_of("xq", i)], :], -XD ** -0.5)

            q_copy(0)
            split_hi("xq1")
            q_copy(2)

            def o_copy(h):
                for c in range(2):
                    act.wait_ge(xpv_done, 2 * h + c + 1)
                    nc.scalar.activation(yT_hi[:, 2 * h + c, :], PS[:, 6 + c, :], ACT.Copy).then_inc(xo_act, 1)

            def exps(h):
                for u in (2 * h, 2 * h + 1):
                    act.wait_ge(xm_done, u + 1)
                    if h >= 2:
                        act.wait_ge(xt_done, h - 1)
                    for i in range(2):
                        nc.scalar.activation(xprob(h)[:, 2 * (u % 2) + i, :], PS[:, u % 4, 256 * i:256 * i + 256], ACT.Exp,
                                             bias=xnmax[:, 2 * u + i:2 * u + i + 1], scale=-1.0,
                                             accum_out=xrsum[:, 2 * u + i:2 * u + i + 1]).then_inc(xe_done, 1)

            def turned(h):
                act.wait_ge(xt_done, h + 1)
                if h >= 2:
                    act.wait_ge(xpv_done, 2 * (h - 1))
                nc.scalar.activation(xprobT[:, h % 2, 0, :], PS[:, 4, :], ACT.Copy).then_inc(xpt_act, 1)

            exps(0)
            exps(1)
            q_copy(4)
            q_copy(6)
            split_hi("xo0")
            for h in range(XH):
                turned(h)
                if h >= 1:
                    o_copy(h - 1)
                if h + 2 < XH:
                    exps(h + 2)
            o_copy(XH - 1)
            split_hi("xo1")
            load_norm(2, ln2_g, ln2_b)
            act.dma_start(router_w[:, :, 0:NG], w_group[0].rearrange("(k p) n -> p k n", p=P)).then_inc(router_in, 16)
            act.dma_start(router_w[:, :, NG:NR], w_router[0].rearrange("(k p) n -> p k n", p=P)).then_inc(router_in, 16)
            act.dma_start(router_b[:, 0:NG], b_group.partition_broadcast(P)).then_inc(router_in, 16)
            act.dma_start(router_b[:, NG:NR], b_router.partition_broadcast(P)).then_inc(router_in, 16)
            def h2_parts(t):
                act.wait_ge(h_ok, 2 * NT + t + 1)
                nc.scalar.activation(h2_part(0)[:, t, :], H[:, t, :], ACT.Copy).then_inc(parts_act, 1)
                act.wait_ge(rest_ok, t + 1)
                nc.scalar.activation(h2_part(1)[:, t, :], rest, ACT.Copy).then_inc(parts_act, 1)

            for i in my_jobs("h2T"):
                if i == 4:
                    h2_parts(0)
                job_copy(job_of("h2T", i), half_tile(h2T, i),
                         PS[:, BANK[job_of("h2T", i)], :].rearrange("p (c s) -> p c s", c=4))
            for t in range(1, NT):
                h2_parts(t)
            load_norm(3, ln3_g, ln3_b)
            act.wait_ge(gexp_in, 1)
            nc.scalar.activation(gexp, gexp, ACT.Exp).then_inc(gexp_ok, 1)
            act.wait_ge(gexp_in, 2)
            nc.scalar.activation(small[:, 4, :], small[:, 4, :], ACT.Exp).then_inc(gexp_ok, 1)

            act.wait_ge(table_ok, 1)
            pairs = act.value_load(n_pairs, min_val=NE // 2, max_val=NE // 2 * LEVELS)

            def rows_of(s, count):
                act.wait_ge(rows_done[s], count)
                nc.scalar.activation(xg(s), PS[:, 2 + s, :], ACT.Copy).then_inc(rows_ok[s], 1)

            def xgt_of(u, s, count):
                act.wait_ge(xt2_done[s], count)
                dst = xgT(u).rearrange("p (b c) s -> p c b s", b=2)[:, :, :, HALF * s:HALF * s + HALF]
                nc.scalar.activation(dst, from_halves(s), ACT.Copy).then_inc(xgt_ok[s], 1)

            first_n = act.value_load(countJ[:, 0:1], min_val=0, max_val=SEQ)
            rows_of(0, 1)
            with act.If(first_n > HALF):
                rows_of(1, 1)
            with act.Else():
                act.sem_inc(rows_ok[1], 1)
            xgt_of(0, 0, 1)
            with act.If(first_n > HALF):
                xgt_of(0, 1, 1)
            with act.Else():
                act.sem_inc(xgt_ok[1], 1)

            def visits(p):
                for u in range(2):
                    n = act.value_load(countJ[:, col_of(p, u)], min_val=0, max_val=SEQ)
                    then = act.value_load(countJ[:, col_of(p, u + 1)], min_val=0, max_val=SEQ)

                    def silu_of(s):
                        act.wait_ge(gu_done[s], p * 2 + (u + 1))
                        nc.scalar.activation(silu[HALF:P, s, :], PS[0:HALF, s, :], ACT.Silu).then_inc(silu_ok[s], 1)

                    def y_left(s):
                        act.wait_ge(down_done[s], p * 2 + (u + 1))
                        nc.scalar.activation(yrow(u)[HALF * s:HALF * s + HALF, 0:512], PS[0:HALF, 5 + s, :],
                                             ACT.Copy).then_inc(ya_ok[s], 1)

                    silu_of(0)
                    with act.If(n > HALF):
                        silu_of(1)
                    with act.Else():
                        act.sem_inc(silu_ok[1], 1)
                    rows_of(0, p * 2 + (u + 2))
                    with act.If(then > HALF):
                        rows_of(1, p * 2 + (u + 2))
                    with act.Else():
                        act.sem_inc(rows_ok[1], 1)
                    xgt_of(1 - u, 0, p * 2 + (u + 2))
                    with act.If(then > HALF):
                        xgt_of(1 - u, 1, p * 2 + (u + 2))
                    with act.Else():
                        act.sem_inc(xgt_ok[1], 1)
                    if not first_pair(p):
                        act.wait_ge(row_out[u], p * 16)
                    y_left(0)
                    with act.If(n > HALF):
                        y_left(1)
                    with act.Else():
                        act.sem_inc(ya_ok[1], 1)

            visits(0)
            with act.Fori(1, pairs) as p:
                visits(p)

        @block.vector
        def _(dve):
            chain = [0]

            def link(ins):
                chain[0] += 1
                ins.then_inc(dve_chain, 1)
                dve.wait_ge(dve_chain, chain[0])

            def my_jobs(name):
                return [i for i, job in enumerate(JOBS[name]) if EVAC[job] == "D"]

            def job_copy(job, dst, src, scale=1.0):
                dve.wait_ge(job_done, job + 1)
                if scale == 1.0:
                    nc.vector.tensor_copy(dst, src).then_inc(evac_dve, 1)
                else:
                    nc.vector.tensor_scalar(dst, src, scale, None, ALU.mult).then_inc(evac_dve, 1)

            def norm_stats(n):
                t = n % NT
                if n < NT:
                    dve.wait_ge(x_in[t], 16)
                for c in range(2):
                    last = nc.vector.bn_stats(stats[:, t, c, :], H[:, t, 512 * c:512 * c + 512])
                link(last)
                nc.vector.bn_aggr(meanvar[:, t, :], stats[:, t, :, :].rearrange("p c s -> p (c s)")).then_inc(var_ok, 1)

            def norm_apply(n):
                t = n % NT
                dve.wait_ge(var_ok, n + 1)
                dve.wait_ge(lng_in[n // NT], 32)
                link(nc.vector.scalar_tensor_tensor(H[:, t, :], H[:, t, :], meanvar[:, t, 0:1], lnG[:, :],
                                                    ALU.subtract, ALU.mult))
                dve.wait_ge(rstd_ok, n + 1)
                nc.vector.scalar_tensor_tensor(H[:, t, :], H[:, t, :], rstd[:, t:t + 1], lnB[:, :],
                                               ALU.mult, ALU.add).then_inc(h_ok, 1)

            def split_lo(name):
                i = SLABS.index(name)
                for c in range(PIECES):
                    dve.wait_ge(hi_ok, PIECES * i + c + 1)
                    if name in ("wo0", "wo1"):
                        for k in range(2 * c, 2 * c + 2):
                            last = nc.vector.scalar_tensor_tensor(slab_lo(i)[:, k, :], slab(name)[:, k, :], gains[:, k:k + 1],
                                                                  slab_hi(i)[:, k, :].bitcast(F32), ALU.mult, ALU.subtract)
                    else:
                        last = nc.vector.tensor_tensor(piece(slab_lo(i), name, c), piece(slab(name), name, c),
                                                       piece(slab_hi(i), name, c).bitcast(F32), ALU.subtract)
                    last.then_inc(lo_dve, 1)

            def tile_lo(name, i, hi, lo, backwards=False):
                job = job_of(name, i)
                dve.wait_ge(job_done, job + 1)
                dve.wait_ge(evac_act, evacs("A", job))
                nc.vector.tensor_tensor(half_tile(lo, i, backwards), PS[:, BANK[job], :].rearrange("p (c s) -> p c s", c=4),
                                        half_tile(hi, i, backwards).bitcast(F32), ALU.subtract).then_inc(evac_dve, 1)

            for i in range(4):
                tile_lo("memT", i, memT_hi, memT_lo)
            split_lo("xk0")
            for i in my_jobs("xk"):
                job_copy(job_of("xk", i), xkT[:, i, :], PS[:, BANK[job_of("xk", i)], 0:MEM])
                if i == 1:
                    split_lo("xk1")
                if i == 3:
                    for t in range(NT):
                        norm_stats(t)
                if i == 5:
                    norm_apply(0)
                    split_lo("xv0")
                if i == 7:
                    norm_apply(1)
            dve.wait_ge(table_in, 48)
            for i in range(2):
                job = job_of("bias", i)
                dve.wait_ge(job_done, job + 1)
                nc.vector.scalar_tensor_tensor(biasrow[:, 512 * i:512 * i + 512], PS[0:16, BANK[job], :], -1.0,
                                               maskrow[:, 512 * i:512 * i + 512], ALU.mult, ALU.add).then_inc(evac_dve, 1)
            norm_apply(2)
            norm_apply(3)
            for i in my_jobs("xv"):
                if i == 3:
                    for j in range(4, 8):
                        tile_lo("hT", j, aT_hi, aT_lo)
                job_copy(job_of("xv", i), xv[:, i % 2, 512 * (i // 2):512 * (i // 2) + 512], PS[:, BANK[job_of("xv", i)], :])
                if i == 1:
                    for j in range(4):
                        tile_lo("hT", j, aT_hi, aT_lo)
                    split_lo("qa")
            dve.wait_ge(small_in, 16)
            link(nc.vector.tensor_scalar(nsink[:, :], nsink[:, :], -1.0, None, ALU.mult))
            for i in my_jobs("qa"):
                job_copy(job_of("qa", i), flipped(qaT[:, i, :]), tiles(PS[:, BANK[job_of("qa", i)], :]), -HD ** -0.5)
                if i == 1:
                    split_lo("kava")
            split_lo("qb")
            job_copy(job_of("va", 0), va.rearrange("p t f -> p (t f)"), PS[:, BANK[job_of("va", 0)], :])
            for i in my_jobs("qb"):
                job_copy(job_of("qb", i), flipped(qbT[:, i, :]), tiles(PS[:, BANK[job_of("qb", i)], :]), -HD ** -0.5)
                if i == 1:
                    split_lo("kb")
            for i in my_jobs("kb"):
                job_copy(job_of("kb", i), kbT[:, i, :], PS[:, BANK[job_of("kb", i)], :])
                if i == 1:
                    split_lo("vb")
            for i in my_jobs("vb"):
                job_copy(job_of("vb", i), vb[:, i, :], PS[:, BANK[job_of("vb", i)], :])
                if i == 1:
                    split_lo("wo0")

            for m in range(34):
                if m < 32:
                    for n in (2 * m, 2 * m + 1):
                        pair, tile, hb = n // 8, (n // 2) % 4, n % 2
                        keys = keys_of(pair, tile)
                        w = P * len(keys)
                        x0 = TZ0 + P * (keys[0] - tile)
                        q = 2 * pair + hb
                        head = head_of(pair, hb)
                        if pair < 4:
                            dve.wait_ge(toep_a_in, 16)
                            bias = toep_a(head)[:, x0 - (TZ0 - P):x0 - (TZ0 - P) + w]
                        else:
                            dve.wait_ge(toep_b_in[q % 4], 16 * (q // 4 - 1))
                            bias = toep_b(q % 4)[:, x0:x0 + w]
                        dve.wait_ge(s_done, n + 1)
                        if n >= 4:
                            dve.wait_ge(t_done, n - 3)
                        nc.vector.tensor_tensor_reduce(
                            out=prob(n % 4)[:, 0:w], in0=PS[:, n % 4, 0:w], in1=bias, scale=1.0,
                            scalar=nsink[:, head:head + 1] if head < 8 else 3e38, op0=ALU.add, op1=ALU.min,
                            accum_out=nmax[:, n:n + 1]).then_inc(l_done, 1)
                if 1 <= m <= 32:
                    n = 2 * (m - 1) + 1
                    w = P * len(keys_of(n // 8, (n // 2) % 4))
                    dve.wait_ge(t_done, n + 1)
                    if n >= 4:
                        dve.wait_ge(pv_done, n - 3)
                    nc.vector.tensor_copy(probT(n % 4)[:, 0:w], PS[:, 4 + n % 2, 0:w]).then_inc(pt_dve, 1)
                if m >= 5 and (m - 2) % 4 == 3:
                    pair = (m - 2) // 4
                    group, j = PAIRS[pair]
                    part = slice(8 * pair, 8 * pair + 8)
                    dve.wait_ge(e_done, 8 * pair + 8)
                    if group == "A":
                        sk = nsink[:, 2 * j:2 * j + 2].unsqueeze(1).to_broadcast([P, NT, 2])
                        if pair:
                            dve.wait_ge(sinke_ok, pair)
                        nc.vector.tensor_tensor(sinkx[:, :].rearrange("p (i b) -> p i b", b=2),
                                                nmax[:, part].rearrange("p (i b) -> p i b", b=2), sk,
                                                ALU.subtract).then_inc(sinkd_ok, 1)
                        dve.wait_ge(sinke_ok, pair + 1)
                        link(nc.vector.tensor_tensor(rsum[:, part], rsum[:, part], sinkx[:, :], ALU.add))
                    dst = Y[:, :, P * pair:P * pair + P].rearrange("p t (b d) -> p t b d", b=2)
                    link(nc.vector.reciprocal(rinv[:, part], rsum[:, part]))
                    dve.wait_ge(pv_done, 8 * pair + 8)
                    inv = rinv[:, part].rearrange("p (i b) -> p i b", b=2).unsqueeze(3).to_broadcast([P, NT, 2, HD])
                    nc.vector.tensor_tensor(dst, PS[:, 6 + pair % 2, :].rearrange("p (i b d) -> p i b d", b=2, d=HD),
                                            inv, ALU.mult).then_inc(y_ok, 1)
                if m == 22:
                    dve.wait_ge(rms_ok, 1)
                    for t in range(NT):
                        nc.vector.tensor_scalar(Y[:, t, 0:512], Y[:, t, 0:512], rms[:, t:t + 1], None,
                                                ALU.mult).then_inc(yn_ok, 1)
            for i in range(4):
                tile_lo("yT", i, yT_hi, yT_lo, backwards=True)
            dve.wait_ge(rms_ok, 2)
            for t in range(NT):
                nc.vector.tensor_scalar(Y[:, t, 512:1024], Y[:, t, 512:1024], rms[:, NT + t:NT + t + 1], None,
                                        ALU.mult).then_inc(yn_ok, 1)
            for i in range(4, 8):
                tile_lo("yT", i, yT_hi, yT_lo, backwards=True)
            split_lo("wo1")

            def residual(name, i, norm):
                job, hf, t = job_of(name, i), i // 4, i % 4
                cols = slice(512 * hf, 512 * hf + 512)
                dve.wait_ge(job_done, job + 1)
                nc.vector.scalar_tensor_tensor(H[:, t, cols], H[:, t, cols], ALPHA, PS[:, BANK[job], :], ALU.mult,
                                               ALU.add).then_inc(evac_dve, 1)
                if hf:
                    dve.wait_ge(evac_dve, evacs("D", job))
                    norm_stats(NT * norm + t)
                    norm_apply(NT * norm + t)

            for i in range(7):
                residual("mix", i, 1)
            for i in range(4):
                tile_lo("h1T", i, aT_hi, aT_lo)
            residual("mix", 7, 1)
            for i in range(4, 8):
                tile_lo("h1T", i, aT_hi, aT_lo)

            def q_copy(i):
                job_copy(job_of("xq", i), xqT[:, i, :], PS[:, BANK[job_of("xq", i)], :], -XD ** -0.5)

            q_copy(1)
            split_lo("xq1")
            q_copy(3)

            def o_copy(h):
                for c in range(2):
                    dve.wait_ge(xo_act, 2 * h + c + 1)
                    nc.vector.tensor_tensor(aT_lo[:, 2 * h + c, :], PS[:, 6 + c, :], yT_hi[:, 2 * h + c, :].bitcast(F32),
                                            ALU.subtract).then_inc(xo_dve, 1)

            def minima(h):
                for u in (2 * h, 2 * h + 1):
                    dve.wait_ge(xs_done, u + 1)
                    nc.vector.tensor_reduce(xnmax[:, 2 * u:2 * u + 2], PS[:, u % 4, :].rearrange("p (i m) -> p i m", i=2),
                                            AX, ALU.min).then_inc(xm_done, 1)

            def divided(h):
                for u in (2 * h, 2 * h + 1):
                    dve.wait_ge(xe_done, 2 * u + 2)
                    link(nc.vector.reciprocal(xrinv[:, 2 * u:2 * u + 2], xrsum[:, 2 * u:2 * u + 2]))
                    for i in range(2):
                        row = xprob(h)[:, 2 * (u % 2) + i, :]
                        nc.vector.tensor_scalar(row, row, xrinv[:, 2 * u + i:2 * u + i + 1], None, ALU.mult).then_inc(xp_done, 1)

            def turned(h):
                dve.wait_ge(xt_done, h + 1)
                if h >= 2:
                    dve.wait_ge(xpv_done, 2 * (h - 1))
                nc.vector.tensor_copy(xprobT[:, h % 2, 1, :], PS[:, 5, :]).then_inc(xpt_dve, 1)

            minima(0)
            minima(1)
            divided(0)
            divided(1)
            q_copy(5)
            q_copy(7)
            split_lo("xo0")
            for h in range(XH):
                if h + 2 < XH:
                    minima(h + 2)
                turned(h)
                if h >= 1:
                    o_copy(h - 1)
                if h + 2 < XH:
                    divided(h + 2)
            o_copy(XH - 1)

            def h2_copy(i):
                if EVAC[job_of("h2T", i)] == "D":
                    job_copy(job_of("h2T", i), half_tile(h2T, i),
                             PS[:, BANK[job_of("h2T", i)], :].rearrange("p (c s) -> p c s", c=4))

            for i in range(7):
                residual("xo", i, 2)
            for i in range(4):
                h2_copy(i)
            residual("xo", 7, 2)
            for i in range(4, 8):
                h2_copy(i)

            over = lambda ap, n: ap.unsqueeze(2).to_broadcast([P, NT, n])
            tt, ts, stt = nc.vector.tensor_tensor, nc.vector.tensor_scalar, nc.vector.scalar_tensor_tensor
            reduce = nc.vector.tensor_reduce
            dve.wait_ge(router_in, 64)
            dve.wait_ge(logits_done, NT)
            link(tt(lg, PS[:, 4, 0:NT * NR].rearrange("p (t c) -> p t c", t=NT),
                    router_b[:, :].unsqueeze(1).to_broadcast([P, NT, NR]), ALU.add))
            gl, el = lg[:, :, 0:NG], lg[:, :, NG:NR]

            def first_of(dst, values, n, top, at):
                link(reduce(top, values, AX, ALU.max))
                link(tt(dst, values, over(top, n), ALU.is_equal))
                link(stt(dst, dst, -100.0, iota_e[:, 0:n].unsqueeze(1).to_broadcast([P, NT, n]), ALU.mult, ALU.add))
                link(reduce(at, dst, AX, ALU.min))
                link(tt(dst, dst, over(at, n), ALU.is_equal))

            first_of(gsel, gl, NG, small[:, 0, :], small[:, 1, :])
            tt(gexp, gl, over(small[:, 0, :], NG), ALU.subtract).then_inc(gexp_in, 1)
            link(ts(tmp[:, :, 0:NG], gsel, -1.0, BIG, ALU.add, ALU.mult))
            group = lambda ap: ap.unsqueeze(3).to_broadcast([P, NT, NG, EG])
            by_group = lambda ap: ap.rearrange("p t (g e) -> p t g e", g=NG)
            link(tt(by_group(es), by_group(el), group(gsel), ALU.mult))
            link(tt(by_group(es), by_group(es), group(tmp[:, :, 0:NG]), ALU.add))
            first_of(first, es, NE, small[:, 2, :], small[:, 1, :])
            link(stt(es, first, -3 * BIG, es, ALU.mult, ALU.add))
            first_of(second, es, NE, small[:, 3, :], small[:, 1, :])
            link(tt(chosen, first, second, ALU.add))
            nc.vector.engine_nop().then_inc(chosen_ok, 1)
            tt(small[:, 4, :], small[:, 3, :], small[:, 2, :], ALU.subtract).then_inc(gexp_in, 1)
            link(stt(tmp, second, 2.0, first, ALU.mult, ALU.add))
            link(nc.vector.tensor_copy(rankJ.rearrange("p t (l e) -> p t l e", e=NE),
                                       tmp.unsqueeze(2).to_broadcast([P, NT, LEVELS + 1, NE])))
            dve.wait_ge(pos_done, 1)
            link(stt(tmp, PS[:, 5, 0:P].rearrange("p (t c) -> p t c", t=NT), 1.0, chosen, ALU.add, ALU.mult))
            link(ts(posJ[:, :, 0:NE], tmp, -1.0, None, ALU.add))

            def pick_rows(u, col):
                for t in range(NT):
                    ts(pick(u)[:, t, :], iota_s[:, :], posJ[:, t, col], None, ALU.is_equal)
                    last = ts(ranked(u)[:, t, :], iota_s[:, :], posJ[:, t, col], rankJ[:, t, col], ALU.is_equal, ALU.mult)
                last.then_inc(pick_ok, 1)

            pick_rows(0, slice(0, 1))
            counts = PS[0:1, 5, P:P + NE]
            for level in range(LEVELS + 1):
                ts(countJ[:, NE * level:NE * level + NE], counts, -1.0 * P * level, 0.0, ALU.add, ALU.max)
            link(reduce(lev[:, 0:1], counts, AX, ALU.max))
            link(ts(lev[:, 1:2], lev[:, 0:1], 1.0 * P, 1.0, ALU.is_gt, ALU.add))
            for level in range(2, LEVELS):
                link(stt(lev[:, 1:2], lev[:, 0:1], 1.0 * P * level, lev[:, 1:2], ALU.is_gt, ALU.add))
            ts(n_pairs, lev[:, 1:2], NE / 2, None, ALU.mult).then_inc(table_ok, 1)
            for level in range(1, LEVELS + 1):
                last = ts(posJ[:, :, NE * level:NE * level + NE], tmp, -1.0 - P * level, None, ALU.add)
            link(last)
            pick_rows(1, slice(1, 2))

            def tokens_of_slots(u, wait_for):
                idx = PS[:, 7, 0:3]
                ts(idxf[:, 0:1], idx[:, 0:1], -0.5, 1.5, ALU.mult, ALU.add)
                ts(idxf[:, 2:3], idx[:, 0:1], 0.0, 1.0 * OOB, ALU.is_equal, ALU.mult)
                ts(idxf[:, 3:4], idx[:, 0:1], 1.0 * SEQ, -1.0 * SEQ, ALU.mult, ALU.add)
                wait_for(ts(idxf[:, 1:2], idx[:, 2:3], 1.0 * P, None, ALU.mult))
                wait_for(tt(idxf[:, 1:2], idxf[:, 1:2], idx[:, 1:2], ALU.add))
                wait_for(stt(idxf[:, 4:5], idxf[:, 1:2], idxf[:, 0:1], idxf[:, 2:3], ALU.mult, ALU.add))
                tt(sidx_next[:, u:u + 1], idxf[:, 4:5], idxf[:, 3:4], ALU.add).then_inc(idx_ok, 1)

            dve.wait_ge(idxmm_done, 1)
            tokens_of_slots(0, link)
            dve.wait_ge(gexp_ok, 2)
            link(reduce(small[:, 5, :], gexp, AX, ALU.add))
            link(nc.vector.reciprocal(small[:, 6, :], small[:, 5, :]))
            link(ts(small[:, 7, :], small[:, 4, :], 1.0, None, ALU.add))
            link(nc.vector.reciprocal(small[:, 8, :], small[:, 7, :]))
            link(tt(gatew[:, :, 0], small[:, 8, :], small[:, 6, :], ALU.mult))
            link(tt(gatew[:, :, 1], gatew[:, :, 0], small[:, 4, :], ALU.mult))

            dve.wait_ge(table_ok, 1)
            pairs = dve.value_load(n_pairs, min_val=NE // 2, max_val=NE // 2 * LEVELS)

            per_visit = 3
            def visits(p):
                for u in range(2):
                    seen = [0]

                    def loop_link(ins):
                        seen[0] += 1
                        ins.then_inc(dve_loop, 1)
                        dve.wait_ge(dve_loop, p * (2 * per_visit) + (per_visit * u + seen[0]))

                    n = dve.value_load(countJ[:, col_of(p, u)], min_val=0, max_val=SEQ)
                    if not first_pair(p):
                        dve.wait_ge(row_out[u], p * 16)
                    dve.wait_ge(idx_ok, p * 2 + (u + 1))
                    nc.vector.tensor_copy(sidx[:, u:u + 1], sidx_next[:, u:u + 1]).then_inc(sidx_ok, 1)
                    dve.wait_ge(idxmm_done, p * 2 + (u + 1))
                    pick_rows(u, col_of(p, u + 2))

                    def gated(s):
                        dve.wait_ge(silu_ok[s], p * 2 + (u + 1))
                        tt(hid[HALF * s:HALF * s + HALF, :], silu[HALF:P, s, :], PS[HALF:P, s, :],
                           ALU.mult).then_inc(hid_ok[s], 1)

                    def y_right(s):
                        dve.wait_ge(down_done[s], p * 2 + (u + 1))
                        nc.vector.tensor_copy(yrow(u)[HALF * s:HALF * s + HALF, 512:1024],
                                              PS[HALF:P, 5 + s, :]).then_inc(yd_ok[s], 1)

                    gated(0)
                    with dve.If(n > HALF):
                        gated(1)
                    with dve.Else():
                        dve.sem_inc(hid_ok[1], 1)
                    dve.wait_ge(ht_done, p * 2 + (u + 1))
                    nc.vector.tensor_copy(hidT(u), PS[:, 4, :].rearrange("p (c s) -> p c s", c=FC)).then_inc(hidt_ok, 1)
                    dve.wait_ge(idxmm_done, p * 2 + (u + 2))
                    tokens_of_slots(1 - u, loop_link)
                    assert seen[0] == per_visit
                    y_right(0)
                    with dve.If(n > HALF):
                        y_right(1)
                    with dve.Else():
                        dve.sem_inc(yd_ok[1], 1)

            visits(0)
            with dve.Fori(1, pairs) as p:
                visits(p)

            dve.wait_ge(alpha_ok, 1)
            for t in range(NT):
                dve.wait_ge(comb_in[t % 2], 16 * (t // 2 + 1))
                link(stt(H[:, t, :], comb[:, t % 2, 0, :], gatew[:, t, 0:1], H[:, t, :], ALU.mult, ALU.add))
                stt(H[:, t, :], comb[:, t % 2, 1, :], gatew[:, t, 1:2], H[:, t, :], ALU.mult, ALU.add).then_inc(comb_used, 1)
                dve.wait_ge(comb_used, t + 1)
                norm_stats(3 * NT + t)
                norm_apply(3 * NT + t)

        @block.tensor
        def _(pe):
            def free(job):
                before = [j for j in range(job) if BANK[j] == BANK[job]]
                if before and EVAC[before[-1]] == "A":
                    pe.wait_ge(evac_act, evacs("A", before[-1]))
                elif before:
                    pe.wait_ge(evac_dve, evacs("D", before[-1]))

            def transposes(job, src, width=4):
                for c in range(width):
                    last = nc.tensor.transpose(PS[:, BANK[job], P * c:P * c + P], src[:, P * c:P * c + P], ident[:, :])
                last.then_inc(job_done, 1)

            def product(dst, lhs, rhs, first_of=None, chunks=(0, KC)):
                for k in range(*chunks):
                    if first_of and k % (KC // PIECES) == 0:
                        lo_written(pe, first_of, k * PIECES // KC + 1)
                    (l_hi, l_lo), (r_hi, r_lo) = lhs(k), rhs(k)
                    nc.tensor.matmul(dst, l_hi, r_hi, start=(k == 0), stop=False)
                    nc.tensor.matmul(dst, l_hi, r_lo, start=False, stop=False)
                    last = nc.tensor.matmul(dst, l_lo, r_hi, start=False, stop=(k == KC - 1))
                return last

            def weight_columns(name, c):
                i, cols = SLABS.index(name), slice(P * c, P * c + P)
                return lambda k: (slab_hi(i)[:, k, cols], slab_lo(i)[:, k, cols])

            def weight_rows(name, cols=slice(0, 512)):
                i = SLABS.index(name)
                return lambda k: (slab_hi(i)[:, k, cols], slab_lo(i)[:, k, cols])

            def act_columns(hi, lo, t):
                return lambda k: (hi[:, k, P * t:P * t + P], lo[:, k, P * t:P * t + P])

            def act_rows(hi, lo, cols=slice(None)):
                return lambda k: (hi[:, k, cols], lo[:, k, cols])

            pe.wait_ge(ident_ok, 1)
            for i in range(4):
                pe.wait_ge(mem_in[i // 2], 16)
                transposes(job_of("memT", i), memR[:, i // 2, 512 * (i % 2):512 * (i % 2) + 512])
            waits_evac(pe, job_of("memT", 3))
            for i in range(4):
                free(job_of("xk", i))
            for c in range(PIECES):
                for i in range(4):
                    last = product(PS[:, BANK[job_of("xk", i)], 0:MEM], weight_columns("xk0", i), act_rows(memT_hi, memT_lo),
                                   "xk0", (2 * c, 2 * c + 2))
                    if c == PIECES - 1:
                        last.then_inc(job_done, 1)
            for i in range(4, 8):
                name = f"xk{i // 4}"
                free(job_of("xk", i))
                product(PS[:, BANK[job_of("xk", i)], 0:MEM], weight_columns(name, i % 4), act_rows(memT_hi, memT_lo),
                        name if i % 4 == 0 else None).then_inc(job_done, 1)
            pe.wait_ge(table_in, 48)
            for i in range(2):
                job = job_of("bias", i)
                free(job)
                nc.tensor.matmul(PS[0:16, BANK[job], :], relb[:, :], onehot[:, 512 * i:512 * i + 512], start=True,
                                 stop=True).then_inc(job_done, 1)
            for i in range(4):
                name = f"xv{i // 2}"
                free(job_of("xv", i))
                product(PS[:, BANK[job_of("xv", i)], :], act_columns(memT_hi, memT_lo, i % 2), weight_rows(name),
                        name if i % 2 == 0 else None).then_inc(job_done, 1)
                if i in (1, 2):
                    for j in range(4 * i - 4, 4 * i):
                        pe.wait_ge(h_ok, j // 2 + 1)
                        free(job_of("hT", j))
                        transposes(job_of("hT", j), H[:, j // 2, 512 * (j % 2):512 * (j % 2) + 512])
            waits_evac(pe, job_of("hT", 7))

            def from_columns(job, name, c):
                free(job)
                product(PS[:, BANK[job], :], weight_columns(name, c), act_rows(aT_hi, aT_lo),
                        name if c == 0 else None).then_inc(job_done, 1)

            for i in range(4):
                from_columns(job_of("qa", i), "qa", i)
            from_columns(job_of("ka", 0), "kava", 0)
            job = job_of("va", 0)
            free(job)
            for t in range(NT):
                last = product(PS[:, BANK[job], P * t:P * t + P], act_columns(aT_hi, aT_lo, t), weight_rows("kava", slice(P, 2 * P)))
            last.then_inc(job_done, 1)
            for name in ("qb", "kb"):
                for i in range(4):
                    from_columns(job_of(name, i), name, i)
            for i in range(4):
                free(job_of("vb", i))
                product(PS[:, BANK[job_of("vb", i)], :], act_columns(aT_hi, aT_lo, i), weight_rows("vb"),
                        "vb" if i == 0 else None).then_inc(job_done, 1)
            waits_evac(pe, job_of("vb", 3))

            def scores(n):
                pair, tile, hb = n // 8, (n // 2) % 4, n % 2
                group, j = PAIRS[pair]
                qT, kT = (qaT[:, j, :], kaT(j // 2)) if group == "A" else (qbT[:, j, :], kbT[:, j, :])
                keys = keys_of(pair, tile)
                rows = slice(HD * hb, HD * hb + HD)
                if n >= 4:
                    pe.wait_ge(l_done, n - 3)
                nc.tensor.matmul(PS[:, n % 4, 0:P * len(keys)], qT[rows, P * tile:P * tile + P],
                                 kT[rows, P * keys[0]:P * (keys[-1] + 1)], start=True, stop=True).then_inc(s_done, 1)

            def turn(n):
                keys = keys_of(n // 8, (n // 2) % 4)
                pe.wait_ge(e_done, n + 1)
                if n >= 2:
                    pe.wait_ge(pt_act if n % 2 == 0 else pt_dve, n // 2)
                for c in range(len(keys)):
                    last = nc.tensor.transpose(PS[:, 4 + n % 2, P * c:P * c + P], prob(n % 4)[:, P * c:P * c + P], ident[:, :])
                last.then_inc(t_done, 1)

            def values(n):
                pair, tile, hb = n // 8, (n // 2) % 4, n % 2
                group, j = PAIRS[pair]
                keys = keys_of(pair, tile)
                pe.wait_ge(pt_act if n % 2 == 0 else pt_dve, n // 2 + 1)
                if n % 8 == 0 and pair >= 2:
                    pe.wait_ge(y_ok, pair - 1)
                col = 2 * tile + hb
                for c, key in enumerate(keys):
                    v = va[:, key, HD * (j // 2):HD * (j // 2) + HD] if group == "A" else vb[:, key, P * j + HD * hb:P * j + HD * hb + HD]
                    last = nc.tensor.matmul(PS[:, 6 + pair % 2, HD * col:HD * col + HD], probT(n % 4)[:, P * c:P * c + P], v,
                                            start=(c == 0), stop=(c == len(keys) - 1))
                last.then_inc(pv_done, 1)

            for m in range(34):
                if m < 32:
                    scores(2 * m)
                    scores(2 * m + 1)
                if 1 <= m <= 32:
                    turn(2 * m - 2)
                    turn(2 * m - 1)
                if m >= 2:
                    values(2 * m - 4)
                    values(2 * m - 3)

            def transpose_y(i):
                pe.wait_ge(yn_ok, i + 1)
                if i >= 4:
                    pe.wait_ge(y_ok, 8)
                free(job_of("yT", i))
                transposes(job_of("yT", i), Y[:, i % 4, 512 * (i // 4):512 * (i // 4) + 512])

            def transpose_h(name, i, norm):
                pe.wait_ge(h_ok, NT * norm + i // 2 + 1)
                free(job_of(name, i))
                transposes(job_of(name, i), H[:, i // 2, 512 * (i % 2):512 * (i % 2) + 512])

            def dense_out(name, i, slab_name, hi, lo, chunks=(0, KC)):
                job = job_of(name, i)
                if chunks[0] == 0:
                    free(job)
                last = product(PS[:, BANK[job], :], act_columns(hi, lo, i % 4), weight_rows(slab_name), slab_name, chunks)
                if chunks[1] == KC:
                    last.then_inc(job_done, 1)

            for i in range(4):
                transpose_y(i)
            waits_evac(pe, job_of("yT", 3))
            for i in range(4):
                dense_out("mix", i, "wo0", yT_hi, yT_lo, (0, 4))
            for i in range(4, 8):
                transpose_y(i)
            waits_evac(pe, job_of("yT", 7))
            for i in range(4):
                dense_out("mix", i, "wo0", yT_hi, yT_lo, (4, KC))
            for i in range(4, 7):
                dense_out("mix", i, "wo1", yT_hi, yT_lo)
            for i in range(4):
                transpose_h("h1T", i, 1)
            dense_out("mix", 7, "wo1", yT_hi, yT_lo)
            waits_evac(pe, job_of("h1T", 3))
            for half in range(2):
                cols = slice(256 * half, 256 * half + 256)
                for i in range(4):
                    job = job_of("xq", i)
                    if half == 0:
                        free(job)
                    last = product(PS[:, BANK[job], cols], weight_columns("xq0", i), act_rows(aT_hi, aT_lo, cols), "xq0")
                    if half:
                        last.then_inc(job_done, 1)
                if half == 0:
                    for i in range(4, 8):
                        transpose_h("h1T", i, 1)
                    waits_evac(pe, job_of("h1T", 7))

            def xscores(h):
                for u in (2 * h, 2 * h + 1):
                    if h >= 2:
                        pe.wait_ge(xe_done, 2 * (u - 4) + 2)
                    for i in range(2):
                        tile = 2 * (u % 2) + i
                        for c in range(2):
                            last = nc.tensor.matmul(PS[:, u % 4, 256 * i:256 * i + 256],
                                                    xqT[:, 2 * h + c, P * tile:P * tile + P], xkT[:, 2 * h + c, :],
                                                    start=(c == 0), stop=(c == 1))
                    last.then_inc(xs_done, 1)

            def xvalues(h):
                pe.wait_ge(xpt_act, h + 1)
                pe.wait_ge(xpt_dve, h + 1)
                for c in range(2):
                    if h:
                        pe.wait_ge(xo_dve, 2 * (h - 1) + c + 1)
                    for mt in range(MT):
                        last = nc.tensor.matmul(PS[:, 6 + c, :], xv[:, mt, XD * h + P * c:XD * h + P * c + P],
                                                xprobT[:, h % 2, mt, :], start=(mt == 0), stop=(mt == MT - 1))
                    last.then_inc(xpv_done, 1)

            def turn_x(h):
                pe.wait_ge(xp_done, 4 * h + 4)
                if h:
                    pe.wait_ge(xpt_act, h)
                    pe.wait_ge(xpt_dve, h)
                for mt in range(MT):
                    for i in range(NT):
                        last = nc.tensor.transpose(PS[:, 4 + mt, P * i:P * i + P],
                                                   xprob(h)[:, i, P * mt:P * mt + P], ident[:, :])
                last.then_inc(xt_done, 1)

            waits_evac(pe, job_of("xq", 3))
            xscores(0)
            xscores(1)
            for i in range(4):
                from_columns(job_of("xq", 4 + i), "xq1", i)
            waits_evac(pe, job_of("xq", 7))
            turn_x(0)
            xscores(2)
            turn_x(1)
            xvalues(0)
            xscores(3)
            turn_x(2)
            xvalues(1)
            turn_x(3)
            xvalues(2)
            xvalues(3)
            pe.wait_ge(xo_dve, 2 * XH - 2)
            for i in range(4):
                dense_out("xo", i, "xo0", yT_hi, aT_lo, (0, 6))
            pe.wait_ge(xo_dve, 2 * XH)
            for i in range(4):
                dense_out("xo", i, "xo0", yT_hi, aT_lo, (6, KC))
            for i in range(4, 7):
                dense_out("xo", i, "xo1", yT_hi, aT_lo)

            def router(t):
                waits_evac(pe, job_of("h2T", 2 * t + 1))
                for k in range(KC):
                    last = nc.tensor.matmul(PS[:, 4, NR * t:NR * t + NR], h2T[:, k, P * t:P * t + P], router_w[:, k, :],
                                            start=(k == 0), stop=(k == KC - 1))
                last.then_inc(logits_done, 1)

            for i in range(4):
                transpose_h("h2T", i, 2)
            dense_out("xo", 7, "xo1", yT_hi, aT_lo)
            pe.wait_ge(router_in, 64)
            router(0)
            transpose_h("h2T", 4, 2)
            transpose_h("h2T", 5, 2)
            router(1)
            transpose_h("h2T", 6, 2)
            transpose_h("h2T", 7, 2)
            router(2)
            router(3)
            pe.wait_ge(consts_ok, 1)
            pe.wait_ge(chosen_ok, 1)
            for t in range(NT):
                for s in range(t + 1):
                    nc.tensor.matmul(PS[:, 5, NE * t:NE * t + NE], before[:, :] if s == t else ones[:, :], chosen[:, s, :],
                                     start=(s == 0), stop=(s == t))
            for t in range(NT):
                last = nc.tensor.matmul(PS[:, 5, P:P + NE], ones[:, :], chosen[:, t, :], start=(t == 0), stop=(t == NT - 1))
            last.then_inc(pos_done, 1)

            def gather(u, s):
                slots = slice(HALF * s, HALF * s + HALF)
                for t in range(NT):
                    for i in range(3):
                        first, end = (t == 0 and i == 0), (t == NT - 1 and i == 2)
                        nc.tensor.matmul(PS[0:HALF, 2 + s, :], pick(u)[:, t, slots], h2_part(i)[:, t, 0:512], start=first, stop=end)
                        last = nc.tensor.matmul(PS[HALF:P, 2 + s, :], pick(u)[:, t, slots], h2_part(i)[:, t, 512:1024],
                                                start=first, stop=end)
                last.then_inc(rows_done[s], 1)

            def slot_tokens(u):
                for t in range(NT):
                    last = nc.tensor.matmul(PS[:, 7, 0:3], ranked(u)[:, t, :], numbers[:, t, :], start=(t == 0), stop=(t == NT - 1))
                last.then_inc(idxmm_done, 1)

            def turn_rows(s, count):
                pe.wait_ge(rows_ok[s], count)
                for c in range(4):
                    last = nc.tensor.transpose(PS[:, 2 + s, P * c:P * c + P], xg(s)[:, P * c:P * c + P], ident[:, :])
                last.then_inc(xt2_done[s], 1)

            pe.wait_ge(pick_ok, 1)
            pe.wait_ge(part_ok, NT)
            gather(0, 0)
            pe.wait_ge(table_ok, 1)
            first_n = pe.value_load(countJ[:, 0:1], min_val=0, max_val=SEQ)
            with pe.If(first_n > HALF):
                gather(0, 1)
            with pe.Else():
                pe.sem_inc(rows_done[1], 1)
            slot_tokens(0)
            turn_rows(0, 1)
            with pe.If(first_n > HALF):
                turn_rows(1, 1)
            with pe.Else():
                pe.sem_inc(xt2_done[1], 1)
            pe.wait_ge(table_ok, 1)
            pairs = pe.value_load(n_pairs, min_val=NE // 2, max_val=NE // 2 * LEVELS)
            def visits(p):
                for u in range(2):
                    n = pe.value_load(countJ[:, col_of(p, u)], min_val=0, max_val=SEQ)
                    then = pe.value_load(countJ[:, col_of(p, u + 1)], min_val=0, max_val=SEQ)

                    def gate_up(s):
                        slots = slice(HALF * s, HALF * s + HALF)
                        for k in range(KC):
                            nc.tensor.matmul(PS[0:HALF, s, :], xgT(u)[:, k, slots], gate_w(u)[:, k, :],
                                             start=(k == 0), stop=(k == KC - 1))
                            last = nc.tensor.matmul(PS[HALF:P, s, :], xgT(u)[:, k, slots], up_w(u)[:, k, :],
                                                    start=(k == 0), stop=(k == KC - 1))
                        last.then_inc(gu_done[s], 1)

                    def down(s):
                        slots = slice(HALF * s, HALF * s + HALF)
                        for k in range(FC):
                            nc.tensor.matmul(PS[0:HALF, 5 + s, :], hidT(u)[:, k, slots], down_w(u)[:, k, 0:512],
                                             start=(k == 0), stop=(k == FC - 1))
                            last = nc.tensor.matmul(PS[HALF:P, 5 + s, :], hidT(u)[:, k, slots], down_w(u)[:, k, 512:1024],
                                                    start=(k == 0), stop=(k == FC - 1))
                        last.then_inc(down_done[s], 1)

                    pe.wait_ge(gate_in[u], p * 16 + 16)
                    pe.wait_ge(up_in[u], p * 16 + 16)
                    for s in range(2):
                        pe.wait_ge(xgt_ok[s], p * 2 + (u + 1))
                    gate_up(0)
                    with pe.If(n > HALF):
                        gate_up(1)
                    with pe.Else():
                        pe.sem_inc(gu_done[1], 1)
                    pe.wait_ge(pick_ok, p * 2 + (u + 2))
                    gather(1 - u, 0)
                    with pe.If(then > HALF):
                        gather(1 - u, 1)
                    with pe.Else():
                        pe.sem_inc(rows_done[1], 1)
                    pe.wait_ge(idx_ok, p * 2 + (u + 1))
                    slot_tokens(1 - u)
                    pe.wait_ge(hid_ok[0], p * 2 + (u + 1))
                    pe.wait_ge(hid_ok[1], p * 2 + (u + 1))
                    for c in range(FC):
                        last = nc.tensor.transpose(PS[:, 4, P * c:P * c + P], hid[:, P * c:P * c + P], ident[:, :])
                    last.then_inc(ht_done, 1)
                    turn_rows(0, p * 2 + (u + 2))
                    with pe.If(then > HALF):
                        turn_rows(1, p * 2 + (u + 2))
                    with pe.Else():
                        pe.sem_inc(xt2_done[1], 1)
                    pe.wait_ge(down_in[u], p * 16 + 16)
                    pe.wait_ge(hidt_ok, p * 2 + (u + 1))
                    for s in range(2):
                        if u or not first_pair(p):
                            pe.wait_ge(ya_ok[s], p * 2 + u)
                            pe.wait_ge(yd_ok[s], p * 2 + u)
                    down(0)
                    with pe.If(n > HALF):
                        down(1)
                    with pe.Else():
                        pe.sem_inc(down_done[1], 1)

            visits(0)
            with pe.Fori(1, pairs) as p:
                visits(p)


def shape_tables():
    import numpy as np

    rel = np.arange(1024) - 512
    n = np.abs(rel)
    large = 8 + (np.log(np.maximum(n, 1) / 8) / np.log(1024 / 8) * 8).astype(np.int32)
    bucket = (rel > 0) * 16 + np.where(n < 8, n, np.minimum(large, 15))
    onehot = (np.arange(32)[:, None] == bucket[None]).astype(np.float32)
    reach_b = (n <= 64) * 1 + ((n <= 256) & (rel % 4 == 0)) + (rel % 16 == 0)
    a = np.where(n <= 128, 0.0, BIG)
    b = np.where(reach_b > 0, -np.log(np.maximum(reach_b, 1)), BIG)
    mask = np.concatenate([np.tile(a, (8, 1)), np.tile(b, (8, 1))]).astype(np.float32)
    return onehot, mask


_INS = ["x", "mem", "ln_in_g", "ln_in_b", "w_in", "rel_bias", "sink_a", "norm_a_g", "norm_b_g", "w_out", "ln1_g",
        "ln1_b", "xq", "xkv", "xo", "ln2_g", "ln2_b", "w_group", "b_group", "w_router", "b_router", "w_gate", "w_up",
        "w_down", "ln3_g", "ln3_b"]


def kernel(**inputs):
    import numpy as np
    import concourse.bacc as bacc
    from concourse.bass_utils import run_bass_kernel_spmd

    nc = bacc.Bacc("TRN2", target_bir_lowering=False, num_devices=1)
    arrays = {f"in_{name}": np.ascontiguousarray(inputs[name]) for name in _INS}
    arrays["in_bucket_onehot"], arrays["in_band_mask"] = shape_tables()
    args = [nc.dram_tensor(n, a.shape, mybir.dt.from_np(a.dtype), kind="ExternalInput").ap() for n, a in arrays.items()]
    out = nc.dram_tensor("out_dram", (1, SEQ, D), F32, kind="ExternalOutput").ap()
    build(nc, *args, out)
    result = run_bass_kernel_spmd(nc, [arrays], core_ids=[0])
    return result.results[0]["out_dram"]
```

```python
from contextlib import ExitStack

import concourse.bass as bass
from concourse import mybir

F32 = mybir.dt.float32
F32R = mybir.dt.float32r
BF16 = mybir.dt.bfloat16
I32 = mybir.dt.int32
U32 = mybir.dt.uint32
ALU = mybir.AluOpType
ACT = mybir.ActivationFunctionType
AX = mybir.AxisListType.X

P = 128
D = 1024
KC = D // P
SEQ = 512
NT = SEQ // P
MEM = 256
MT = MEM // P
HD = 64
XH, XD = 4, 256
NG, EG = 4, 8
NE = NG * EG
FE = 512
FC = FE // P
NR = NG + NE
ALPHA = 2.0 ** 0.25
EPS = 1e-5
BIG = 1e30
HALF = 64
UNIT = 4096
LEVELS = SEQ // P
COLS = (LEVELS + 1) * NE
OOB = 4096
TZW = 896
TZ0 = 384

PLAN = [("memT", 4, "BB", None), ("xk", 8, "AD", None), ("bias", 2, "DD", None), ("xv", 2, "AD", None),
        ("hT", 4, "BB", None), ("xv", 1, "A", None), ("hT", 4, "BB", None), ("xv", 1, "D", None), ("qa", 4, "AD", None), ("ka", 1, "A", None), ("va", 1, "D", None), ("qb", 4, "AD", None),
        ("kb", 4, "AD", None), ("vb", 4, "AD", None), ("yT", 4, "BB", (4, 5, 4, 5)), ("yT", 4, "BB", (6, 7, 4, 5)),
        ("mix", 7, "DD", None), ("h1T", 4, "BB", (4, 5, 6, 7)), ("mix", 1, "DD", None), ("h1T", 4, "BB", (4, 5, 6, 7)),
        ("xq", 4, "AD", None), ("xq", 4, "AD", (4, 5, 6, 7)), ("xo", 7, "DD", None), ("h2T", 4, "AD", (5, 6, 7, 5)),
        ("xo", 1, "DD", None), ("h2T", 4, "AD", None)]
JOBS, EVAC, BANK, _ring = {}, "", [], 0
for _name, _n, _engines, _banks in PLAN:
    for _i in range(_n):
        JOBS.setdefault(_name, []).append(len(EVAC))
        EVAC += _engines[_i % 2]
        BANK.append(_banks[_i] if _banks else _ring % 4)
        _ring += not _banks


def job_of(name, i):
    return JOBS[name][i]


def evacs(engine, job):
    return sum(letter in (engine, "B") for letter in EVAC[:job + 1])


SLABS = ["xk0", "xk1", "xv0", "xv1", "qa", "kava", "qb", "kb", "vb", "wo0", "wo1", "xq0", "xq1", "xo0", "xo1"]
LAST = dict(xk0=job_of("xk", 3), xk1=job_of("xk", 7), xv0=job_of("xv", 1), xv1=job_of("xv", 3), qa=job_of("qa", 3),
            kava=job_of("va", 0), qb=job_of("qb", 3), kb=job_of("kb", 3), vb=job_of("vb", 3), wo0=job_of("mix", 3),
            wo1=job_of("mix", 7), xq0=job_of("xq", 3), xq1=job_of("xq", 7), xo0=job_of("xo", 3), xo1=job_of("xo", 7))
STAGES = 3
PIECES = 4
POOL_SLABS = ["xv1", "xq0", "xo1"]

PAIRS = [("A", j) for j in range(4)] + [("B", j) for j in range(4)]


def head_of(pair, hb):
    group, j = PAIRS[pair]
    return 2 * j + hb + (8 if group == "B" else 0)


def keys_of(pair, tile):
    if PAIRS[pair][0] == "B":
        return list(range(NT))
    return [k for k in (tile - 1, tile, tile + 1) if 0 <= k < NT]


def build(nc, x, mem, ln_in_g, ln_in_b, w_in, rel_bias, sink_a, norm_a_g, norm_b_g, w_out, ln1_g, ln1_b,
          xq, xkv, xo, ln2_g, ln2_b, w_group, b_group, w_router, b_router, w_gate, w_up, w_down,
          ln3_g, ln3_b, bucket_onehot, band_mask, out):
    y_dram = nc.dram_tensor("y_dram", (2 * SEQ, D), F32, kind="Internal").ap()
    bias_dram = nc.dram_tensor("bias_dram", (16, 1024), F32, kind="Internal").ap()

    wk = lambda w, a, b: w[0, :, a:b].rearrange("(k p) n -> p k n", p=P)
    slab_src = {"xk0": wk(xkv, 0, 512), "xk1": wk(xkv, 512, 1024), "xv0": wk(xkv, 1024, 1536),
                "xv1": wk(xkv, 1536, 2048), "qa": wk(w_in, 0, 512), "kava": wk(w_in, 512, 768),
                "qb": wk(w_in, 768, 1280), "kb": wk(w_in, 1280, 1792), "vb": wk(w_in, 1792, 2304),
                "wo0": wk(w_out, 0, 512), "wo1": wk(w_out, 512, 1024), "xq0": wk(xq, 0, 512),
                "xq1": wk(xq, 512, 1024), "xo0": wk(xo, 0, 512), "xo1": wk(xo, 512, 1024)}
    gate_src = w_gate.rearrange("a g e (k p) n -> (a g e) p k n", p=P)
    up_src = w_up.rearrange("a g e (k p) n -> (a g e) p k n", p=P)
    down_src = w_down.rearrange("a g e (k p) n -> (a g e) p k n", p=P)

    with ExitStack() as ctx:
        def sb(name, shape, dt=F32):
            return ctx.enter_context(nc.sbuf_tensor(name, shape, dt))

        def sem(name):
            return ctx.enter_context(nc.semaphore(name))

        PS = ctx.enter_context(nc.psum_tensor("PS", [P, 8, 512], F32))

        arena = -(-nc.sbuf_base // 32) * 32
        units = sb("units", [P, 6 * UNIT])
        R2 = sb("R2", [P, 4096])
        Q = sb("Q", [P, 9216])

        def parts(name, start, floats):
            return nc.alloc_sbuf_tensor_at(name, [P, floats], F32R, offset=arena + 4 * start, align_bytes=32)

        unit = lambda u: units[:, u * UNIT:(u + 1) * UNIT]
        slab = lambda s: unit(SLABS.index(s) % STAGES).rearrange("p (k n) -> p k n", k=KC)
        w_lo = parts("w_lo", 0, STAGES * UNIT)
        w_hi = parts("w_hi", STAGES * UNIT, 2 * UNIT)
        slab_lo = lambda i: w_lo[:, (i % STAGES) * UNIT:(i % STAGES + 1) * UNIT].rearrange("p (k n) -> p k n", k=KC)
        slab_hi = lambda i: w_hi[:, (i % 2) * UNIT:(i % 2 + 1) * UNIT].rearrange("p (k n) -> p k n", k=KC)
        aT_lo = parts("aT_lo", 5 * UNIT, UNIT)[:, :].rearrange("p (k s) -> p k s", k=KC)
        toep_b = lambda s: units[:, 5 * UNIT + s * TZW:5 * UNIT + (s + 1) * TZW]
        pairT = units[:, 5 * UNIT + 4 * TZW:6 * UNIT]

        H = sb("H", [P, NT, D])
        aT_hi = parts("aT_hi", 6 * UNIT, 4096)[:, :].rearrange("p (k s) -> p k s", k=KC)
        h2T = R2[:, :].rearrange("p (k s) -> p k s", k=KC)
        Y = R2[:, :].rearrange("p (t f) -> p t f", t=NT)
        comb = units[:, 0:8 * D].rearrange("p (t r f) -> p t r f", t=NT, r=2)

        in_q = lambda name, start, floats: parts(name, 6 * UNIT + 4096 + start, floats)[:, :].rearrange("p (k s) -> p k s", k=KC)
        memR = Q[:, 0:2048].rearrange("p (t f) -> p t f", t=MT)
        memT_hi = in_q("memT_hi", 2048, 2048)
        memT_lo = in_q("memT_lo", 4096, 2048)
        qaT = Q[:, 0:2048].rearrange("p (j s) -> p j s", j=4)
        va = Q[:, 2560:3072].rearrange("p (t f) -> p t f", t=NT)
        qbT = Q[:, 3072:5120].rearrange("p (j s) -> p j s", j=4)
        kbT = Q[:, 5120:7168].rearrange("p (j s) -> p j s", j=4)
        qkb = Q[:, 3072:7168].rearrange("p (j s) -> p j s", j=8)
        qkb_hi = slab_hi(0)
        qkb_lo = parts("qkb_lo", 6 * UNIT + 4096 + 3072, 4096)[:, :].rearrange("p (j s) -> p j s", j=8)
        vb = Q[:, 7168:9216].rearrange("p (t f) -> p t f", t=NT)
        yT_hi = in_q("yT_hi", 0, 4096)
        yT_lo = in_q("yT_lo", 4096, 4096)
        xqT = Q[:, 4096:8192].rearrange("p (k s) -> p k s", k=KC)

        XKV = sb("XKV", [P, 4096])
        xkT = XKV[:, 0:2048].rearrange("p (k s) -> p k s", k=KC)
        xv = XKV[:, 2048:4096].rearrange("p (t f) -> p t f", t=MT)
        lnG = sb("lnG", [P, D])
        kaT = lambda g: Q[:, 2048:2560] if g == 0 else lnG[:, 0:512]
        lnB = sb("lnB", [P, D])
        XW = sb("XW", [P, 3072])
        toep_a = lambda s: XW[:, s * 3 * P:(s + 1) * 3 * P]

        def prob(n):
            return units[:, 2 * UNIT + 384 * (n % 6):2 * UNIT + 384 * (n % 6 + 1)] if n < 32 else XW[:, 512 * (n % 6):512 * (n % 6 + 1)]

        def probT(n):
            start = 2 * UNIT + (2304 + 448 * (n % 4) if n < 32 else 2048 + 512 * (n % 4))
            return units[:, start:start + (384 if n < 32 else 512)]

        onehot = XW[0:32, 0:1024]
        maskrow = XW[0:16, 1024:2048]
        biasrow = XW[0:16, 2048:3072]
        xprob = lambda h: (XW[:, 0:1024] if h % 2 == 0 else lnG[:, :]).rearrange("p (t m) -> p t m", t=NT)
        xprobT = XW[:, 1024:3072].rearrange("p (b m s) -> p b m s", b=2, m=MT)

        ident = sb("ident", [P, P])
        relb = sb("relb", [32, 16])
        nsink = sb("nsink", [P, 8])
        gains = sb("gains", [P, KC])
        stats = sb("stats", [P, NT, 2, 6])
        meanvar = sb("meanvar", [P, NT, 2])
        rstd = sb("rstd", [P, NT])
        half_neg = sb("half_neg", [P, 8])
        nmax = sb("nmax", [P, 64])
        rsum = sb("rsum", [P, 64])
        rinv = sb("rinv", [P, 64])
        sinkx = sb("sinkx", [P, 2, 8])
        ssq = sb("ssq", [P, 8])
        rms = sb("rms", [P, 8])
        xnmax = sb("xnmax", [P, 16])
        xrsum = sb("xrsum", [P, 16])
        xrinv = sb("xrinv", [P, 16])

        h2_part = lambda i: (XKV[:, 2048 * i:2048 * i + 2048] if i < 2 else Q[:, 7168:9216]).bitcast(BF16).rearrange(
            "p (t f) -> p t f", t=NT)
        rest = Q[:, 6144:7168]
        xg = lambda s: lnG[:, 0:512] if s else Q[:, 6656:7168]
        silu = lnB[:, :].rearrange("p (b f) -> p b f", b=2)
        yrow = lambda u: Q[:, 4608 + 1024 * u:5632 + 1024 * u]
        xgT = lambda u: Q[:, 1024 * u:1024 + 1024 * u].rearrange("p (k s) -> p k s", k=KC)
        hid = Q[:, 2048:2560]
        hidT = lambda u: Q[:, 2560 + 512 * u:3072 + 512 * u].rearrange("p (k s) -> p k s", k=FC)
        in_bf16 = lambda start: Q[:, start:start + 256].bitcast(BF16).rearrange("p (t s) -> p t s", t=NT)
        pick = lambda u: in_bf16(3584 + 256 * u)
        ranked = lambda u: in_bf16(4096 + 256 * u)
        gate_w = lambda u: unit(3 * u).rearrange("p (k n) -> p k n", k=KC)
        gate_w2 = R2[:, :].rearrange("p (k n) -> p k n", k=KC)
        up_w = lambda u: unit(3 * u + 1).rearrange("p (k n) -> p k n", k=KC)
        down_w = lambda u: unit(3 * u + 2).rearrange("p (k n) -> p k n", k=FC)
        posJ = XW[:, 0:NT * COLS].rearrange("p (t c) -> p t c", t=NT)
        rankJ = XW[:, 640:640 + NT * COLS].rearrange("p (t c) -> p t c", t=NT)
        lg = XW[:, 1280:1424].rearrange("p (t c) -> p t c", t=NT)
        gsel = XW[:, 1424:1440].rearrange("p (t c) -> p t c", t=NT)
        gexp = XW[:, 1440:1456].rearrange("p (t c) -> p t c", t=NT)
        es = XW[:, 1456:1584].rearrange("p (t c) -> p t c", t=NT)
        tmp = XW[:, 1584:1712].rearrange("p (t c) -> p t c", t=NT)
        first = XW[:, 1712:1840].rearrange("p (t c) -> p t c", t=NT)
        second = XW[:, 1840:1968].rearrange("p (t c) -> p t c", t=NT)
        small = XW[:, 1968:2016].rearrange("p (n t) -> p n t", t=NT)
        countJ = XW[0:1, 2048:2048 + COLS].bitcast(I32)
        n_pairs = XW[0:1, 2210:2211].bitcast(I32)
        lev = XW[0:1, 2212:2216]
        chosen = XW[:, 2240:2304].bitcast(BF16).rearrange("p (t c) -> p t c", t=NT)
        gatew = sb("gatew", [P, NT, 2])
        router_w = sb("router_w", [P, KC, NR])
        router_b = sb("router_b", [P, NR])
        iota_e = sb("iota_e", [P, NE])
        iota_s = sb("iota_s", [P, P], BF16)
        before = sb("before", [P, P], BF16)
        ones = sb("ones", [P, P], BF16)
        numbers = sb("numbers", [P, NT, 3], BF16)
        idxf = sb("idxf", [P, 5])
        sidx = sb("sidx", [P, 2], U32)
        sidx_next = sb("sidx_next", [P, 2])

        small_in, gain_in, table_in = map(sem, ["small_in", "gain_in", "table_in"])
        mem_in = [sem(f"mem_in{t}") for t in range(MT)]
        x_in = [sem(f"x_in{t}") for t in range(NT)]
        lng_in = [sem(f"lng_in{i}") for i in range(4)]
        slab_in = [sem(f"slab_in{i}") for i in range(STAGES)]
        first_in = [sem(f"first_in{c}") for c in range(PIECES)]
        hi_ok, lo_dve, lo_pool = map(sem, ["hi_ok", "lo_dve", "lo_pool"])
        ident_ok = sem("ident_ok")
        consts_ok = sem("consts_ok")
        job_done = sem("job_done")
        evac_act = sem("evac_act")
        evac_dve = sem("evac_dve")
        bias_out = sem("bias_out")
        toep_a_in = sem("toep_a_in")
        toep_b_in = [sem(f"toep_b_in{i}") for i in range(4)]
        var_ok, rstd_ok, h_ok = map(sem, ["var_ok", "rstd_ok", "h_ok"])
        s_done, l_done, e_done, t_done, pv_done = map(sem, ["s_done", "l_done", "e_done", "t_done", "pv_done"])
        qk_hi_ok, qk_lo_ok = map(sem, ["qk_hi_ok", "qk_lo_ok"])
        pt_act, pt_dve = map(sem, ["pt_act", "pt_dve"])
        pair_ok, pair_turned = map(sem, ["pair_ok", "pair_turned"])
        sinkd_ok, sinke_ok, y_ok = map(sem, ["sinkd_ok", "sinke_ok", "y_ok"])
        ssq_ok, rms_ok, yn_ok = map(sem, ["ssq_ok", "rms_ok", "yn_ok"])
        xs_done, xm_done, xe_done, xp_done, xt_done = map(sem, ["xs_done", "xm_done", "xe_done", "xp_done", "xt_done"])
        xpt_act, xpt_dve, xpv_done, xo_act, xo_dve = map(sem, ["xpt_act", "xpt_dve", "xpv_done", "xo_act", "xo_dve"])
        dve_chain, pool_chain, act_chain = map(sem, ["dve_chain", "pool_chain", "act_chain"])
        out_done = sem("out_done")
        router_in = sem("router_in")
        gate_in = [sem(f"gate_in{u}") for u in range(2)]
        gate_w2_in = sem("gate_w2_in")
        up_in = [sem(f"up_in{u}") for u in range(2)]
        down_in = [sem(f"down_in{u}") for u in range(2)]
        part_ok, rest_ok = map(sem, ["part_ok", "rest_ok"])
        parts_act = sem("parts_act")
        logits_done, gexp_in, gexp_ok, chosen_ok, pos_done, table_ok = map(
            sem, ["logits_done", "gexp_in", "gexp_ok", "chosen_ok", "pos_done", "table_ok"])
        pick_ok, ranked_ok, idxmm_done, idx_ok, sidx_ok = map(sem, ["pick_ok", "ranked_ok", "idxmm_done", "idx_ok", "sidx_ok"])
        row_out = [sem(f"row_out{u}") for u in range(2)]
        ht_done, hidt_ok = map(sem, ["ht_done", "hidt_ok"])
        gu_done, silu_ok, hid_ok, down_done, ya_ok, yd_ok, rows_done, rows_ok, xt2_done, xgt_ok = (
            [sem(f"{name}{s}") for s in range(2)]
            for name in ("gu_done", "silu_ok", "hid_ok", "down_done", "ya_ok", "yd_ok", "rows_done", "rows_ok",
                         "xt2_done", "xgt_ok"))
        dve_loop, alpha_ok, comb_ok, comb_used, pool_turn, gatew_ok, weighed_ok = map(
            sem, ["dve_loop", "alpha_ok", "comb_ok", "comb_used", "pool_turn", "gatew_ok", "weighed_ok"])
        gain_ok, scaled_ok, shift_ok = map(sem, ["gain_ok", "scaled_ok", "shift_ok"])
        comb_in = [[sem(f"comb_in{r}_{t}") for t in range(NT)] for r in range(2)]

        block = ctx.enter_context(nc.Block())

        def waits_evac(eng, job):
            eng.wait_ge(evac_act, evacs("A", job))
            eng.wait_ge(evac_dve, evacs("D", job))

        def first_pair(p):
            return isinstance(p, int) and p == 0

        def from_halves(s):
            return PS[:, 2 + s, :].rearrange("p (c b s) -> p c b s", c=4, b=2)

        def col_of(p, u):
            return slice(2 * p + u, 2 * p + u + 1) if isinstance(p, int) else bass.ds(p * 2 + u, 1)

        def flipped(ap):
            return ap.rearrange("p (t s) -> p t s", s=P)[:, :, ::-1]

        def tiles(ap):
            return ap.rearrange("p (t s) -> p t s", s=P)

        def piece(ap, s, c):
            n = KC // PIECES
            return ap[:, n * c:n * c + n, 0:256 if s == "kava" else 512]

        def landings(s):
            i = SLABS.index(s)
            return 16 * (i // STAGES + (i % STAGES > 0))

        def lo_written(eng, name, pieces=PIECES):
            mine = [x for x in SLABS if (x in POOL_SLABS) == (name in POOL_SLABS)]
            eng.wait_ge(lo_pool if name in POOL_SLABS else lo_dve, PIECES * mine.index(name) + pieces)

        def half_tile(ap, i, backwards=False):
            t, half = (i % 4, i // 4) if backwards else (i // 2, i % 2)
            ap = ap[:, 4 * half:4 * half + 4, P * t:P * t + P]
            return ap[:, :, ::-1] if backwards else ap

        @block.sync
        def _(sp):
            for t in range(MT):
                sp.dma_start(memR[:, t, :], mem[0, P * t:P * t + P, :]).then_inc(mem_in[t], 16)

            def load_slab(s):
                i = SLABS.index(s)
                if i >= STAGES:
                    sp.wait_ge(job_done, LAST[SLABS[i - STAGES]] + 1)
                if s == "xq0":
                    sp.wait_ge(pv_done, 32)
                if s == "kava":
                    sp.dma_start(slab(s)[:, :, 0:256], slab_src[s]).then_inc(slab_in[i % STAGES], 16)
                elif i == 0:
                    for c in range(PIECES):
                        sp.dma_start(piece(slab(s), s, c), piece(slab_src[s], s, c)).then_inc(first_in[c], 16)
                else:
                    sp.dma_start(slab(s), slab_src[s]).then_inc(slab_in[i % STAGES], 16)

            load_slab("xk0")
            load_slab("xk1")
            for t in range(NT):
                sp.dma_start(H[:, t, :], x[0, P * t:P * t + P, :]).then_inc(x_in[t], 16)
            sp.dma_start(lnG[:, :], ln_in_g.rearrange("(a f) -> a f", a=1).partition_broadcast(P)).then_inc(lng_in[0], 16)
            sp.dma_start(lnB[:, :], ln_in_b.rearrange("(a f) -> a f", a=1).partition_broadcast(P)).then_inc(lng_in[0], 16)
            load_slab("xv0")
            load_slab("xv1")
            load_slab("qa")
            sp.wait_ge(evac_dve, evacs("D", job_of("bias", 1)))
            sp.dma_start(bias_dram, biasrow).then_inc(bias_out, 16)
            sp.wait_ge(bias_out, 16)
            sp.dma_start(XW[:, :].rearrange("p (h w) -> p h w", h=8),
                         bass.AP(bias_dram.tensor, 1 + TZ0 - P, [[1, P], [1024, 8], [1, 3 * P]])).then_inc(toep_a_in, 16)
            sp.dma_start(nsink[:, :], sink_a.partition_broadcast(P)).then_inc(small_in, 16)
            for s in SLABS[5:11]:
                load_slab(s)
                if s == "kava":
                    for g, gain in enumerate((norm_a_g, norm_b_g)):
                        sp.dma_start(gains[:, 4 * g:4 * g + 4], gain[0].rearrange("(k p) -> p k", p=P),
                                     allow_slow_non_contiguous=True).then_inc(gain_in, 16)
            sp.wait_ge(job_done, job_of("vb", 3) + 1)
            for q in range(8):
                if q >= 4:
                    sp.wait_ge(l_done, 8 * (4 + q // 2 - 1))
                src = bass.AP(bias_dram.tensor, (8 + q) * 1024 + 1, [[1, P], [1, TZW]])
                sp.dma_start(toep_b(q % 4), src).then_inc(toep_b_in[q % 4], 16)
            for s in SLABS[11:15]:
                load_slab(s)
            sp.wait_ge(job_done, LAST["xq1"] + 1)
            sp.dma_start(gate_w(0), gate_src[0]).then_inc(gate_in[0], 16)
            sp.wait_ge(job_done, LAST["xo0"] + 1)
            sp.dma_start(up_w(0), up_src[0]).then_inc(up_in[0], 16)
            sp.dma_start(up_w(1), up_src[1]).then_inc(up_in[1], 16)
            sp.wait_ge(job_done, LAST["xo1"] + 1)
            sp.dma_start(down_w(0), down_src[0]).then_inc(down_in[0], 16)
            sp.dma_start(gate_w(1), gate_src[1]).then_inc(gate_in[1], 16)
            sp.dma_start(down_w(1), down_src[1]).then_inc(down_in[1], 16)

            sp.wait_ge(logits_done, NT)
            sp.dma_start(gate_w2, gate_src[2]).then_inc(gate_w2_in, 16)

            def load_pair(pair, expert):
                for u in range(2):
                    for s in range(2):
                        sp.wait_ge(gu_done[s], pair * 2 + (u - 1))
                    if not (isinstance(pair, int) and (pair, u) == (1, 0)):
                        sp.dma_start(gate_w(u), gate_src[bass.ds(expert + u, 1)].rearrange("a p k n -> p (a k) n")).then_inc(gate_in[u], 16)
                    sp.dma_start(up_w(u), up_src[bass.ds(expert + u, 1)].rearrange("a p k n -> p (a k) n")).then_inc(up_in[u], 16)
                    for s in range(2):
                        sp.wait_ge(down_done[s], pair * 2 + (u - 1))
                    sp.dma_start(down_w(u), down_src[bass.ds(expert + u, 1)].rearrange("a p k n -> p (a k) n")).then_inc(down_in[u], 16)

            load_pair(1, 2)
            with sp.Fori(2, NE // 2) as p:
                load_pair(p, p * 2)
            sp.wait_ge(table_ok, 1)
            pairs = sp.value_load(n_pairs, min_val=NE // 2, max_val=NE // 2 * LEVELS)
            with sp.If(pairs > NE // 2):
                with sp.Fori(NE // 2, pairs, NE // 2) as base:
                    with sp.Fori(0, NE // 2) as p:
                        load_pair(base + p, p * 2)
            for u in range(2):
                sp.wait_ge(row_out[u], pairs * 16)
            y_src = y_dram.rearrange("(r t p) f -> t p r f", r=2, p=P)
            for t in range(NT):
                for r in range(2):
                    sp.dma_start(comb[:, t, r], y_src[t, :, r]).then_inc(comb_in[r][t], 16)
                if t == 0:
                    sp.dma_start(lnG[:, :], ln3_g.partition_broadcast(P)).then_inc(lng_in[3], 16)
                    sp.dma_start(lnB[:, :], ln3_b.partition_broadcast(P)).then_inc(lng_in[3], 16)
            for t in range(NT):
                if t < 2:
                    sp.wait_ge(shift_ok, t + 1)
                else:
                    sp.wait_ge(h_ok, 3 * NT + t - 1)
                sp.dma_start(out[0, P * t:P * t + P, :], H[:, t, :]).then_inc(out_done, 16)
            sp.wait_ge(out_done, 16 * NT)

        @block.gpsimd
        def _(pool):
            chain = [0]

            def link(ins):
                chain[0] += 1
                ins.then_inc(pool_chain, 1)
                pool.wait_ge(pool_chain, chain[0])

            link(nc.gpsimd.memset(ident[:, :], 0.0))
            nc.gpsimd.affine_select(out=ident[:, :], in_=ident[:, :], compare_op=ALU.not_equal, fill=1.0, base=0,
                                    pattern=[[-1, P]], channel_multiplier=1).then_inc(ident_ok, 1)
            nc.gpsimd.memset(half_neg[:, :], -0.5)
            nc.gpsimd.iota(iota_e[:, :], [[1, NE]], base=0, channel_multiplier=0, allow_small_or_imprecise_dtypes=True)
            nc.gpsimd.iota(iota_s[:, :], [[1, P]], base=0, channel_multiplier=0, allow_small_or_imprecise_dtypes=True)
            nc.gpsimd.memset(numbers[:, :, 0:1], 1.0)
            nc.gpsimd.iota(numbers[:, :, 1:2], [[0, NT]], base=0, channel_multiplier=1, allow_small_or_imprecise_dtypes=True)
            nc.gpsimd.iota(numbers[:, :, 2:3], [[1, NT]], base=0, channel_multiplier=0, allow_small_or_imprecise_dtypes=True)
            link(nc.gpsimd.memset(ones[:, :], 1.0))
            nc.gpsimd.affine_select(out=before[:, :], in_=ones[:, :], compare_op=ALU.is_gt, fill=0.0, base=0,
                                    pattern=[[1, P]], channel_multiplier=-1).then_inc(consts_ok, 1)
            pool.wait_ge(consts_ok, 1)

            def layer_rstd(n):
                t = n % NT
                pool.wait_ge(var_ok, n + 1)
                link(nc.gpsimd.tensor_scalar(rstd[:, t:t + 1], meanvar[:, t, 1:2], EPS, None, ALU.add))
                nc.gpsimd.tensor_tensor(rstd[:, t:t + 1], rstd[:, t:t + 1], half_neg[:, 0:1], ALU.pow).then_inc(rstd_ok, 1)

            def split_lo(name, pieces=range(PIECES)):
                i = SLABS.index(name)
                for c in pieces:
                    pool.wait_ge(hi_ok, PIECES * i + c + 1)
                    nc.gpsimd.tensor_tensor(piece(slab_lo(i), name, c), piece(slab(name), name, c),
                                            piece(slab_hi(i), name, c).bitcast(F32), ALU.subtract).then_inc(lo_pool, 1)

            for n in range(NT):
                layer_rstd(n)
            split_lo("xv1")
            for i in range(8):
                j = i // 2 + 4 * (i % 2)
                pool.wait_ge(qk_hi_ok, i + 1)
                nc.gpsimd.tensor_tensor(qkb_lo[:, j, :], qkb[:, j, :], qkb_hi[:, j, :].bitcast(F32),
                                        ALU.subtract).then_inc(qk_lo_ok, 1)
            for g in range(2):
                pool.wait_ge(ssq_ok, NT * (g + 1))
                part = slice(NT * g, NT * g + NT)
                link(nc.gpsimd.tensor_scalar(rms[:, part], ssq[:, part], 1.0 / 512, EPS, ALU.mult, ALU.add))
                nc.gpsimd.tensor_tensor(rms[:, part], rms[:, part], half_neg[:, part], ALU.pow).then_inc(rms_ok, 1)
            def h2_parts(t):
                pool.wait_ge(parts_act, 2 * t + 1)
                nc.gpsimd.tensor_tensor(rest, H[:, t, :], h2_part(0)[:, t, :], ALU.subtract).then_inc(rest_ok, 1)
                pool.wait_ge(rest_ok, t + 1)
                pool.wait_ge(parts_act, 2 * t + 2)
                nc.gpsimd.tensor_tensor(h2_part(2)[:, t, :], rest, h2_part(1)[:, t, :], ALU.subtract).then_inc(part_ok, 1)
                pool.wait_ge(part_ok, t + 1)

            split_lo("xq0", range(0, 2))
            layer_rstd(NT)
            split_lo("xq0", range(2, PIECES))
            for n in range(NT + 1, 2 * NT):
                layer_rstd(n)
            split_lo("xo1")
            for t in range(NT):
                if t >= 2:
                    h2_parts(t - 2)
                layer_rstd(2 * NT + t)
            h2_parts(2)
            h2_parts(3)

            def scatter(u, rows):
                pool.indirect_dma_start(y_dram, bass.IndirectOffsetOnAxis(sidx[0:rows, u:u + 1], 0), yrow(u)[0:rows], None,
                                        bounds_check=2 * SEQ - 1, oob_is_err=False).then_inc(row_out[u], 16)

            pool.wait_ge(table_ok, 1)
            pairs = pool.value_load(n_pairs, min_val=NE // 2, max_val=NE // 2 * LEVELS)
            nc.gpsimd.tensor_scalar(H[:, :, :].rearrange("p t f -> p (t f)"), H[:, :, :].rearrange("p t f -> p (t f)"),
                                    ALPHA, None, ALU.mult).then_inc(alpha_ok, 1)
            def visits(p):
                for u in range(2):
                    now = pool.value_load(countJ[:, col_of(p, u)], min_val=0, max_val=SEQ)
                    pool.wait_ge(sidx_ok, p * 2 + (u + 1))
                    for s in range(2):
                        pool.wait_ge(ya_ok[s], p * 2 + (u + 1))
                        pool.wait_ge(yd_ok[s], p * 2 + (u + 1))
                    pool.sem_inc(pool_turn, 1)
                    with pool.If(now > HALF):
                        scatter(u, P)
                    with pool.Else():
                        scatter(u, HALF)

            visits(0)
            with pool.Fori(1, pairs) as p:
                visits(p)
            pool.sem_inc(pool_turn, 1)

            def first_output(t):
                pool.wait_ge(weighed_ok, t - 1)
                nc.gpsimd.tensor_tensor(H[:, t, :], H[:, t, :], comb[:, t, 0, :], ALU.add).then_inc(comb_ok, 1)

            def shift(t):
                pool.wait_ge(scaled_ok, t + 1)
                nc.gpsimd.tensor_tensor(H[:, t, :], H[:, t, :], lnB[:, :], ALU.add).then_inc(shift_ok, 1)

            pool.wait_ge(alpha_ok, 1)
            pool.wait_ge(lng_in[3], 32)
            layer_rstd(3 * NT)
            shift(0)
            first_output(2)
            layer_rstd(3 * NT + 1)
            first_output(3)
            layer_rstd(3 * NT + 2)
            shift(1)
            layer_rstd(3 * NT + 3)

        @block.scalar
        def _(act):
            act.dma_start(relb[:, :], rel_bias).then_inc(table_in, 16)
            act.dma_start(onehot, bucket_onehot).then_inc(table_in, 16)
            act.dma_start(maskrow, band_mask).then_inc(table_in, 16)

            def load_norm(i, g, b):
                act.wait_ge(h_ok, NT * i)
                act.dma_start(lnG[:, :], g.partition_broadcast(P)).then_inc(lng_in[i], 16)
                act.dma_start(lnB[:, :], b.partition_broadcast(P)).then_inc(lng_in[i], 16)

            def job_copy(job, dst, src, scale=1.0):
                act.wait_ge(job_done, job + 1)
                nc.scalar.activation(dst, src, ACT.Copy, scale=scale).then_inc(evac_act, 1)

            def my_jobs(name):
                return [i for i, job in enumerate(JOBS[name]) if EVAC[job] == "A"]

            def split_hi(name):
                i = SLABS.index(name)
                if i:
                    act.wait_ge(slab_in[i % STAGES], landings(name))
                if i >= 2:
                    act.wait_ge(job_done, LAST[SLABS[i - 2]] + 1)
                for c in range(PIECES):
                    if i == 0:
                        act.wait_ge(first_in[c], 16)
                    if name in ("wo0", "wo1"):
                        for k in range(2 * c, 2 * c + 2):
                            last = nc.scalar.activation(slab_hi(i)[:, k, :], slab(name)[:, k, :], ACT.Copy,
                                                        scale=gains[:, k:k + 1])
                    else:
                        last = nc.scalar.activation(piece(slab_hi(i), name, c), piece(slab(name), name, c), ACT.Copy)
                    last.then_inc(hi_ok, 1)

            def tile_hi(name, i, dst, backwards=False):
                job = job_of(name, i)
                act.wait_ge(job_done, job + 1)
                nc.scalar.activation(half_tile(dst, i, backwards), PS[:, BANK[job], :].rearrange("p (c s) -> p c s", c=4),
                                     ACT.Copy).then_inc(evac_act, 1)

            for i in range(4):
                tile_hi("memT", i, memT_hi)
            split_hi("xk0")
            for i in my_jobs("xk"):
                job_copy(job_of("xk", i), xkT[:, i, :], PS[:, BANK[job_of("xk", i)], 0:MEM])
                if i % 4 == 0:
                    split_hi(("xk1", "xv0")[i // 4])
            split_hi("xv1")
            for i in my_jobs("xv"):
                job_copy(job_of("xv", i), xv[:, i % 2, 512 * (i // 2):512 * (i // 2) + 512], PS[:, BANK[job_of("xv", i)], :])
                for j in range(2 * i, 2 * i + 4):
                    tile_hi("hT", j, aT_hi)
                if i == 0:
                    split_hi("qa")
            for i in my_jobs("qa"):
                job_copy(job_of("qa", i), flipped(qaT[:, i, :]), tiles(PS[:, BANK[job_of("qa", i)], :]), -HD ** -0.5)
                if i == 0:
                    split_hi("kava")
            split_hi("qb")
            act.wait_ge(job_done, job_of("ka", 0) + 1)
            for g in range(2):
                for part in range(2):
                    last = nc.scalar.activation(kaT(g)[HD * part:HD * part + HD, :],
                                                PS[HD * g:HD * g + HD, BANK[job_of("ka", 0)], :], ACT.Copy)
            last.then_inc(evac_act, 1)
            for i in my_jobs("qb"):
                job_copy(job_of("qb", i), flipped(qbT[:, i, :]), tiles(PS[:, BANK[job_of("qb", i)], :]), -HD ** -0.5)
                if i == 0:
                    split_hi("kb")
            for i in my_jobs("kb"):
                job_copy(job_of("kb", i), kbT[:, i, :], PS[:, BANK[job_of("kb", i)], :])
                if i == 0:
                    split_hi("vb")
            act.wait_ge(gain_in, 32)
            for i in my_jobs("vb"):
                job_copy(job_of("vb", i), vb[:, i, :], PS[:, BANK[job_of("vb", i)], :])
                if i == 0:
                    split_hi("wo0")

            def sum_squares(g, t):
                junk = XW[:, 0:512] if g else units[:, 2 * UNIT:2 * UNIT + 512]
                nc.scalar.activation(junk, Y[:, t, 512 * g:512 * g + 512], ACT.Square,
                                     accum_out=ssq[:, NT * g + t:NT * g + t + 1]).then_inc(ssq_ok, 1)
                act.wait_ge(ssq_ok, NT * g + t + 1)

            for m in range(35):
                if m < 32:
                    for n in (2 * m, 2 * m + 1):
                        w = P * len(keys_of(n // 8, (n // 2) % 4))
                        act.wait_ge(l_done, n + 1)
                        nc.scalar.activation(prob(n)[:, 0:w], prob(n)[:, 0:w], ACT.Exp, bias=nmax[:, n:n + 1],
                                             scale=-1.0, accum_out=rsum[:, n:n + 1]).then_inc(e_done, 1)
                if 2 <= m <= 33:
                    n = 2 * (m - 2)
                    w = P * len(keys_of(n // 8, (n // 2) % 4))
                    act.wait_ge(t_done, n + 1)
                    if n >= 4:
                        act.wait_ge(pv_done, n // 2 - 1)
                    nc.scalar.activation(probT(n)[:, 0:w], PS[:, 4 + n % 2, 0:w], ACT.Copy).then_inc(pt_act, 1)
                if m >= 4 and m % 4 == 0 and m // 4 <= 4:
                    pair = m // 4 - 1
                    act.wait_ge(sinkd_ok, pair + 1)
                    nc.scalar.activation(sinkx[:, pair % 2, :], sinkx[:, pair % 2, :], ACT.Exp).then_inc(sinke_ok, 1)
                if 1 <= m <= 8:
                    if m == 1:
                        act.wait_ge(evac_dve, evacs("D", job_of("vb", 3)))
                        act.wait_ge(s_done, 1)
                    j = (m - 1) // 2 + 4 * ((m - 1) % 2)
                    nc.scalar.activation(qkb_hi[:, j, :], qkb[:, j, :], ACT.Copy).then_inc(qk_hi_ok, 1)
                if m % 4 == 2 and m >= 6:
                    pair = m // 4 - 1
                    act.wait_ge(pv_done, 4 * pair + 4)
                    if pair:
                        act.wait_ge(pair_turned, pair)
                    nc.scalar.activation(pairT, PS[:, 6 + pair % 2, :], ACT.Copy).then_inc(pair_ok, 1)
                if m == 20:
                    act.wait_ge(y_ok, 4)
                    load_norm(1, ln1_g, ln1_b)
                    for t in range(NT):
                        sum_squares(0, t)
            for i in range(4):
                tile_hi("yT", i, yT_hi, backwards=True)
            act.wait_ge(y_ok, 8)
            for t in range(NT):
                sum_squares(1, t)
            for i in range(4, 8):
                tile_hi("yT", i, yT_hi, backwards=True)
            split_hi("wo1")
            split_hi("xq0")
            for i in range(8):
                tile_hi("h1T", i, aT_hi)

            def q_copy(i):
                job_copy(job_of("xq", i), xqT[:, i, :], PS[:, BANK[job_of("xq", i)], :], -XD ** -0.5)

            q_copy(0)
            split_hi("xq1")
            q_copy(2)

            def o_copy(h):
                for c in range(2):
                    act.wait_ge(xpv_done, 2 * h + c + 1)
                    nc.scalar.activation(yT_hi[:, 2 * h + c, :], PS[:, 6 + c, :], ACT.Copy).then_inc(xo_act, 1)

            def exps(h):
                for u in (2 * h, 2 * h + 1):
                    act.wait_ge(xm_done, u + 1)
                    if h >= 2:
                        act.wait_ge(xt_done, h - 1)
                    for i in range(2):
                        nc.scalar.activation(xprob(h)[:, 2 * (u % 2) + i, :], PS[:, u % 4, 256 * i:256 * i + 256], ACT.Exp,
                                             bias=xnmax[:, 2 * u + i:2 * u + i + 1], scale=-1.0,
                                             accum_out=xrsum[:, 2 * u + i:2 * u + i + 1]).then_inc(xe_done, 1)

            def turned(h):
                act.wait_ge(xt_done, h + 1)
                if h >= 2:
                    act.wait_ge(xpv_done, 2 * (h - 1))
                nc.scalar.activation(xprobT[:, h % 2, 0, :], PS[:, 4, :], ACT.Copy).then_inc(xpt_act, 1)

            exps(0)
            exps(1)
            q_copy(4)
            q_copy(6)
            split_hi("xo0")
            for h in range(XH):
                turned(h)
                if h >= 1:
                    o_copy(h - 1)
                if h + 2 < XH:
                    exps(h + 2)
            o_copy(XH - 1)
            split_hi("xo1")
            load_norm(2, ln2_g, ln2_b)
            act.dma_start(router_w[:, :, 0:NG], w_group[0].rearrange("(k p) n -> p k n", p=P)).then_inc(router_in, 16)
            act.dma_start(router_w[:, :, NG:NR], w_router[0].rearrange("(k p) n -> p k n", p=P)).then_inc(router_in, 16)
            act.dma_start(router_b[:, 0:NG], b_group.partition_broadcast(P)).then_inc(router_in, 16)
            act.dma_start(router_b[:, NG:NR], b_router.partition_broadcast(P)).then_inc(router_in, 16)
            def h2_parts(t):
                act.wait_ge(h_ok, 2 * NT + t + 1)
                nc.scalar.activation(h2_part(0)[:, t, :], H[:, t, :], ACT.Copy).then_inc(parts_act, 1)
                act.wait_ge(rest_ok, t + 1)
                nc.scalar.activation(h2_part(1)[:, t, :], rest, ACT.Copy).then_inc(parts_act, 1)

            h2_parts(0)
            for i in my_jobs("h2T"):
                if i == 4:
                    h2_parts(1)
                job_copy(job_of("h2T", i), half_tile(h2T, i),
                         PS[:, BANK[job_of("h2T", i)], :].rearrange("p (c s) -> p c s", c=4))
            h2_parts(2)
            h2_parts(3)
            act.wait_ge(gexp_in, 1)
            nc.scalar.activation(gexp, gexp, ACT.Exp).then_inc(gexp_ok, 1)
            act.wait_ge(gexp_in, 2)
            nc.scalar.activation(small[:, 4, :], small[:, 4, :], ACT.Exp).then_inc(gexp_ok, 1)

            act.wait_ge(table_ok, 1)
            pairs = act.value_load(n_pairs, min_val=NE // 2, max_val=NE // 2 * LEVELS)

            def rows_of(s, count):
                act.wait_ge(rows_done[s], count)
                nc.scalar.activation(xg(s), PS[:, 2 + s, :], ACT.Copy).then_inc(rows_ok[s], 1)

            def xgt_of(u, s, count):
                act.wait_ge(xt2_done[s], count)
                dst = xgT(u).rearrange("p (b c) s -> p c b s", b=2)[:, :, :, HALF * s:HALF * s + HALF]
                nc.scalar.activation(dst, from_halves(s), ACT.Copy).then_inc(xgt_ok[s], 1)

            first_n = act.value_load(countJ[:, 0:1], min_val=0, max_val=SEQ)
            rows_of(0, 1)
            xgt_of(0, 0, 1)
            with act.If(first_n > HALF):
                rows_of(1, 1)
                xgt_of(0, 1, 1)
            with act.Else():
                act.sem_inc(rows_ok[1], 1)
                act.sem_inc(xgt_ok[1], 1)

            def visits(p):
                for u in range(2):
                    n = act.value_load(countJ[:, col_of(p, u)], min_val=0, max_val=SEQ)
                    then = act.value_load(countJ[:, col_of(p, u + 1)], min_val=0, max_val=SEQ)

                    def silu_of(s):
                        act.wait_ge(gu_done[s], p * 2 + (u + 1))
                        nc.scalar.activation(silu[HALF:P, s, :], PS[0:HALF, s, :], ACT.Silu).then_inc(silu_ok[s], 1)

                    def y_left(s):
                        act.wait_ge(down_done[s], p * 2 + (u + 1))
                        nc.scalar.activation(yrow(u)[HALF * s:HALF * s + HALF, 0:512], PS[0:HALF, 5 + s, :],
                                             ACT.Copy).then_inc(ya_ok[s], 1)

                    silu_of(0)
                    with act.If(n > HALF):
                        silu_of(1)
                    with act.Else():
                        act.sem_inc(silu_ok[1], 1)
                    rows_of(0, p * 2 + (u + 2))
                    with act.If(then > HALF):
                        rows_of(1, p * 2 + (u + 2))
                    with act.Else():
                        act.sem_inc(rows_ok[1], 1)
                    xgt_of(1 - u, 0, p * 2 + (u + 2))
                    with act.If(then > HALF):
                        xgt_of(1 - u, 1, p * 2 + (u + 2))
                    with act.Else():
                        act.sem_inc(xgt_ok[1], 1)
                    if not first_pair(p):
                        act.wait_ge(row_out[u], p * 16)
                    y_left(0)
                    with act.If(n > HALF):
                        y_left(1)
                    with act.Else():
                        act.sem_inc(ya_ok[1], 1)

            visits(0)
            with act.Fori(1, pairs) as p:
                visits(p)
            act.wait_ge(gatew_ok, 1)
            for t in range(2):
                act.wait_ge(rstd_ok, 3 * NT + t + 1)
                act.wait_ge(gain_ok, t + 1)
                nc.scalar.activation(H[:, t, :], H[:, t, :], ACT.Copy, scale=rstd[:, t:t + 1]).then_inc(scaled_ok, 1)
                act.wait_ge(comb_in[0][t + 2], 16)
                nc.scalar.activation(comb[:, t + 2, 0, :], comb[:, t + 2, 0, :], ACT.Copy,
                                     scale=gatew[:, t + 2, 0:1]).then_inc(weighed_ok, 1)

        @block.vector
        def _(dve):
            chain = [0]

            def link(ins):
                chain[0] += 1
                ins.then_inc(dve_chain, 1)
                dve.wait_ge(dve_chain, chain[0])

            def my_jobs(name):
                return [i for i, job in enumerate(JOBS[name]) if EVAC[job] == "D"]

            def job_copy(job, dst, src, scale=1.0):
                dve.wait_ge(job_done, job + 1)
                if scale == 1.0:
                    nc.vector.tensor_copy(dst, src).then_inc(evac_dve, 1)
                else:
                    nc.vector.tensor_scalar(dst, src, scale, None, ALU.mult).then_inc(evac_dve, 1)

            def norm_stats(n):
                t = n % NT
                if n < NT:
                    dve.wait_ge(x_in[t], 16)
                for c in range(2):
                    last = nc.vector.bn_stats(stats[:, t, c, :], H[:, t, 512 * c:512 * c + 512])
                link(last)
                nc.vector.bn_aggr(meanvar[:, t, :], stats[:, t, :, :].rearrange("p c s -> p (c s)")).then_inc(var_ok, 1)

            def norm_apply(n):
                t = n % NT
                dve.wait_ge(var_ok, n + 1)
                dve.wait_ge(lng_in[n // NT], 32)
                link(nc.vector.scalar_tensor_tensor(H[:, t, :], H[:, t, :], meanvar[:, t, 0:1], lnG[:, :],
                                                    ALU.subtract, ALU.mult))
                dve.wait_ge(rstd_ok, n + 1)
                nc.vector.scalar_tensor_tensor(H[:, t, :], H[:, t, :], rstd[:, t:t + 1], lnB[:, :],
                                               ALU.mult, ALU.add).then_inc(h_ok, 1)

            def split_lo(name):
                i = SLABS.index(name)
                for c in range(PIECES):
                    dve.wait_ge(hi_ok, PIECES * i + c + 1)
                    if name in ("wo0", "wo1"):
                        for k in range(2 * c, 2 * c + 2):
                            last = nc.vector.scalar_tensor_tensor(slab_lo(i)[:, k, :], slab(name)[:, k, :], gains[:, k:k + 1],
                                                                  slab_hi(i)[:, k, :].bitcast(F32), ALU.mult, ALU.subtract)
                    else:
                        last = nc.vector.tensor_tensor(piece(slab_lo(i), name, c), piece(slab(name), name, c),
                                                       piece(slab_hi(i), name, c).bitcast(F32), ALU.subtract)
                    last.then_inc(lo_dve, 1)

            def tile_lo(name, i, hi, lo, backwards=False):
                job = job_of(name, i)
                dve.wait_ge(job_done, job + 1)
                dve.wait_ge(evac_act, evacs("A", job))
                nc.vector.tensor_tensor(half_tile(lo, i, backwards), PS[:, BANK[job], :].rearrange("p (c s) -> p c s", c=4),
                                        half_tile(hi, i, backwards).bitcast(F32), ALU.subtract).then_inc(evac_dve, 1)

            for i in range(4):
                tile_lo("memT", i, memT_hi, memT_lo)
            split_lo("xk0")
            for i in my_jobs("xk"):
                job_copy(job_of("xk", i), xkT[:, i, :], PS[:, BANK[job_of("xk", i)], 0:MEM])
                if i == 1:
                    split_lo("xk1")
                if i == 3:
                    for t in range(NT):
                        norm_stats(t)
                if i == 5:
                    norm_apply(0)
                    split_lo("xv0")
                if i == 7:
                    norm_apply(1)
            dve.wait_ge(table_in, 48)
            for i in range(2):
                job = job_of("bias", i)
                dve.wait_ge(job_done, job + 1)
                nc.vector.scalar_tensor_tensor(biasrow[:, 512 * i:512 * i + 512], PS[0:16, BANK[job], :], -1.0,
                                               maskrow[:, 512 * i:512 * i + 512], ALU.mult, ALU.add).then_inc(evac_dve, 1)
            norm_apply(2)
            norm_apply(3)
            for i in my_jobs("xv"):
                if i == 3:
                    for j in range(4, 8):
                        tile_lo("hT", j, aT_hi, aT_lo)
                job_copy(job_of("xv", i), xv[:, i % 2, 512 * (i // 2):512 * (i // 2) + 512], PS[:, BANK[job_of("xv", i)], :])
                if i == 1:
                    for j in range(4):
                        tile_lo("hT", j, aT_hi, aT_lo)
                    split_lo("qa")
            dve.wait_ge(small_in, 16)
            link(nc.vector.tensor_scalar(nsink[:, :], nsink[:, :], -1.0, None, ALU.mult))
            for i in my_jobs("qa"):
                job_copy(job_of("qa", i), flipped(qaT[:, i, :]), tiles(PS[:, BANK[job_of("qa", i)], :]), -HD ** -0.5)
                if i == 1:
                    split_lo("kava")
            split_lo("qb")
            job_copy(job_of("va", 0), va.rearrange("p t f -> p (t f)"), PS[:, BANK[job_of("va", 0)], :])
            for i in my_jobs("qb"):
                job_copy(job_of("qb", i), flipped(qbT[:, i, :]), tiles(PS[:, BANK[job_of("qb", i)], :]), -HD ** -0.5)
                if i == 1:
                    split_lo("kb")
            for i in my_jobs("kb"):
                job_copy(job_of("kb", i), kbT[:, i, :], PS[:, BANK[job_of("kb", i)], :])
                if i == 1:
                    split_lo("vb")
            for i in my_jobs("vb"):
                job_copy(job_of("vb", i), vb[:, i, :], PS[:, BANK[job_of("vb", i)], :])
                if i == 1:
                    split_lo("wo0")

            def sink_logits(pair):
                sk = nsink[:, 2 * pair:2 * pair + 2].unsqueeze(1).to_broadcast([P, NT, 2])
                dve.wait_ge(l_done, 8 * pair + 8)
                nc.vector.tensor_tensor(sinkx[:, pair % 2, :].rearrange("p (i b) -> p i b", b=2),
                                        nmax[:, 8 * pair:8 * pair + 8].rearrange("p (i b) -> p i b", b=2), sk,
                                        ALU.subtract).then_inc(sinkd_ok, 1)

            def divide(pair):
                group, j = PAIRS[pair]
                part = slice(8 * pair, 8 * pair + 8)
                dve.wait_ge(e_done, 8 * pair + 8)
                if group == "A":
                    dve.wait_ge(sinke_ok, pair + 1)
                    link(nc.vector.tensor_tensor(rsum[:, part], rsum[:, part], sinkx[:, pair % 2, :], ALU.add))
                dst = Y[:, :, P * pair:P * pair + P].rearrange("p t (b d) -> p t b d", b=2)
                link(nc.vector.reciprocal(rinv[:, part], rsum[:, part]))
                dve.wait_ge(pair_turned, pair + 1)
                inv = rinv[:, part].rearrange("p (i b) -> p i b", b=2).unsqueeze(3).to_broadcast([P, NT, 2, HD])
                nc.vector.tensor_tensor(dst, PS[:, 6 + pair % 2, :].rearrange("p (i b d) -> p i b d", b=2, d=HD),
                                        inv, ALU.mult).then_inc(y_ok, 1)

            for m in range(35):
                if m < 32:
                    for n in (2 * m, 2 * m + 1):
                        pair, tile, hb = n // 8, (n // 2) % 4, n % 2
                        keys = keys_of(pair, tile)
                        w = P * len(keys)
                        x0 = TZ0 + P * (keys[0] - tile)
                        q = 2 * pair + hb
                        head = head_of(pair, hb)
                        if pair < 4:
                            dve.wait_ge(toep_a_in, 16)
                            bias = toep_a(head)[:, x0 - (TZ0 - P):x0 - (TZ0 - P) + w]
                        else:
                            dve.wait_ge(toep_b_in[q % 4], 16 * (q // 4 - 1))
                            bias = toep_b(q % 4)[:, x0:x0 + w]
                        dve.wait_ge(s_done, n + 1)
                        if n >= 6:
                            dve.wait_ge(t_done, n - 5)
                        nc.vector.tensor_tensor_reduce(
                            out=prob(n)[:, 0:w], in0=PS[:, n % 4, 0:w], in1=bias, scale=1.0,
                            scalar=nsink[:, head:head + 1] if head < 8 else 3e38, op0=ALU.add, op1=ALU.min,
                            accum_out=nmax[:, n:n + 1]).then_inc(l_done, 1)
                if 2 <= m <= 33:
                    n = 2 * (m - 2) + 1
                    w = P * len(keys_of(n // 8, (n // 2) % 4))
                    dve.wait_ge(t_done, n + 1)
                    if n >= 4:
                        dve.wait_ge(pv_done, n // 2 - 1)
                    nc.vector.tensor_copy(probT(n)[:, 0:w], PS[:, 4 + n % 2, 0:w]).then_inc(pt_dve, 1)
                if m < 16 and m % 4 == 3:
                    sink_logits(m // 4)
                if m >= 7 and m % 4 == 3:
                    divide(m // 4 - 1)
                if m == 23:
                    dve.wait_ge(rms_ok, 1)
                    for t in range(NT):
                        nc.vector.tensor_scalar(Y[:, t, 0:512], Y[:, t, 0:512], rms[:, t:t + 1], None,
                                                ALU.mult).then_inc(yn_ok, 1)
            for i in range(4):
                tile_lo("yT", i, yT_hi, yT_lo, backwards=True)
            divide(7)
            dve.wait_ge(rms_ok, 2)
            for t in range(NT):
                nc.vector.tensor_scalar(Y[:, t, 512:1024], Y[:, t, 512:1024], rms[:, NT + t:NT + t + 1], None,
                                        ALU.mult).then_inc(yn_ok, 1)
            for i in range(4, 8):
                tile_lo("yT", i, yT_hi, yT_lo, backwards=True)
            split_lo("wo1")

            def residual(name, i):
                job, hf, t = job_of(name, i), i // 4, i % 4
                cols = slice(512 * hf, 512 * hf + 512)
                dve.wait_ge(job_done, job + 1)
                nc.vector.scalar_tensor_tensor(H[:, t, cols], H[:, t, cols], ALPHA, PS[:, BANK[job], :], ALU.mult,
                                               ALU.add).then_inc(evac_dve, 1)

            def norm(n):
                norm_stats(n)
                norm_apply(n)

            for i in range(4):
                residual("mix", i)
            for i in range(4, 7):
                residual("mix", i)
                if i < 6:
                    dve.wait_ge(evac_dve, evacs("D", job_of("mix", i)))
                    norm(NT + i - 4)
            for i in range(4):
                tile_lo("h1T", i, aT_hi, aT_lo)
            dve.wait_ge(evac_dve, evacs("D", job_of("mix", 6)))
            norm(NT + 2)
            residual("mix", 7)
            dve.wait_ge(evac_dve, evacs("D", job_of("mix", 7)))
            norm(NT + 3)
            for i in range(4, 8):
                tile_lo("h1T", i, aT_hi, aT_lo)

            def q_copy(i):
                job_copy(job_of("xq", i), xqT[:, i, :], PS[:, BANK[job_of("xq", i)], :], -XD ** -0.5)

            q_copy(1)
            split_lo("xq1")
            q_copy(3)

            def o_copy(h):
                for c in range(2):
                    dve.wait_ge(xo_act, 2 * h + c + 1)
                    nc.vector.tensor_tensor(aT_lo[:, 2 * h + c, :], PS[:, 6 + c, :], yT_hi[:, 2 * h + c, :].bitcast(F32),
                                            ALU.subtract).then_inc(xo_dve, 1)

            def minima(h):
                for u in (2 * h, 2 * h + 1):
                    dve.wait_ge(xs_done, u + 1)
                    nc.vector.tensor_reduce(xnmax[:, 2 * u:2 * u + 2], PS[:, u % 4, :].rearrange("p (i m) -> p i m", i=2),
                                            AX, ALU.min).then_inc(xm_done, 1)

            def divided(h):
                for u in (2 * h, 2 * h + 1):
                    dve.wait_ge(xe_done, 2 * u + 2)
                    link(nc.vector.reciprocal(xrinv[:, 2 * u:2 * u + 2], xrsum[:, 2 * u:2 * u + 2]))
                    for i in range(2):
                        row = xprob(h)[:, 2 * (u % 2) + i, :]
                        nc.vector.tensor_scalar(row, row, xrinv[:, 2 * u + i:2 * u + i + 1], None, ALU.mult).then_inc(xp_done, 1)

            def turned(h):
                dve.wait_ge(xt_done, h + 1)
                if h >= 2:
                    dve.wait_ge(xpv_done, 2 * (h - 1))
                nc.vector.tensor_copy(xprobT[:, h % 2, 1, :], PS[:, 5, :]).then_inc(xpt_dve, 1)

            minima(0)
            minima(1)
            divided(0)
            divided(1)
            q_copy(5)
            q_copy(7)
            split_lo("xo0")
            for h in range(XH):
                if h + 2 < XH:
                    minima(h + 2)
                turned(h)
                if h >= 1:
                    o_copy(h - 1)
                if h + 2 < XH:
                    divided(h + 2)
            o_copy(XH - 1)

            def h2_copy(i):
                if EVAC[job_of("h2T", i)] == "D":
                    job_copy(job_of("h2T", i), half_tile(h2T, i),
                             PS[:, BANK[job_of("h2T", i)], :].rearrange("p (c s) -> p c s", c=4))

            for i in range(8):
                residual("xo", i)
                if i >= 4:
                    dve.wait_ge(evac_dve, evacs("D", job_of("xo", i)))
                    norm(2 * NT + i - 4)
                if i == 6:
                    for j in range(4):
                        h2_copy(j)
            for i in range(4, 8):
                h2_copy(i)

            over = lambda ap, n: ap.unsqueeze(2).to_broadcast([P, NT, n])
            tt, ts, stt = nc.vector.tensor_tensor, nc.vector.tensor_scalar, nc.vector.scalar_tensor_tensor
            reduce = nc.vector.tensor_reduce
            dve.wait_ge(router_in, 64)
            dve.wait_ge(logits_done, NT)
            link(tt(lg, PS[:, 4, 0:NT * NR].rearrange("p (t c) -> p t c", t=NT),
                    router_b[:, :].unsqueeze(1).to_broadcast([P, NT, NR]), ALU.add))
            gl, el = lg[:, :, 0:NG], lg[:, :, NG:NR]

            def first_of(dst, values, n, top, at):
                link(reduce(top, values, AX, ALU.max))
                link(tt(dst, values, over(top, n), ALU.is_equal))
                link(stt(dst, dst, -100.0, iota_e[:, 0:n].unsqueeze(1).to_broadcast([P, NT, n]), ALU.mult, ALU.add))
                link(reduce(at, dst, AX, ALU.min))
                link(tt(dst, dst, over(at, n), ALU.is_equal))

            first_of(gsel, gl, NG, small[:, 0, :], small[:, 1, :])
            tt(gexp, gl, over(small[:, 0, :], NG), ALU.subtract).then_inc(gexp_in, 1)
            link(ts(tmp[:, :, 0:NG], gsel, -1.0, BIG, ALU.add, ALU.mult))
            group = lambda ap: ap.unsqueeze(3).to_broadcast([P, NT, NG, EG])
            by_group = lambda ap: ap.rearrange("p t (g e) -> p t g e", g=NG)
            link(tt(by_group(es), by_group(el), group(tmp[:, :, 0:NG]), ALU.add))
            first_of(first, es, NE, small[:, 2, :], small[:, 1, :])
            link(stt(es, first, -3 * BIG, es, ALU.mult, ALU.add))
            first_of(second, es, NE, small[:, 3, :], small[:, 1, :])
            tt(chosen, first, second, ALU.add).then_inc(chosen_ok, 1)
            dve.wait_ge(chosen_ok, 1)
            tt(small[:, 4, :], small[:, 3, :], small[:, 2, :], ALU.subtract).then_inc(gexp_in, 1)
            link(stt(tmp, second, 2.0, first, ALU.mult, ALU.add))
            dve.wait_ge(pos_done, 1)
            link(stt(es, PS[:, 5, 0:P].rearrange("p (t c) -> p t c", t=NT), 1.0, chosen, ALU.add, ALU.mult))
            link(ts(posJ[:, :, 0:NE], es, -1.0, None, ALU.add))

            def pick_rows(u, col):
                for t in range(NT):
                    last = ts(pick(u)[:, t, :], iota_s[:, :], posJ[:, t, col], None, ALU.is_equal)
                last.then_inc(pick_ok, 1)

            def rank_rows(u, col):
                for t in range(NT):
                    last = ts(ranked(u)[:, t, :], iota_s[:, :], posJ[:, t, col], rankJ[:, t, col], ALU.is_equal, ALU.mult)
                last.then_inc(ranked_ok, 1)

            pick_rows(0, slice(0, 1))
            counts = PS[0:1, 5, P:P + NE]
            for level in range(LEVELS + 1):
                ts(countJ[:, NE * level:NE * level + NE], counts, -1.0 * P * level, 0.0, ALU.add, ALU.max)
            link(reduce(lev[:, 0:1], counts, AX, ALU.max))
            link(ts(lev[:, 1:2], lev[:, 0:1], 1.0 * P, 1.0, ALU.is_gt, ALU.add))
            for level in range(2, LEVELS):
                link(stt(lev[:, 1:2], lev[:, 0:1], 1.0 * P * level, lev[:, 1:2], ALU.is_gt, ALU.add))
            ts(n_pairs, lev[:, 1:2], NE / 2, None, ALU.mult).then_inc(table_ok, 1)
            for level in range(1, LEVELS + 1):
                ts(posJ[:, :, NE * level:NE * level + NE], es, -1.0 - P * level, None, ALU.add)
            link(nc.vector.tensor_copy(rankJ.rearrange("p t (l e) -> p t l e", e=NE),
                                       tmp.unsqueeze(2).to_broadcast([P, NT, LEVELS + 1, NE])))
            rank_rows(0, slice(0, 1))
            pick_rows(1, slice(1, 2))
            rank_rows(1, slice(1, 2))

            def tokens_of_slots(u, wait_for):
                idx = PS[:, 7, 0:3]
                ts(idxf[:, 0:1], idx[:, 0:1], -0.5, 1.5, ALU.mult, ALU.add)
                ts(idxf[:, 2:3], idx[:, 0:1], 0.0, 1.0 * OOB, ALU.is_equal, ALU.mult)
                ts(idxf[:, 3:4], idx[:, 0:1], 1.0 * SEQ, -1.0 * SEQ, ALU.mult, ALU.add)
                wait_for(ts(idxf[:, 1:2], idx[:, 2:3], 1.0 * P, None, ALU.mult))
                wait_for(tt(idxf[:, 1:2], idxf[:, 1:2], idx[:, 1:2], ALU.add))
                wait_for(stt(idxf[:, 4:5], idxf[:, 1:2], idxf[:, 0:1], idxf[:, 2:3], ALU.mult, ALU.add))
                tt(sidx_next[:, u:u + 1], idxf[:, 4:5], idxf[:, 3:4], ALU.add).then_inc(idx_ok, 1)

            dve.wait_ge(idxmm_done, 1)
            tokens_of_slots(0, link)
            dve.wait_ge(gexp_ok, 2)
            link(reduce(small[:, 5, :], gexp, AX, ALU.add))
            link(nc.vector.reciprocal(small[:, 6, :], small[:, 5, :]))
            link(ts(small[:, 7, :], small[:, 4, :], 1.0, None, ALU.add))
            link(nc.vector.reciprocal(small[:, 8, :], small[:, 7, :]))
            link(tt(gatew[:, :, 0], small[:, 8, :], small[:, 6, :], ALU.mult))
            tt(gatew[:, :, 1], gatew[:, :, 0], small[:, 4, :], ALU.mult).then_inc(gatew_ok, 1)

            dve.wait_ge(table_ok, 1)
            pairs = dve.value_load(n_pairs, min_val=NE // 2, max_val=NE // 2 * LEVELS)

            per_visit = 3
            def visits(p):
                for u in range(2):
                    seen = [0]

                    def loop_link(ins):
                        seen[0] += 1
                        ins.then_inc(dve_loop, 1)
                        dve.wait_ge(dve_loop, p * (2 * per_visit) + (per_visit * u + seen[0]))

                    n = dve.value_load(countJ[:, col_of(p, u)], min_val=0, max_val=SEQ)
                    if not first_pair(p):
                        dve.wait_ge(row_out[u], p * 16)
                    dve.wait_ge(idx_ok, p * 2 + (u + 1))
                    nc.vector.tensor_copy(sidx[:, u:u + 1], sidx_next[:, u:u + 1]).then_inc(sidx_ok, 1)
                    dve.wait_ge(idxmm_done, p * 2 + (u + 1))
                    pick_rows(u, col_of(p, u + 2))
                    rank_rows(u, col_of(p, u + 2))

                    def gated(s):
                        dve.wait_ge(silu_ok[s], p * 2 + (u + 1))
                        tt(hid[HALF * s:HALF * s + HALF, :], silu[HALF:P, s, :], PS[HALF:P, s, :],
                           ALU.mult).then_inc(hid_ok[s], 1)

                    def y_right(s):
                        dve.wait_ge(down_done[s], p * 2 + (u + 1))
                        nc.vector.tensor_copy(yrow(u)[HALF * s:HALF * s + HALF, 512:1024],
                                              PS[HALF:P, 5 + s, :]).then_inc(yd_ok[s], 1)

                    gated(0)
                    with dve.If(n > HALF):
                        gated(1)
                    with dve.Else():
                        dve.sem_inc(hid_ok[1], 1)
                    dve.wait_ge(ht_done, p * 2 + (u + 1))
                    nc.vector.tensor_copy(hidT(u), PS[:, 4, :].rearrange("p (c s) -> p c s", c=FC)).then_inc(hidt_ok, 1)
                    dve.wait_ge(idxmm_done, p * 2 + (u + 2))
                    tokens_of_slots(1 - u, loop_link)
                    assert seen[0] == per_visit
                    y_right(0)
                    with dve.If(n > HALF):
                        y_right(1)
                    with dve.Else():
                        dve.sem_inc(yd_ok[1], 1)

            visits(0)
            with dve.Fori(1, pairs) as p:
                visits(p)

            dve.wait_ge(gatew_ok, 1)
            for t in range(NT):
                if t < 2:
                    dve.wait_ge(alpha_ok, 1)
                    dve.wait_ge(comb_in[0][t], 16)
                    link(stt(H[:, t, :], comb[:, t, 0, :], gatew[:, t, 0:1], H[:, t, :], ALU.mult, ALU.add))
                else:
                    dve.wait_ge(comb_ok, t - 1)
                dve.wait_ge(comb_in[1][t], 16)
                stt(H[:, t, :], comb[:, t, 1, :], gatew[:, t, 1:2], H[:, t, :], ALU.mult, ALU.add).then_inc(comb_used, 1)
                dve.wait_ge(comb_used, t + 1)
                norm_stats(3 * NT + t)
                if t < 2:
                    dve.wait_ge(var_ok, 3 * NT + t + 1)
                    dve.wait_ge(lng_in[3], 32)
                    stt(H[:, t, :], H[:, t, :], meanvar[:, t, 0:1], lnG[:, :], ALU.subtract, ALU.mult).then_inc(gain_ok, 1)
                else:
                    norm_apply(3 * NT + t)

        @block.tensor
        def _(pe):
            def free(job):
                before = [j for j in range(job) if BANK[j] == BANK[job]]
                if before and EVAC[before[-1]] == "A":
                    pe.wait_ge(evac_act, evacs("A", before[-1]))
                elif before:
                    pe.wait_ge(evac_dve, evacs("D", before[-1]))

            def transposes(job, src, width=4):
                for c in range(width):
                    last = nc.tensor.transpose(PS[:, BANK[job], P * c:P * c + P], src[:, P * c:P * c + P], ident[:, :])
                last.then_inc(job_done, 1)

            def product(dst, lhs, rhs, first_of=None, chunks=(0, KC)):
                for k in range(*chunks):
                    if first_of and k % (KC // PIECES) == 0:
                        lo_written(pe, first_of, k * PIECES // KC + 1)
                    (l_hi, l_lo), (r_hi, r_lo) = lhs(k), rhs(k)
                    nc.tensor.matmul(dst, l_hi, r_hi, start=(k == 0), stop=False)
                    nc.tensor.matmul(dst, l_hi, r_lo, start=False, stop=False)
                    last = nc.tensor.matmul(dst, l_lo, r_hi, start=False, stop=(k == KC - 1))
                return last

            def weight_columns(name, c):
                i, cols = SLABS.index(name), slice(P * c, P * c + P)
                return lambda k: (slab_hi(i)[:, k, cols], slab_lo(i)[:, k, cols])

            def weight_rows(name, cols=slice(0, 512)):
                i = SLABS.index(name)
                return lambda k: (slab_hi(i)[:, k, cols], slab_lo(i)[:, k, cols])

            def act_columns(hi, lo, t):
                return lambda k: (hi[:, k, P * t:P * t + P], lo[:, k, P * t:P * t + P])

            def act_rows(hi, lo, cols=slice(None)):
                return lambda k: (hi[:, k, cols], lo[:, k, cols])

            pe.wait_ge(ident_ok, 1)
            for i in range(4):
                pe.wait_ge(mem_in[i // 2], 16)
                transposes(job_of("memT", i), memR[:, i // 2, 512 * (i % 2):512 * (i % 2) + 512])
            waits_evac(pe, job_of("memT", 3))
            for i in range(4):
                free(job_of("xk", i))
            for c in range(PIECES):
                for i in range(4):
                    last = product(PS[:, BANK[job_of("xk", i)], 0:MEM], weight_columns("xk0", i), act_rows(memT_hi, memT_lo),
                                   "xk0", (2 * c, 2 * c + 2))
                    if c == PIECES - 1:
                        last.then_inc(job_done, 1)
            for i in range(4, 8):
                name = f"xk{i // 4}"
                free(job_of("xk", i))
                product(PS[:, BANK[job_of("xk", i)], 0:MEM], weight_columns(name, i % 4), act_rows(memT_hi, memT_lo),
                        name if i % 4 == 0 else None).then_inc(job_done, 1)
            pe.wait_ge(table_in, 48)
            for i in range(2):
                job = job_of("bias", i)
                free(job)
                nc.tensor.matmul(PS[0:16, BANK[job], :], relb[:, :], onehot[:, 512 * i:512 * i + 512], start=True,
                                 stop=True).then_inc(job_done, 1)
            for i in range(4):
                name = f"xv{i // 2}"
                free(job_of("xv", i))
                product(PS[:, BANK[job_of("xv", i)], :], act_columns(memT_hi, memT_lo, i % 2), weight_rows(name),
                        name if i % 2 == 0 else None).then_inc(job_done, 1)
                if i in (1, 2):
                    for j in range(4 * i - 4, 4 * i):
                        pe.wait_ge(h_ok, j // 2 + 1)
                        free(job_of("hT", j))
                        transposes(job_of("hT", j), H[:, j // 2, 512 * (j % 2):512 * (j % 2) + 512])
            waits_evac(pe, job_of("hT", 7))

            def from_columns(job, name, c):
                free(job)
                product(PS[:, BANK[job], :], weight_columns(name, c), act_rows(aT_hi, aT_lo),
                        name if c == 0 else None).then_inc(job_done, 1)

            for i in range(4):
                from_columns(job_of("qa", i), "qa", i)
            from_columns(job_of("ka", 0), "kava", 0)
            job = job_of("va", 0)
            free(job)
            for t in range(NT):
                last = product(PS[:, BANK[job], P * t:P * t + P], act_columns(aT_hi, aT_lo, t), weight_rows("kava", slice(P, 2 * P)))
            last.then_inc(job_done, 1)
            for name in ("qb", "kb"):
                for i in range(4):
                    from_columns(job_of(name, i), name, i)
            for i in range(4):
                free(job_of("vb", i))
                product(PS[:, BANK[job_of("vb", i)], :], act_columns(aT_hi, aT_lo, i), weight_rows("vb"),
                        "vb" if i == 0 else None).then_inc(job_done, 1)
            waits_evac(pe, job_of("vb", 3))

            def scores(n):
                pair, tile, hb = n // 8, (n // 2) % 4, n % 2
                group, j = PAIRS[pair]
                keys = keys_of(pair, tile)
                rows = slice(HD * hb, HD * hb + HD)
                if n >= 4:
                    pe.wait_ge(l_done, n - 3)
                if group == "B":
                    if n % 8 == 0:
                        pe.wait_ge(qk_lo_ok, 2 * j + 2)
                    for i, (q_part, k_part) in enumerate(((qkb_hi, qkb_hi), (qkb_hi, qkb_lo), (qkb_lo, qkb_hi))):
                        last = nc.tensor.matmul(PS[:, n % 4, :], q_part[rows, j, P * tile:P * tile + P],
                                                k_part[rows, 4 + j, :], start=(i == 0), stop=(i == 2))
                    last.then_inc(s_done, 1)
                    return
                nc.tensor.matmul(PS[:, n % 4, 0:P * len(keys)], qaT[rows, j, P * tile:P * tile + P],
                                 kaT(j // 2)[rows, P * keys[0]:P * (keys[-1] + 1)], start=True, stop=True).then_inc(s_done, 1)

            def turn(n):
                keys = keys_of(n // 8, (n // 2) % 4)
                pe.wait_ge(e_done, n + 1)
                if n >= 2:
                    pe.wait_ge(pt_act if n % 2 == 0 else pt_dve, n // 2)
                for c in range(len(keys)):
                    last = nc.tensor.transpose(PS[:, 4 + n % 2, P * c:P * c + P], prob(n)[:, P * c:P * c + P], ident[:, :])
                last.then_inc(t_done, 1)

            def values(r):
                pair, tile = r // 4, r % 4
                group, j = PAIRS[pair]
                keys = keys_of(pair, tile)
                pe.wait_ge(pt_act, r + 1)
                pe.wait_ge(pt_dve, r + 1)
                if tile == 0 and pair >= 2:
                    pe.wait_ge(y_ok, pair - 1)
                for c, key in enumerate(keys):
                    for hb in range(2):
                        rows = slice(HD * hb, HD * hb + HD)
                        v = va[:, key, HD * (j // 2):HD * (j // 2) + HD] if group == "A" else vb[:, key, P * j + HD * hb:P * j + HD * hb + HD]
                        last = nc.tensor.matmul(PS[rows, 6 + pair % 2, P * tile:P * tile + P], v,
                                                probT(2 * r + hb)[:, P * c:P * c + P],
                                                start=(c == 0), stop=(c == len(keys) - 1))
                last.then_inc(pv_done, 1)

            def turn_pair(pair):
                pe.wait_ge(pair_ok, pair + 1)
                for t in range(NT):
                    last = nc.tensor.transpose(PS[:, 6 + pair % 2, P * t:P * t + P], pairT[:, P * t:P * t + P], ident[:, :])
                last.then_inc(pair_turned, 1)

            for m in range(35):
                if m < 32:
                    scores(2 * m)
                    scores(2 * m + 1)
                if 2 <= m <= 33:
                    turn(2 * m - 4)
                    turn(2 * m - 3)
                if m >= 3:
                    values(m - 3)
                if m % 4 == 3 and m >= 7:
                    turn_pair(m // 4 - 1)

            def transpose_y(i):
                pe.wait_ge(yn_ok, i + 1)
                if i >= 4:
                    pe.wait_ge(y_ok, 8)
                free(job_of("yT", i))
                transposes(job_of("yT", i), Y[:, i % 4, 512 * (i // 4):512 * (i // 4) + 512])

            def transpose_h(name, i, norm):
                pe.wait_ge(h_ok, NT * norm + i // 2 + 1)
                free(job_of(name, i))
                transposes(job_of(name, i), H[:, i // 2, 512 * (i % 2):512 * (i % 2) + 512])

            def dense_out(name, i, slab_name, hi, lo, chunks=(0, KC)):
                job = job_of(name, i)
                if chunks[0] == 0:
                    free(job)
                last = product(PS[:, BANK[job], :], act_columns(hi, lo, i % 4), weight_rows(slab_name), slab_name, chunks)
                if chunks[1] == KC:
                    last.then_inc(job_done, 1)

            for i in range(4):
                transpose_y(i)
            turn_pair(7)
            waits_evac(pe, job_of("yT", 3))
            for i in range(4):
                dense_out("mix", i, "wo0", yT_hi, yT_lo, (0, 4))
                if i == 2:
                    for j in range(4, 8):
                        transpose_y(j)
            waits_evac(pe, job_of("yT", 7))
            for i in range(4):
                dense_out("mix", i, "wo0", yT_hi, yT_lo, (4, KC))
            for i in range(4, 7):
                dense_out("mix", i, "wo1", yT_hi, yT_lo)
            for i in range(4):
                transpose_h("h1T", i, 1)
            dense_out("mix", 7, "wo1", yT_hi, yT_lo)
            waits_evac(pe, job_of("h1T", 3))
            for half in range(2):
                cols = slice(256 * half, 256 * half + 256)
                for i in range(4):
                    job = job_of("xq", i)
                    if half == 0:
                        free(job)
                    last = product(PS[:, BANK[job], cols], weight_columns("xq0", i), act_rows(aT_hi, aT_lo, cols), "xq0")
                    if half:
                        last.then_inc(job_done, 1)
                    elif i == 2:
                        for j in range(4, 8):
                            transpose_h("h1T", j, 1)
                if half == 0:
                    waits_evac(pe, job_of("h1T", 7))

            def xscores(h):
                for u in (2 * h, 2 * h + 1):
                    if h >= 2:
                        pe.wait_ge(xe_done, 2 * (u - 4) + 2)
                    for i in range(2):
                        tile = 2 * (u % 2) + i
                        for c in range(2):
                            last = nc.tensor.matmul(PS[:, u % 4, 256 * i:256 * i + 256],
                                                    xqT[:, 2 * h + c, P * tile:P * tile + P], xkT[:, 2 * h + c, :],
                                                    start=(c == 0), stop=(c == 1))
                    last.then_inc(xs_done, 1)

            def xvalues(h):
                pe.wait_ge(xpt_act, h + 1)
                pe.wait_ge(xpt_dve, h + 1)
                for c in range(2):
                    if h:
                        pe.wait_ge(xo_dve, 2 * (h - 1) + c + 1)
                    for mt in range(MT):
                        last = nc.tensor.matmul(PS[:, 6 + c, :], xv[:, mt, XD * h + P * c:XD * h + P * c + P],
                                                xprobT[:, h % 2, mt, :], start=(mt == 0), stop=(mt == MT - 1))
                    last.then_inc(xpv_done, 1)

            def turn_x(h):
                pe.wait_ge(xp_done, 4 * h + 4)
                if h:
                    pe.wait_ge(xpt_act, h)
                    pe.wait_ge(xpt_dve, h)
                for mt in range(MT):
                    for i in range(NT):
                        last = nc.tensor.transpose(PS[:, 4 + mt, P * i:P * i + P],
                                                   xprob(h)[:, i, P * mt:P * mt + P], ident[:, :])
                last.then_inc(xt_done, 1)

            from_columns(job_of("xq", 4), "xq1", 0)
            waits_evac(pe, job_of("xq", 3))
            xscores(0)
            xscores(1)
            for i in range(1, 4):
                from_columns(job_of("xq", 4 + i), "xq1", i)
            waits_evac(pe, job_of("xq", 7))
            turn_x(0)
            xscores(2)
            turn_x(1)
            xvalues(0)
            xscores(3)
            turn_x(2)
            xvalues(1)
            turn_x(3)
            xvalues(2)
            xvalues(3)
            pe.wait_ge(xo_dve, 2 * XH - 2)
            for i in range(4):
                dense_out("xo", i, "xo0", yT_hi, aT_lo, (0, 6))
            pe.wait_ge(xo_dve, 2 * XH)
            for i in range(4):
                dense_out("xo", i, "xo0", yT_hi, aT_lo, (6, KC))
            for i in range(4, 7):
                dense_out("xo", i, "xo1", yT_hi, aT_lo)

            def router(t):
                waits_evac(pe, job_of("h2T", 2 * t + 1))
                for k in range(KC):
                    last = nc.tensor.matmul(PS[:, 4, NR * t:NR * t + NR], h2T[:, k, P * t:P * t + P], router_w[:, k, :],
                                            start=(k == 0), stop=(k == KC - 1))
                last.then_inc(logits_done, 1)

            for i in range(4):
                transpose_h("h2T", i, 2)
            dense_out("xo", 7, "xo1", yT_hi, aT_lo)
            pe.wait_ge(router_in, 64)
            router(0)
            transpose_h("h2T", 4, 2)
            transpose_h("h2T", 5, 2)
            router(1)
            transpose_h("h2T", 6, 2)
            transpose_h("h2T", 7, 2)
            router(2)
            router(3)
            pe.wait_ge(consts_ok, 1)
            pe.wait_ge(chosen_ok, 1)
            for t in range(NT):
                for s in range(t + 1):
                    nc.tensor.matmul(PS[:, 5, NE * t:NE * t + NE], before[:, :] if s == t else ones[:, :], chosen[:, s, :],
                                     start=(s == 0), stop=(s == t))
            for t in range(NT):
                last = nc.tensor.matmul(PS[:, 5, P:P + NE], ones[:, :], chosen[:, t, :], start=(t == 0), stop=(t == NT - 1))
            last.then_inc(pos_done, 1)

            def gather(u, s):
                slots = slice(HALF * s, HALF * s + HALF)
                for t in range(NT):
                    for i in range(3):
                        first, end = (t == 0 and i == 0), (t == NT - 1 and i == 2)
                        nc.tensor.matmul(PS[0:HALF, 2 + s, :], pick(u)[:, t, slots], h2_part(i)[:, t, 0:512], start=first, stop=end)
                        last = nc.tensor.matmul(PS[HALF:P, 2 + s, :], pick(u)[:, t, slots], h2_part(i)[:, t, 512:1024],
                                                start=first, stop=end)
                last.then_inc(rows_done[s], 1)

            def slot_tokens(u):
                for t in range(NT):
                    last = nc.tensor.matmul(PS[:, 7, 0:3], ranked(u)[:, t, :], numbers[:, t, :], start=(t == 0), stop=(t == NT - 1))
                last.then_inc(idxmm_done, 1)

            def turn_rows(s, count):
                pe.wait_ge(rows_ok[s], count)
                for c in range(4):
                    last = nc.tensor.transpose(PS[:, 2 + s, P * c:P * c + P], xg(s)[:, P * c:P * c + P], ident[:, :])
                last.then_inc(xt2_done[s], 1)

            pe.wait_ge(pick_ok, 1)
            pe.wait_ge(part_ok, NT)
            gather(0, 0)
            turn_rows(0, 1)
            pe.wait_ge(table_ok, 1)
            first_n = pe.value_load(countJ[:, 0:1], min_val=0, max_val=SEQ)
            with pe.If(first_n > HALF):
                gather(0, 1)
                turn_rows(1, 1)
            with pe.Else():
                pe.sem_inc(rows_done[1], 1)
                pe.sem_inc(xt2_done[1], 1)
            pe.wait_ge(ranked_ok, 1)
            slot_tokens(0)
            pairs = pe.value_load(n_pairs, min_val=NE // 2, max_val=NE // 2 * LEVELS)
            def visits(p):
                for u in range(2):
                    n = pe.value_load(countJ[:, col_of(p, u)], min_val=0, max_val=SEQ)
                    then = pe.value_load(countJ[:, col_of(p, u + 1)], min_val=0, max_val=SEQ)

                    second = isinstance(p, int) and (p, u) == (1, 0)
                    gate = gate_w2 if second else gate_w(u)

                    def gate_up(s):
                        slots = slice(HALF * s, HALF * s + HALF)
                        for k in range(KC):
                            nc.tensor.matmul(PS[0:HALF, s, :], xgT(u)[:, k, slots], gate[:, k, :],
                                             start=(k == 0), stop=(k == KC - 1))
                            last = nc.tensor.matmul(PS[HALF:P, s, :], xgT(u)[:, k, slots], up_w(u)[:, k, :],
                                                    start=(k == 0), stop=(k == KC - 1))
                        last.then_inc(gu_done[s], 1)

                    def down(s):
                        slots = slice(HALF * s, HALF * s + HALF)
                        for k in range(FC):
                            nc.tensor.matmul(PS[0:HALF, 5 + s, :], hidT(u)[:, k, slots], down_w(u)[:, k, 0:512],
                                             start=(k == 0), stop=(k == FC - 1))
                            last = nc.tensor.matmul(PS[HALF:P, 5 + s, :], hidT(u)[:, k, slots], down_w(u)[:, k, 512:1024],
                                                    start=(k == 0), stop=(k == FC - 1))
                        last.then_inc(down_done[s], 1)

                    if second:
                        pe.wait_ge(gate_w2_in, 16)
                    else:
                        pe.wait_ge(gate_in[u], p * 16 + (0 if u == 0 and not first_pair(p) else 16))
                    pe.wait_ge(up_in[u], p * 16 + 16)
                    pe.wait_ge(xgt_ok[0], p * 2 + (u + 1))
                    gate_up(0)
                    pe.wait_ge(xgt_ok[1], p * 2 + (u + 1))
                    with pe.If(n > HALF):
                        gate_up(1)
                    with pe.Else():
                        pe.sem_inc(gu_done[1], 1)
                    pe.wait_ge(pick_ok, p * 2 + (u + 2))
                    gather(1 - u, 0)
                    with pe.If(then > HALF):
                        gather(1 - u, 1)
                    with pe.Else():
                        pe.sem_inc(rows_done[1], 1)
                    pe.wait_ge(idx_ok, p * 2 + (u + 1))
                    pe.wait_ge(ranked_ok, p * 2 + (u + 2))
                    slot_tokens(1 - u)
                    pe.wait_ge(hid_ok[0], p * 2 + (u + 1))
                    pe.wait_ge(hid_ok[1], p * 2 + (u + 1))
                    for c in range(FC):
                        last = nc.tensor.transpose(PS[:, 4, P * c:P * c + P], hid[:, P * c:P * c + P], ident[:, :])
                    last.then_inc(ht_done, 1)
                    turn_rows(0, p * 2 + (u + 2))
                    with pe.If(then > HALF):
                        turn_rows(1, p * 2 + (u + 2))
                    with pe.Else():
                        pe.sem_inc(xt2_done[1], 1)
                    pe.wait_ge(down_in[u], p * 16 + 16)
                    pe.wait_ge(hidt_ok, p * 2 + (u + 1))
                    for s in range(2):
                        if u or not first_pair(p):
                            pe.wait_ge(ya_ok[s], p * 2 + u)
                            pe.wait_ge(yd_ok[s], p * 2 + u)
                    down(0)
                    with pe.If(n > HALF):
                        down(1)
                    with pe.Else():
                        pe.sem_inc(down_done[1], 1)

            visits(0)
            visits(1)
            with pe.Fori(2, pairs) as p:
                visits(p)


def shape_tables():
    import numpy as np

    rel = np.arange(1024) - 512
    n = np.abs(rel)
    large = 8 + (np.log(np.maximum(n, 1) / 8) / np.log(1024 / 8) * 8).astype(np.int32)
    bucket = (rel > 0) * 16 + np.where(n < 8, n, np.minimum(large, 15))
    onehot = (np.arange(32)[:, None] == bucket[None]).astype(np.float32)
    reach_b = (n <= 64) * 1 + ((n <= 256) & (rel % 4 == 0)) + (rel % 16 == 0)
    a = np.where(n <= 128, 0.0, BIG)
    b = np.where(reach_b > 0, -np.log(np.maximum(reach_b, 1)), BIG)
    mask = np.concatenate([np.tile(a, (8, 1)), np.tile(b, (8, 1))]).astype(np.float32)
    return onehot, mask


_INS = ["x", "mem", "ln_in_g", "ln_in_b", "w_in", "rel_bias", "sink_a", "norm_a_g", "norm_b_g", "w_out", "ln1_g",
        "ln1_b", "xq", "xkv", "xo", "ln2_g", "ln2_b", "w_group", "b_group", "w_router", "b_router", "w_gate", "w_up",
        "w_down", "ln3_g", "ln3_b"]


def kernel(**inputs):
    import numpy as np
    import concourse.bacc as bacc
    from concourse.bass_utils import run_bass_kernel_spmd

    nc = bacc.Bacc("TRN2", target_bir_lowering=False, num_devices=1)
    arrays = {f"in_{name}": np.ascontiguousarray(inputs[name]) for name in _INS}
    arrays["in_bucket_onehot"], arrays["in_band_mask"] = shape_tables()
    args = [nc.dram_tensor(n, a.shape, mybir.dt.from_np(a.dtype), kind="ExternalInput").ap() for n, a in arrays.items()]
    out = nc.dram_tensor("out_dram", (1, SEQ, D), F32, kind="ExternalOutput").ap()
    build(nc, *args, out)
    result = run_bass_kernel_spmd(nc, [arrays], core_ids=[0])
    return result.results[0]["out_dram"]
```
